# Optimizing a Trainium2 kernel written in Bass

```python
import functools
import jax, jax.numpy as jnp
from jax import lax
import numpy as np

D_MODEL = 1024
BATCH = 1
SEQ = 2048
DEPTH = 1
DEC_BATCH = 8
DEC_SEQ = 4
PAST_LEN = 2048
PAGE_SIZE = 128

CHUNK = 128
A_GROUPS = 4
A_WIDTH = D_MODEL // 2
A_GROUP_DIM = A_WIDTH // A_GROUPS
HEAD_DIM = 64
B_HEADS = (D_MODEL // 2) // HEAD_DIM
B_KV_HEADS = 2
B_GROUP = B_HEADS // B_KV_HEADS
WINDOW = 128
ROPE_THETA = 10000.0
N_BRANCH = 2
N_GROUPS = 4
EXPERTS_PER_GROUP = 8
N_EXPERTS = N_GROUPS * EXPERTS_PER_GROUP
TOP_K = 2
EXPERT_HIDDEN = D_MODEL // 4
MOE_BLOCK = 128
EPS = 1e-6
Q_WIDTH = B_HEADS * HEAD_DIM
KV_WIDTH = B_KV_HEADS * HEAD_DIM
PROJ_SPLITS = [A_WIDTH, 2 * A_WIDTH, 2 * A_WIDTH + Q_WIDTH, 2 * A_WIDTH + Q_WIDTH + KV_WIDTH, 2 * A_WIDTH + Q_WIDTH + 2 * KV_WIDTH]
PROJ_COLS = 2 * A_WIDTH + Q_WIDTH + 2 * KV_WIDTH + N_BRANCH * D_MODEL

kernel_name = "gated_parallel_chunkmlp_swa_hmoe_step"

def rms_norm(x, g):
    x32 = x.astype(jnp.float32)
    y = x32 * lax.rsqrt(jnp.mean(x32 * x32, axis=-1, keepdims=True) + EPS)
    return (y * g.astype(jnp.float32)).astype(x.dtype)

def layer_norm(x, g, b):
    x32 = x.astype(jnp.float32)
    mu = jnp.mean(x32, axis=-1, keepdims=True)
    xc = x32 - mu
    y = xc * lax.rsqrt(jnp.mean(xc * xc, axis=-1, keepdims=True) + EPS)
    return (y * g.astype(jnp.float32) + b.astype(jnp.float32)).astype(x.dtype)

def adaln_params(c, w_ada, b_ada):
    m = jax.nn.silu(c) @ w_ada + b_ada
    return [p[:, None, :] for p in jnp.split(m, 6, axis=-1)]

def rope(x, positions):
    half = HEAD_DIM // 2
    inv = jnp.power(jnp.float32(ROPE_THETA), -2.0 * jnp.arange(half, dtype=jnp.float32) / HEAD_DIM)
    ang = positions.astype(jnp.float32)[:, None] * inv[None, :]
    cos = jnp.cos(ang)[:, None, :]
    sin = jnp.sin(ang)[:, None, :]
    x32 = x.astype(jnp.float32)
    x1, x2 = x32[..., :half], x32[..., half:]
    return jnp.concatenate([x1 * cos - x2 * sin, x2 * cos + x1 * sin], axis=-1).astype(x.dtype)

def sink_softmax(s, sink):
    m = jnp.maximum(jnp.max(s, axis=-1, keepdims=True), sink)
    e = jnp.exp(s - m)
    z = jnp.sum(e, axis=-1, keepdims=True) + jnp.exp(sink - m)
    return e / z

def chunk_spatial_gate(u, v_n, w_s, b_s):
    n, l, wd = v_n.shape
    nc = -(-l // CHUNK)
    lp = nc * CHUNK
    vp = jnp.pad(v_n, ((0, 0), (0, lp - l), (0, 0))).reshape(n, nc, CHUNK, A_GROUPS, A_GROUP_DIM)
    w = w_s * jnp.tril(jnp.ones((CHUNK, CHUNK), w_s.dtype))
    mixed = jnp.einsum('gij,ncjgd->ncigd', w, vp) + b_s.T[None, None, :, :, None]
    return u * mixed.reshape(n, lp, wd)[:, :l]

def swa_prompt(q, k, v, sinks):
    n, s_len, _, dh = q.shape
    nb = s_len // WINDOW
    qb = q.reshape(n, nb, WINDOW, B_KV_HEADS, B_GROUP, dh)
    kb = k.reshape(n, nb, WINDOW, B_KV_HEADS, dh)
    vb = v.reshape(n, nb, WINDOW, B_KV_HEADS, dh)
    prev = lambda t: jnp.concatenate([jnp.zeros_like(t[:, :1]), t[:, :-1]], axis=1)
    kk = jnp.concatenate([prev(kb), kb], axis=2)
    vv = jnp.concatenate([prev(vb), vb], axis=2)
    s = jnp.einsum('bnqhgd,bnkhd->bnhgqk', qb, kk).astype(jnp.float32) * (HEAD_DIM ** -0.5)
    qi = jnp.arange(WINDOW)[:, None]
    kj = jnp.arange(2 * WINDOW)[None, :]
    band = (kj >= qi) & (kj <= qi + WINDOW)
    not_first = jnp.arange(nb)[:, None, None] > 0
    valid = band[None] & (not_first | (kj >= WINDOW)[None])
    s = jnp.where(valid[None, :, None, None], s, -jnp.inf)
    sink = sinks.reshape(B_KV_HEADS, B_GROUP).astype(jnp.float32)[None, None, :, :, None, None]
    p = sink_softmax(s, sink)
    o = jnp.einsum('bnhgqk,bnkhd->bnqhgd', p.astype(vv.dtype), vv).reshape(n, s_len, B_HEADS * dh)
    cw = min(WINDOW, s_len)
    return o, k[:, s_len - cw:], v[:, s_len - cw:]

def swa_sample(q, k, v, cache_k, cache_v, sinks):
    n, t_len, _, dh = q.shape
    cw = cache_k.shape[1]
    kk = jnp.concatenate([cache_k.astype(k.dtype), k], axis=1)
    vv = jnp.concatenate([cache_v.astype(v.dtype), v], axis=1)
    qg = q.reshape(n, t_len, B_KV_HEADS, B_GROUP, dh)
    s = jnp.einsum('bqhgd,bkhd->bhgqk', qg, kk).astype(jnp.float32) * (HEAD_DIM ** -0.5)
    q_pos = PAST_LEN + jnp.arange(t_len)
    k_pos = jnp.concatenate([PAST_LEN - cw + jnp.arange(cw), PAST_LEN + jnp.arange(t_len)])
    diff = q_pos[:, None] - k_pos[None, :]
    valid = (diff >= 0) & (diff <= WINDOW)
    s = jnp.where(valid[None, None, None], s, -jnp.inf)
    sink = sinks.reshape(B_KV_HEADS, B_GROUP).astype(jnp.float32)[None, :, :, None, None]
    p = sink_softmax(s, sink)
    o = jnp.einsum('bhgqk,bkhd->bqhgd', p.astype(vv.dtype), vv).reshape(n, t_len, B_HEADS * dh)
    return o, k, v

def hier_route(h, w_rg, b_rg, w_re, b_re):
    lg = (h @ w_rg).astype(jnp.float32) + b_rg.astype(jnp.float32)
    pg = jax.nn.softmax(lg, axis=-1)
    g_sel = jnp.argmax(lg, axis=-1)
    p_top = jnp.take_along_axis(pg, g_sel[:, None], axis=-1)
    le = ((h @ w_re).astype(jnp.float32) + b_re.astype(jnp.float32)).reshape(-1, N_GROUPS, EXPERTS_PER_GROUP)
    le_g = jnp.take_along_axis(le, g_sel[:, None, None], axis=1)[:, 0]
    top_v, top_i = lax.top_k(le_g, TOP_K)
    wts = p_top * jax.nn.softmax(top_v, axis=-1)
    idx = (g_sel[:, None] * EXPERTS_PER_GROUP + top_i).astype(jnp.int32)
    return idx, wts

def routed_experts(h, idx, wts, w_gate, w_up, w_down):
    n, d = h.shape
    a = n * TOP_K
    flat_e = idx.reshape(-1)
    order = jnp.argsort(flat_e).astype(jnp.int32)
    sorted_e = flat_e[order]
    counts = jnp.zeros((N_EXPERTS,), jnp.int32).at[flat_e].add(1)
    padded = (counts + MOE_BLOCK - 1) // MOE_BLOCK * MOE_BLOCK
    pad_end = jnp.cumsum(padded)
    pad_start = pad_end - padded
    seg_start = jnp.cumsum(counts) - counts
    rank = jnp.arange(a, dtype=jnp.int32) - seg_start[sorted_e]
    dest = pad_start[sorted_e] + rank
    n_blocks = -(-a // MOE_BLOCK) + N_EXPERTS
    rows = n_blocks * MOE_BLOCK
    tok_sorted = order // TOP_K
    row_token = jnp.full((rows,), n, jnp.int32).at[dest].set(tok_sorted)
    block_expert = jnp.minimum(jnp.searchsorted(pad_end, jnp.arange(n_blocks, dtype=jnp.int32) * MOE_BLOCK, side='right'), N_EXPERTS - 1)
    h_pad = jnp.concatenate([h, jnp.zeros((1, d), h.dtype)], axis=0)
    xb = h_pad[row_token].reshape(n_blocks, MOE_BLOCK, d)

    def one_group(args):
        xg, e = args
        return (jax.nn.silu(xg @ w_gate[e]) * (xg @ w_up[e])) @ w_down[e]

    yb = lax.map(one_group, (xb, block_expert)).reshape(rows, d)
    y_sorted = yb[dest] * wts.reshape(-1)[order][:, None].astype(h.dtype)
    return jax.ops.segment_sum(y_sorted, tok_sorted, num_segments=n)

def layer_forward(x, c, positions, attn_fn, w_ada, b_ada, norm1_g, w_in, ln_v_g, ln_v_b, w_s, b_s, w_pa, w_pb, w_o, norm2_g, w_rg, b_rg, w_re, b_re, w_gate, w_up, w_down):
    n, l, d = x.shape
    shift1, scale1, gate1, shift2, scale2, gate2 = adaln_params(c, w_ada, b_ada)
    h = rms_norm(x, norm1_g) * (1 + scale1) + shift1
    u, v_a, q, k, v_b, gates = jnp.split(h @ w_in, PROJ_SPLITS, axis=-1)
    u = jax.nn.gelu(u)
    v_n = layer_norm(jax.nn.gelu(v_a), ln_v_g, ln_v_b)
    out_a = chunk_spatial_gate(u, v_n, w_s, b_s)
    q = rope(q.reshape(n, l, B_HEADS, HEAD_DIM), positions)
    k = rope(k.reshape(n, l, B_KV_HEADS, HEAD_DIM), positions)
    v_b = v_b.reshape(n, l, B_KV_HEADS, HEAD_DIM)
    out_b, k_rows, v_rows = attn_fn(q, k, v_b)
    g = jax.nn.sigmoid(gates.astype(jnp.float32)).astype(x.dtype)
    g_a, g_b = jnp.split(g, N_BRANCH, axis=-1)
    merged = g_a * (out_a @ w_pa) + g_b * (out_b @ w_pb)
    x = x + gate1 * (merged @ w_o)
    h2 = (rms_norm(x, norm2_g) * (1 + scale2) + shift2).reshape(n * l, d)
    idx, wts = hier_route(h2, w_rg, b_rg, w_re, b_re)
    y = routed_experts(h2, idx, wts, w_gate, w_up, w_down).reshape(n, l, d)
    x = x + gate2 * y
    return x, k_rows, v_rows, v_n

def setup_inputs(seed: int = 0) -> dict:
    key = jax.random.key(seed)
    ks = jax.random.split(key, 32)
    f32 = jnp.float32

    def nrm(k, shape, scale=1.0):
        return jax.random.normal(k, shape, f32) * scale

    L = DEPTH
    D = D_MODEL
    cw = min(WINDOW, PAST_LEN)
    return {
        'x_prompt': nrm(ks[0], (BATCH, SEQ, D)),
        'x_sample': nrm(ks[1], (DEC_BATCH, DEC_SEQ, D)),
        'cache_k': nrm(ks[2], (L, DEC_BATCH, cw, B_KV_HEADS, HEAD_DIM)),
        'cache_v': nrm(ks[3], (L, DEC_BATCH, cw, B_KV_HEADS, HEAD_DIM)),
        'c_prompt': nrm(ks[4], (BATCH, D)),
        'c_sample': nrm(ks[5], (DEC_BATCH, D)),
        'w_ada': nrm(ks[6], (L, D, 6 * D), 0.5 * D ** -0.5),
        'b_ada': nrm(ks[7], (L, 6 * D), 0.02),
        'norm1_g': 1.0 + nrm(ks[8], (L, D), 0.02),
        'w_in': nrm(ks[9], (L, D, PROJ_COLS), D ** -0.5),
        'ln_v_g': 1.0 + nrm(ks[10], (L, A_WIDTH), 0.02),
        'ln_v_b': nrm(ks[11], (L, A_WIDTH), 0.02),
        'w_s': nrm(ks[12], (L, A_GROUPS, CHUNK, CHUNK), CHUNK ** -0.5),
        'b_s': 1.0 + nrm(ks[13], (L, A_GROUPS, CHUNK), 0.02),
        'attn_sinks': nrm(ks[14], (L, B_HEADS), 0.5),
        'w_pa': nrm(ks[15], (L, A_WIDTH, D), A_WIDTH ** -0.5),
        'w_pb': nrm(ks[16], (L, Q_WIDTH, D), Q_WIDTH ** -0.5),
        'w_o': nrm(ks[17], (L, D, D), D ** -0.5),
        'norm2_g': 1.0 + nrm(ks[18], (L, D), 0.02),
        'w_rg': nrm(ks[19], (L, D, N_GROUPS), D ** -0.5),
        'b_rg': nrm(ks[20], (L, N_GROUPS), 0.01),
        'w_re': nrm(ks[21], (L, D, N_EXPERTS), D ** -0.5),
        'b_re': nrm(ks[22], (L, N_EXPERTS), 0.01),
        'w_gate': nrm(ks[23], (L, N_EXPERTS, D, EXPERT_HIDDEN), D ** -0.5),
        'w_up': nrm(ks[24], (L, N_EXPERTS, D, EXPERT_HIDDEN), D ** -0.5),
        'w_down': nrm(ks[25], (L, N_EXPERTS, EXPERT_HIDDEN, D), EXPERT_HIDDEN ** -0.5),
        'normf_g': 1.0 + nrm(ks[26], (D,), 0.02),
    }

def reference(x_prompt, x_sample, cache_k, cache_v, c_prompt, c_sample, w_ada, b_ada, norm1_g, w_in, ln_v_g, ln_v_b, w_s, b_s, attn_sinks, w_pa, w_pb, w_o, norm2_g, w_rg, b_rg, w_re, b_re, w_gate, w_up, w_down, normf_g):
    xp, xs = x_prompt, x_sample
    pos_p = jnp.arange(xp.shape[1])
    pos_s = PAST_LEN + jnp.arange(xs.shape[1])
    kp_list, vp_list, ks_list, vs_list, cv_list = [], [], [], [], []
    for l in range(DEPTH):
        lw = (w_ada[l], b_ada[l], norm1_g[l], w_in[l], ln_v_g[l], ln_v_b[l], w_s[l], b_s[l], w_pa[l], w_pb[l], w_o[l], norm2_g[l], w_rg[l], b_rg[l], w_re[l], b_re[l], w_gate[l], w_up[l], w_down[l])
        prompt_attn = functools.partial(swa_prompt, sinks=attn_sinks[l])
        sample_attn = functools.partial(swa_sample, cache_k=cache_k[l], cache_v=cache_v[l], sinks=attn_sinks[l])
        xp, kp, vp, _ = layer_forward(xp, c_prompt, pos_p, prompt_attn, *lw)
        xs, k_s, v_s, cv_s = layer_forward(xs, c_sample, pos_s, sample_attn, *lw)
        kp_list.append(kp)
        vp_list.append(vp)
        ks_list.append(k_s)
        vs_list.append(v_s)
        cv_list.append(cv_s)
    y_prompt = rms_norm(xp, normf_g)
    y_sample = rms_norm(xs, normf_g)
    k_prompt = jnp.stack(kp_list)
    v_prompt = jnp.stack(vp_list)
    k_sample = jnp.stack(ks_list)
    v_sample = jnp.stack(vs_list)
    chunk_v_sample = jnp.stack(cv_list)
    return (y_prompt, y_sample, k_prompt, v_prompt, k_sample, v_sample, chunk_v_sample)


_drawn_inputs = setup_inputs


def setup_inputs(seed=0):
    import zlib

    import numpy as np

    out = dict(_drawn_inputs(seed))
    spreads = {}
    factors = {'cache_k': 2.884,
     'norm1_g': 2.69,
     'ln_v_g': 2.686,
     'ln_v_b': 2.755,
     'b_s': 8.0,
     'attn_sinks': 63.882,
     'norm2_g': 5.338,
     'b_rg': 8.0,
     'b_re': 8.0,
     'normf_g': 7.669}
    for name, (base, spread) in spreads.items():
        noise = np.random.default_rng([zlib.crc32(name.encode()), seed]).standard_normal(out[name].shape)
        drawn = base * np.exp(spread * noise) if base else spread * noise
        out[name] = __import__('jax').numpy.asarray(drawn.astype(out[name].dtype))
    for name, factor in factors.items():
        out[name] = (out[name] * factor).astype(out[name].dtype)
    return out
```

```python
from contextlib import ExitStack

import numpy as np

import concourse.bass as bass
from concourse import mybir

F32 = mybir.dt.float32
F32R = mybir.dt.float32r
I32 = mybir.dt.int32
U32 = mybir.dt.uint32
ALU = mybir.AluOpType
ACT = mybir.ActivationFunctionType
AX_X = mybir.AxisListType.X

P = 128
D = 1024
KD = D // P
SEQ = 2048
PAST = 2048
DEC_B, DEC_T = 8, 4
MS = DEC_B * DEC_T
NT = SEQ // P
TOKENS = SEQ + MS
AW = 512
GROUPS_A = 4
HD = 64
NH = 8
NKV = 2
NC = NH // NKV
WIN = 128
N_GROUPS, PER_GROUP = 4, 8
NE = N_GROUPS * PER_GROUP
EH = 256
HALF = HD // 2
EPS = 1e-6
MIX_COLS = 2 * AW + NH * HD + 2 * NKV * HD
GATE_A, GATE_B = MIX_COLS, MIX_COLS + D
MASKED = -1.0e30
REGION = (TOKENS + P - 1) // P * P
MAX_BLOCKS = (2 * TOKENS + NE * P) // P
TABLE = (NE + 1) * REGION + P
ROUTE_STEPS = 20
RING = 4
SHIFT1, SCALE1, GATE1, SHIFT2, SCALE2, GATE2 = range(6)


class Count:

    def __init__(self, tile, per):
        self.base, self.n, self.per = tile * per, 0, per

    def next(self):
        self.n += 1
        assert self.n <= self.per
        return self.base + self.n

    def all(self):
        assert self.n == self.per


def constants():
    inv = np.power(10000.0, -2.0 * np.arange(HALF) / HD).astype(np.float32)
    pos = np.concatenate([np.arange(SEQ), np.tile(PAST + np.arange(DEC_T), DEC_B)]).astype(np.float32)
    ang = (pos[:, None] * inv[None, :]).astype(np.float32)
    cos, sin = np.cos(ang).astype(np.float32), np.sin(ang).astype(np.float32)
    rope = np.concatenate([cos, cos, -sin, sin], axis=1).astype(np.float32)
    q = np.arange(P)[:, None]
    k = np.arange(P)[None, :]
    ok_prev, ok_cur = k >= q, k <= q
    mask = np.full((P, 2, 2 * P), MASKED, np.float32)
    mask[:, 0, P:][ok_cur] = 0.0
    mask[:, 1, :P][ok_prev] = 0.0
    mask[:, 1, P:][ok_cur] = 0.0
    t = (np.arange(P) % DEC_T)[:, None]
    mask_s = np.full((P, P + DEC_T), MASKED, np.float32)
    mask_s[:, :P][k >= t] = 0.0
    mask_s[:, P:][np.arange(DEC_T)[None, :] <= t] = 0.0
    small = np.zeros((P, 128), np.float32)
    small[:, 0:NE] = np.arange(NE)
    small[:, 32:36] = [4, 3, 2, 1]
    small[:, 36:40] = [0, 1, 2, 3]
    small[:, 40] = np.arange(P)
    tri = (np.arange(P)[:, None] < np.arange(P)[None, :]).astype(np.float32)
    return {"rope": rope, "mask": mask.reshape(P, 4 * P), "mask_s": mask_s, "small": small, "before": tri,
            "ident": np.eye(P, dtype=np.float32)}


def program(nc, a, outs):
    stack = ExitStack()
    with stack:
        def dram(name, shape, dt=F32):
            return nc.dram_tensor(name, shape, dt).ap()

        s = {
            "ada": dram("ada_rows", (1 + DEC_B, 6 * D)),
            "hT": dram("hT_split", (NT + 1, P, 2 * D)),
            "oT": dram("oT_split", (NT + 1, 2, P, 2 * AW)),
            "ma": dram("gated_a", (TOKENS, D)),
            "pb": dram("out_b_projected", (TOKENS, D)),
            "x1": dram("x_after_mixers", (TOKENS, D)),
            "h2": dram("h2_rows", (TOKENS, D)),
            "table": dram("slot_tokens", (TABLE, 1), I32),
            "blocks": dram("block_list", (4, P), I32),
            "cum": dram("block_ends", (1, NE), I32),
            "ys": dram("expert_rows", (MAX_BLOCKS * P, D)),
        }
        kept = {
            "wts": stack.enter_context(nc.sbuf_tensor("route_weights", [P, NT + 1, 2], F32)),
            "eid": stack.enter_context(nc.sbuf_tensor("route_experts", [P, NT + 1, 2], F32)),
            "rank": stack.enter_context(nc.sbuf_tensor("route_ranks", [P, NT + 1, 2], F32)),
            "counts": stack.enter_context(nc.sbuf_tensor("expert_counts", [P, NE], F32)),
            "ident": stack.enter_context(nc.sbuf_tensor("identity", [P, P], F32)),
            "yrow": stack.enter_context(nc.sbuf_tensor("y_rows", [P, NT + 1, 2], I32)),
        }
        with ExitStack() as weights_a:
            wa = [weights_a.enter_context(nc.sbuf_tensor(f"w_mix_{x}", [P, KD, MIX_COLS], F32R)) for x in ("hi", "lo")]
            condition(nc, a, s, kept, wa)
            sweep_mixers(nc, a, s, kept, wa, outs)
        sweep_gate_a(nc, a, s)
        sweep_gate_b(nc, a, s, kept)
        list_blocks(nc, a, s, kept)
        experts(nc, a, s, kept)
        combine(nc, a, s, kept, outs)


def tools(nc, ctx):
    def sb(name, shape, dt=F32):
        return ctx.enter_context(nc.sbuf_tensor(name, shape, dt))

    used = []

    def clear():
        nc.clear_and_free_semaphores(used)
        nc.all_engine_barrier()

    ctx.callback(clear)

    def sem(name):
        used.append(nc.alloc_semaphore(name))
        return used[-1]

    return sb, sem


def wait_apart(eng, sem, value, passed):
    eng.wait_ge(sem, value)
    eng.sem_inc(passed, 1)


def banks(nc, ctx, name):
    return [ctx.enter_context(nc.psum_tensor(f"{name}{n}", [P, 512], F32)) for n in range(8)]


def condition(nc, a, s, kept, wa):
    CH = 512
    NCH = 6 * D // CH
    with ExitStack() as ctx:
        sb, sem = tools(nc, ctx)
        ps = banks(nc, ctx, "cond")
        R = 1 + DEC_B
        c_rows = sb("c_rows", [R, D])
        c_tanh = sb("c_tanh", [R, D])
        c_t = sb("c_t", [P, KD, R])
        w = sb("w_ada_ring", [P, 2, KD, CH])
        rows = sb("ada_sums", [R, 6 * D])
        gains = sb("gain_rows", [R, 2, D])
        raw = sb("w_mix_raw", [P, 2, MIX_COLS])
        c_in, ident_in, w_in0, w_in1, b_in, raw_in0, raw_in1 = [
            sem(n) for n in ("c_in", "ident_in", "w_ada_in0", "w_ada_in1", "b_ada_in", "raw_in0", "raw_in1")]
        w_in, raw_in = (w_in0, w_in1), (raw_in0, raw_in1)
        tanhed, silued, turned, c_ready, summed, row_ready, stored = [
            sem(n) for n in ("c_tanhed", "c_silued", "c_turned", "c_t_ready", "ada_summed", "ada_row", "ada_stored")]
        hi_ready, lo_ready = sem("w_hi_ready"), sem("w_lo_ready")
        block = ctx.enter_context(nc.Block())

        @block.sync
        def _(sp):
            sp.dma_start(c_rows[0:1, :], a["c_prompt"]).then_inc(c_in, 16)
            sp.dma_start(c_rows[1:R, :], a["c_sample"]).then_inc(c_in, 16)
            sp.dma_start(kept["ident"][:, :], a["ident"]).then_inc(ident_in, 16)
            sp.dma_start(rows[:, :], a["b_ada"][0:1, :].to_broadcast([R, 6 * D])).then_inc(b_in, 16)
            for n, g in enumerate(("norm1_g", "norm2_g")):
                sp.dma_start(gains[:, n, :], a[g][0:1, :].to_broadcast([R, D])).then_inc(b_in, 16)
            for n in range(NCH):
                if n >= 2:
                    sp.wait_ge(summed, n - 1)
                sp.dma_start(w[:, n % 2, :, :],
                             a["w_ada"][0, :, n * CH:(n + 1) * CH].rearrange("(k p) c -> p k c", p=P)).then_inc(w_in[n % 2], 16)
            sp.wait_ge(row_ready, NCH + 2)
            sp.dma_start(s["ada"], rows[:, :]).then_inc(stored, 16)
            sp.wait_ge(stored, 16)

        @block.gpsimd
        def _(pool):
            for k in range(KD):
                if k >= 2:
                    pool.wait_ge(lo_ready, k - 1)
                pool.dma_start(raw[:, k % 2, :], a["w_in"][0, k * P:(k + 1) * P, 0:MIX_COLS]).then_inc(raw_in[k % 2], 16)

        @block.scalar
        def _(act):
            act.wait_ge(c_in, 32)
            nc.scalar.activation(c_tanh[:, :], c_rows[:, :], ACT.Tanh, scale=0.5).then_inc(tanhed, 1)
            for k in range(KD):
                act.wait_ge(raw_in[k % 2], 16 * (k // 2 + 1))
                nc.scalar.copy(wa[0][:, k, :], raw[:, k % 2, :]).then_inc(hi_ready, 1)

        @block.vector
        def _(dve):
            dve.wait_ge(tanhed, 1)
            nc.vector.scalar_tensor_tensor(out=c_rows[:, :], in0=c_tanh[:, :], scalar=1.0, in1=c_rows[:, :],
                                           op0=ALU.add, op1=ALU.mult).then_inc(silued, 1)
            dve.wait_ge(turned, 1)
            nc.vector.tensor_scalar(c_t[:, :, :], ps[0][:, 0:KD * R].rearrange("p (k r) -> p k r", r=R), 0.5, None,
                                    ALU.mult).then_inc(c_ready, 1)
            dve.wait_ge(b_in, 48)
            for n in range(NCH):
                if n < KD:
                    dve.wait_ge(hi_ready, n + 1)
                    nc.vector.tensor_tensor(wa[1][:, n, :], raw[:, n % 2, :], wa[0][:, n, :].bitcast(F32),
                                            ALU.subtract).then_inc(lo_ready, 1)
                dve.wait_ge(summed, n + 1)
                at = slice(n * CH, (n + 1) * CH)
                nc.vector.tensor_tensor(rows[:, at], ps[1 + n % 2][0:R, :], rows[:, at], ALU.add).then_inc(row_ready, 1)
            dve.wait_ge(row_ready, NCH)
            for n, at in enumerate((SCALE1, SCALE2)):
                part = rows[:, at * D:(at + 1) * D]
                nc.vector.scalar_tensor_tensor(out=part, in0=part, scalar=1.0, in1=gains[:, n, :],
                                               op0=ALU.add, op1=ALU.mult).then_inc(row_ready, 1)

        @block.tensor
        def _(pe):
            pe.wait_ge(silued, 1)
            pe.wait_ge(ident_in, 16)
            for k in range(KD):
                last = nc.tensor.transpose(ps[0][:, k * R:(k + 1) * R], c_rows[:, k * P:(k + 1) * P],
                                           kept["ident"][0:R, 0:R])
            last.then_inc(turned, 1)
            pe.wait_ge(c_ready, 1)
            for n in range(NCH):
                pe.wait_ge(w_in[n % 2], 16 * (n // 2 + 1))
                if n >= 2:
                    pe.wait_ge(row_ready, n - 1)
                for k in range(KD):
                    last = nc.tensor.matmul(ps[1 + n % 2][0:R, :], c_t[:, k, :], w[:, n % 2, k, :],
                                            start=(k == 0), stop=(k == KD - 1))
                last.then_inc(summed, 1)


def three(pe, out, left, right, first=True, last=True):
    nc_mm = pe.matmul
    nc_mm(out, left[0], right[0], start=first, stop=False)
    nc_mm(out, left[1], right[0], start=False, stop=False)
    return nc_mm(out, left[0], right[1], start=False, stop=last)


def sweep_mixers(nc, a, s, kept, wa, outs):
    y_prompt, y_sample, k_prompt, v_prompt, k_sample, v_sample, chunk_v = outs
    with ExitStack() as ctx:
        sb, sem = tools(nc, ctx)
        ps = banks(nc, ctx, "mix")
        x = sb("x_rows", [P, D])
        hT = [sb(f"hT_{n}", [P, KD, P], F32R) for n in ("hi", "lo")]
        mod = sb("mod_prompt", [P, 2, D])
        mod_s = sb("mod_sample", [MS, 2, D])
        u = sb("u_rows", [P, AW])
        v = sb("v_rows", [P, AW])
        ln = sb("ln_rows", [P, 2, AW])
        t1 = sb("rope_cos_part", [P, AW])
        t2 = sb("rope_sin_part", [P, AW])
        qr = sb("q_rotated", [P, NC, NKV, HD])
        kr = sb("k_rotated", [P, NKV * HD])
        qT = sb("qT", [P, NC, P])
        kT = sb("kT_prev_cur", [P, 2, P])
        vv = sb("v_prev_cur_next", [P, 3, NKV * HD])
        sc = sb("scores", [P, NH, 2 * P])
        pT = sb("probs_T", [P, 2 * NH, P])
        ob = sb("out_b_rows", [P, AW])
        oa = sb("out_a_rows", [P, AW])
        oaT = sb("out_a_T", [P, 2, AW], F32R)
        obT = sb("out_b_T", [P, 2, AW], F32R)
        rope = sb("rope_rows", [P, 2 * HD])
        mask = sb("masks", [P, 2, 2 * P])
        mask_s = sb("mask_sample", [P, P + DEC_T])
        ws = sb("w_s_rows", [P, GROUPS_A, P])
        wsT = sb("w_s_T", [P, GROUPS_A, P])
        ws_s = sb("w_s_sample_rows", [MS, GROUPS_A, MS])
        wsT_s = sb("w_s_sample_T", [MS, GROUPS_A, MS])
        bs = sb("b_s_cols", [P, GROUPS_A])
        bs_s = sb("b_s_sample", [MS, GROUPS_A])
        sink = sb("sink_rows", [P, NH])
        sink_s = sb("sink_sample", [P, NKV])
        tiny = sb("tiny", [P, 64])
        stats = sb("ln_stats", [P, 8])
        half = sb("minus_half", [P, 1])
        sq = sb("squares", [P, D])

        x_in, rope_in, const_in, mod_in = sem("x_in"), sem("rope_in"), sem("const_in"), sem("mod_in")
        d_front, d_back, d_norm = sem("dve_front_steps"), sem("dve_back_steps"), sem("dve_norm_steps")
        mean_sq, var_eps, half_ready = sem("mean_sq"), sem("var_eps"), sem("half_ready")
        k_moved, v_moved = sem("k_moved"), sem("v_moved")
        sumsq, rrms, h_ready = sem("sumsq"), sem("rrms"), sem("h_ready")
        h_turned, hi_ready, lo_ready = sem("h_turned"), sem("h_hi_ready"), sem("h_lo_ready")
        q_done, kv_done, v_done, u_done = sem("q_proj"), sem("kv_proj"), sem("v_proj"), sem("u_proj")
        q_parts, k_parts, qk_rot = sem("q_parts"), sem("k_parts"), sem("qk_rotated")
        vb_ready, v_gelu, u_gelu = sem("vb_ready"), sem("v_gelu"), sem("u_gelu")
        ln_ready, lnr_in, lnr = sem("v_n_ready"), sem("ln_var"), sem("ln_rstd")
        qk_turned, qT_ready, kT_ready = sem("qk_turned"), sem("qT_ready"), sem("kT_ready")
        scored, masked, maxed, probs, z_ready = sem("scored"), sem("masked"), sem("maxed"), sem("probs"), sem("z_ready")
        p_turned, pT_a, pT_d = sem("probs_turned"), sem("pT_act"), sem("pT_dve")
        pv_done, ob_ready, ob_turned, obT_hi, obT_lo = (sem("pv"), sem("out_b"), sem("ob_turned"), sem("obT_hi"), sem("obT_lo"))
        mixed, oa_ready, oa_turned, oaT_hi, oaT_lo = (sem("mixed"), sem("out_a"), sem("oa_turned"), sem("oaT_hi"), sem("oaT_lo"))
        stored_h, stored_oa, stored_ob, stored_kv = sem("stored_h"), sem("stored_oa"), sem("stored_ob"), sem("stored_kv")
        ws_ready, ws_turned, wsT_ready = sem("w_s_ready"), sem("w_s_turned"), sem("w_s_T_ready")
        cache_in, vnew_in = sem("cache_in"), sem("v_new_in")
        smp_turned, smp_scored, smp_dve, smp_max, smp_out = [sem(f"sample_{n}") for n in ("turned", "pe", "dve", "max", "out")]
        passed = sem("waits_passed")
        block = ctx.enter_context(nc.Block())
        S = NT

        def tok(ap, i, m):
            return ap[bass.ds(i * P, m), :] if not isinstance(i, int) else ap[i * P:i * P + m, :]

        ck = mod[:, 0, :].rearrange("p (b d) -> p b d", b=DEC_B)
        cv = mod[:, 1, :].rearrange("p (b d) -> p b d", b=DEC_B)
        ckT = x[:, :].rearrange("p (b r) -> p b r", b=DEC_B)
        sT = t1[:, 0:256]
        sT2 = t2[0:DEC_T, 0:256]
        s_rows = sc[:, 0:2, 0:P + DEC_T]
        pT_s = pT[:, 0:2, :].rearrange("p a b -> p (a b)")
        pT2_s = pT[0:DEC_T, 2:4, :].rearrange("p a b -> p (a b)")
        v_new = pT[0:DEC_T, 4:12, :]
        obT_f = ob[:, 0:4 * MS].rearrange("p (k m) -> p k m", m=MS)

        @block.sync
        def _(sp):
            sp.dma_start(x[:, :], a["x_prompt"][0, 0:P, :]).then_inc(x_in, 16)
            sp.dma_start(mod[:, 0, :], s["ada"][0:1, SCALE1 * D:(SCALE1 + 1) * D].to_broadcast([P, D])).then_inc(mod_in, 16)
            sp.dma_start(mod[:, 1, :], s["ada"][0:1, SHIFT1 * D:(SHIFT1 + 1) * D].to_broadcast([P, D])).then_inc(mod_in, 16)
            for n, part in enumerate((SCALE1, SHIFT1)):
                for b in range(DEC_B):
                    sp.dma_start(mod_s[b * DEC_T:(b + 1) * DEC_T, n, :],
                                 s["ada"][1 + b:2 + b, part * D:(part + 1) * D].to_broadcast([DEC_T, D])).then_inc(mod_in, 16)
            sp.dma_start(mask[:, :, :], a["mask"].rearrange("p (n k) -> p n k", n=2)).then_inc(const_in, 16)
            sp.dma_start(mask_s[:, :], a["mask_s"]).then_inc(const_in, 16)
            sp.dma_start(ln[:, 0, :], a["ln_v_g"][0:1, :].to_broadcast([P, AW])).then_inc(const_in, 16)
            sp.dma_start(ln[:, 1, :], a["ln_v_b"][0:1, :].to_broadcast([P, AW])).then_inc(const_in, 16)
            sp.dma_start(sink[:, :], a["attn_sinks"][0:1, :].to_broadcast([P, NH])).then_inc(const_in, 16)
            sp.dma_start(ws[:, :, :], a["w_s"][0].rearrange("g i j -> i g j")).then_inc(const_in, 16)
            with nc.allow_non_contiguous_dma(reason="a few small transposed vectors, once"):
                sp.dma_start(bs[:, :], a["b_s"][0].rearrange("g i -> i g")).then_inc(const_in, 16)
                for b in range(DEC_B):
                    at = slice(b * DEC_T, (b + 1) * DEC_T)
                    sp.dma_start(bs_s[at, :], a["b_s"][0, :, 0:DEC_T].rearrange("g i -> i g")).then_inc(const_in, 16)
                by_head = a["attn_sinks"].rearrange("o (h x) -> (o h) x", x=1)
                for b in range(DEC_B):
                    for g in range(NKV):
                        sp.dma_start(sink_s[b * 16:(b + 1) * 16, g:g + 1],
                                     by_head[g * NC:(g + 1) * NC, :].unsqueeze(1).to_broadcast([NC, DEC_T, 1])).then_inc(const_in, 16)
            sp.wait_ge(ws_ready, 1)
            for b in range(DEC_B):
                at = slice(b * DEC_T, (b + 1) * DEC_T)
                sp.dma_start(ws_s[at, :, at], a["w_s"][0, :, 0:DEC_T, 0:DEC_T].rearrange("g i j -> i g j")).then_inc(cache_in, 16)

            def stores(i, m):
                sp.wait_ge(lo_ready, i + 1)
                sp.wait_ge(hi_ready, i + 1)
                for n in range(2):
                    dst = s["hT"][bass.ds(i, 1), :, n * D:(n + 1) * D] if not isinstance(i, int) else s["hT"][i:i + 1, :, n * D:(n + 1) * D]
                    sp.dma_start(dst.rearrange("o p (k m) -> p (o k) m", m=P)[:, :, 0:m], hT[n][:, :, 0:m].bitcast(F32)).then_inc(stored_h, 16)

            def rows_b(i):
                sp.wait_ge(obT_lo, i + 1)
                dst = s["oT"][bass.ds(i, 1), 1, :, :] if not isinstance(i, int) else s["oT"][i:i + 1, 1, :, :]
                sp.dma_start(dst.rearrange("o p c -> p (o c)"), obT[:, :, :].rearrange("p n c -> p (n c)").bitcast(F32)).then_inc(stored_ob, 16)

            def rows_a(i, m):
                sp.wait_ge(oaT_lo, i + 1)
                dst = s["oT"][bass.ds(i, 1), 0, :, :] if not isinstance(i, int) else s["oT"][i:i + 1, 0, :, :]
                if m == P:
                    sp.dma_start(dst.rearrange("o p c -> p (o c)"), oaT[:, :, :].rearrange("p n c -> p (n c)").bitcast(F32)).then_inc(stored_oa, 16)
                else:
                    sp.dma_start(dst.rearrange("o p (c m) -> p (o c) m", m=P)[:, :, 0:m],
                                 oaT[:, :, :].rearrange("p n (k m) -> p (n k) m", m=P)[:, :, 0:m].bitcast(F32)).then_inc(stored_oa, 16)

            def ahead(i):
                sp.wait_ge(h_turned, i)
                sp.dma_start(x[:, :], tok(a["x_prompt"][0], i, P)).then_inc(x_in, 16)

            def angles(i, m):
                if not isinstance(i, int) or i > 0:
                    sp.wait_ge(k_parts, i)
                sp.dma_start(rope[0:m, :], tok(a["rope"], i, m)).then_inc(rope_in, 16)

            angles(0, P)
            ahead(1)
            stores(0, P)
            angles(1, P)
            ahead(2)
            stores(1, P)
            rows_a(0, P)
            with sp.Fori(1, NT - 2) as i:
                angles(i + 1, P)
                rows_b(i - 1)
                ahead(i + 2)
                stores(i + 1, P)
                rows_a(i, P)
            angles(NT - 1, P)
            rows_b(NT - 3)
            sp.wait_ge(h_turned, NT)
            sp.dma_start(x[0:MS, :], a["x_sample"].rearrange("b t d -> (b t) d")).then_inc(x_in, 16)
            for t, src in ((ck, "cache_k"), (cv, "cache_v")):
                sp.dma_start(t, a[src][0].rearrange("b r g d -> r b (g d)")).then_inc(cache_in, 16)
            stores(NT - 1, P)
            rows_a(NT - 2, P)
            angles(S, MS)
            sp.wait_ge(qk_rot, NT)
            sp.wait_ge(vb_ready, NT)
            sp.dma_start(k_prompt[0, 0].rearrange("r g d -> r (g d)"), kr[:, :]).then_inc(stored_kv, 16)
            sp.dma_start(v_prompt[0, 0].rearrange("r g d -> r (g d)"), vv[:, 2, :]).then_inc(stored_kv, 16)
            rows_b(NT - 2)
            stores(S, MS)
            rows_a(NT - 1, P)
            rows_b(NT - 1)
            sp.wait_ge(qk_rot, S + 1)
            sp.wait_ge(vb_ready, S + 1)
            sp.dma_start(k_sample[0].rearrange("b t g d -> (b t) (g d)"), kr[0:MS, :]).then_inc(stored_kv, 16)
            sp.dma_start(v_sample[0].rearrange("b t g d -> (b t) (g d)"), vv[0:MS, 2, :]).then_inc(stored_kv, 16)
            sp.wait_ge(stored_kv, 64)
            sp.wait_ge(pv_done, NT)
            sp.dma_start(v_new, v_sample[0].rearrange("b t g d -> t b (g d)")).then_inc(vnew_in, 16)
            sp.wait_ge(ln_ready, S + 1)
            sp.dma_start(chunk_v[0].rearrange("b t w -> (b t) w"), v[0:MS, :]).then_inc(stored_kv, 16)
            rows_a(S, MS)
            sp.wait_ge(obT_lo, S + 1)
            sp.dma_start(s["oT"][S, 1].rearrange("p (c m) -> p c m", m=P)[:, :, 0:MS],
                         obT[:, :, :].rearrange("p n (k m) -> p (n k) m", m=P)[:, :, 0:MS].bitcast(F32)).then_inc(stored_ob, 16)
            sp.wait_ge(stored_kv, 80)
            sp.wait_ge(stored_h, 32 * (NT + 1))
            sp.wait_ge(stored_oa, 16 * (NT + 1))
            sp.wait_ge(stored_ob, 16 * (NT + 1))

        @block.gpsimd
        def _(pool):
            pool.memset(half[:, :], -0.5).then_inc(half_ready, 1)
            pool.memset(ws_s[:, :, :], 0.0).then_inc(ws_ready, 1)
            pool.memset(kT[:, 0, :], 0.0).then_inc(ws_ready, 1)
            pool.memset(vv[:, 0:2, :], 0.0).then_inc(ws_ready, 1)
            pool.wait_ge(half_ready, 1)
            pool.wait_ge(ws_ready, 3)
            pool.wait_ge(const_in, 16 * (7 + DEC_B + DEC_B * NKV))
            pool.wait_ge(cache_in, 16 * DEC_B)
            pool.affine_select(out=ws[:, :, :], in_=ws[:, :, :], compare_op=ALU.is_ge, fill=0.0, base=0,
                               pattern=[[0, GROUPS_A], [-1, P]], channel_multiplier=1).then_inc(ws_ready, 1)
            pool.affine_select(out=ws_s[:, :, :], in_=ws_s[:, :, :], compare_op=ALU.is_ge, fill=0.0, base=0,
                               pattern=[[0, GROUPS_A], [-1, MS]], channel_multiplier=1).then_inc(ws_ready, 1)

            def rms_root(i, m):
                wait_apart(pool, sumsq, i + 1, passed)
                pool.tensor_scalar(tiny[0:m, 1:2], tiny[0:m, 0:1], 1.0 / D, EPS, ALU.mult, ALU.add).then_inc(mean_sq, 1)
                pool.wait_ge(mean_sq, i + 1)
                pool.tensor_tensor(tiny[0:m, 2:3], tiny[0:m, 1:2], half[0:m, :], ALU.pow).then_inc(rrms, 1)

            def ln_root(i, m):
                wait_apart(pool, lnr_in, i + 1, passed)
                pool.tensor_scalar(tiny[0:m, 3:4], stats[0:m, 7:8], EPS, None, ALU.add).then_inc(var_eps, 1)
                pool.wait_ge(var_eps, i + 1)
                pool.tensor_tensor(tiny[0:m, 4:5], tiny[0:m, 3:4], half[0:m, :], ALU.pow).then_inc(lnr, 1)

            rms_root(0, P)
            rms_root(1, P)
            with pool.Fori(0, NT - 2) as i:
                ln_root(i, P)
                rms_root(i + 2, P)
            ln_root(NT - 2, P)
            rms_root(S, MS)
            ln_root(NT - 1, P)
            ln_root(S, MS)

        @block.scalar
        def _(act):
            def square(i, m):
                act.wait_ge(x_in, i * 16 + 16)
                nc.scalar.activation(sq[0:m, :], x[0:m, :], ACT.Square, accum_out=tiny[0:m, 0:1]).then_inc(sumsq, 1)

            def high(i, m, first=False):
                act.wait_ge(h_turned, i + 1)
                if not first:
                    act.wait_ge(u_done, i)
                    act.wait_ge(stored_h, i * 32)
                for n in range(2):
                    last = nc.scalar.copy(hT[0][:, 4 * n:4 * n + 4, 0:m],
                                          ps[n][:, :].rearrange("p (k m) -> p k m", m=P)[:, :, 0:m])
                last.then_inc(hi_ready, 1)

            def keep_k(i):
                act.wait_ge(scored, i + 1)
                nc.scalar.copy(kT[:, 0, :], kT[:, 1, :]).then_inc(k_moved, 1)

            def keep_v(i, first):
                if not first:
                    act.wait_ge(pv_done, i)
                nc.scalar.copy(vv[:, 0, :], vv[:, 1, :]).then_inc(v_moved, 1)
                act.wait_ge(v_moved, i * 2 + 1)
                nc.scalar.copy(vv[:, 1, :], vv[:, 2, :]).then_inc(v_moved, 1)

            def back_probs(i):
                act.wait_ge(p_turned, i + 1)
                for n in (6, 7):
                    last = nc.scalar.copy(pT[:, 4 * n - 16:4 * n - 12, :], ps[n][:, :].rearrange("p (k m) -> p k m", m=P))
                last.then_inc(pT_a, 1)

            def back_out(i):
                act.wait_ge(ob_turned, i + 1)
                if not isinstance(i, int) or i > 0:
                    act.wait_ge(stored_ob, i * 16)
                nc.scalar.copy(obT[:, 0, :], ps[5][:, :]).then_inc(obT_hi, 1)

            def values(i, m, first):
                act.wait_ge(kv_done, i + 1)
                if not first:
                    act.wait_ge(v_moved, i * 2)
                nc.scalar.copy(vv[0:m, 2, :], ps[2][0:m, 128:256]).then_inc(vb_ready, 1)

            def gelu_v(i, m):
                act.wait_ge(v_done, i + 1)
                nc.scalar.activation(v[0:m, :], ps[3][0:m, :], ACT.Gelu_apprx_tanh).then_inc(v_gelu, 1)

            def turned(i, m, first):
                act.wait_ge(qk_turned, i + 1)
                nc.scalar.copy(qT[:, :, 0:m], ps[0][:, :].rearrange("p (k m) -> p k m", m=P)[:, :, 0:m]).then_inc(qT_ready, 1)
                if not first:
                    act.wait_ge(k_moved, i)
                nc.scalar.copy(kT[:, 1, 0:m], ps[1][:, 0:m]).then_inc(kT_ready, 1)

            def gelu_u(i, m, first):
                act.wait_ge(u_done, i + 1)
                if not first:
                    act.wait_ge(oa_ready, i)
                nc.scalar.activation(u[0:m, :], ps[2][0:m, :], ACT.Gelu_apprx_tanh).then_inc(u_gelu, 1)

            def out_a(i, m, first):
                act.wait_ge(oa_turned, i + 1)
                if not first:
                    act.wait_ge(stored_oa, i * 16)
                view = lambda t: t.rearrange("p (k m) -> p k m", m=P)[:, :, 0:m]
                nc.scalar.copy(view(oaT[:, 0, :]), view(ps[2][:, :])).then_inc(oaT_hi, 1)

            def softmax(i):
                for h in range(NH):
                    act.wait_ge(maxed, i + 1)
                    last = nc.scalar.activation(sc[:, h, :], sc[:, h, :], ACT.Exp, scale=HD ** -0.5,
                                                bias=tiny[:, 16 + h:17 + h], accum_out=tiny[:, 32 + h:33 + h])
                last = nc.scalar.activation(tiny[:, 40:48], tiny[:, 24:32], ACT.Exp).then_inc(probs, 1)

            def tile(i, first=False, m_next=P):
                values(i, P, first)
                if not first:
                    back_probs(i - 1)
                gelu_v(i, P)
                keep_v(i, first)
                turned(i, P, first)
                if not first:
                    back_out(i - 1)
                gelu_u(i, P, first)
                high(i + 1, m_next)
                out_a(i, P, first)
                softmax(i)
                keep_k(i)

            act.wait_ge(ws_turned, 1)
            nc.scalar.copy(wsT[:, :, :], ps[6][:, :].rearrange("p (g i) -> p g i", i=P)).then_inc(wsT_ready, 1)
            nc.scalar.copy(wsT_s[:, :, :], ps[7][0:MS, 0:4 * MS].rearrange("p (g i) -> p g i", i=MS)).then_inc(wsT_ready, 1)
            square(0, P)
            high(0, P, True)
            square(1, P)
            tile(0, True)
            square(2, P)
            with act.Fori(1, NT - 2) as i:
                tile(i)
                square(i + 2, P)
            tile(NT - 2)
            square(S, MS)
            tile(NT - 1, m_next=MS)
            act.wait_ge(stored_kv, 32)
            values(S, MS, False)
            back_probs(NT - 1)
            gelu_v(S, MS)
            turned(S, MS, False)
            back_out(NT - 1)
            gelu_u(S, MS, False)
            out_a(S, MS, False)
            act.wait_ge(smp_max, 1)
            for j in range(2):
                nc.scalar.activation(s_rows[:, j, :], s_rows[:, j, :], ACT.Exp, scale=HD ** -0.5,
                                     bias=tiny[:, 16 + j:17 + j], accum_out=tiny[:, 32 + j:33 + j])
            nc.scalar.activation(tiny[:, 40:42], tiny[:, 24:26], ACT.Exp).then_inc(probs, 1)
            act.wait_ge(smp_out, 1)
            act.wait_ge(stored_ob, 16 * NT)
            nc.scalar.copy(obT[:, 0, :].rearrange("p (k m) -> p k m", m=P)[:, :, 0:MS], obT_f).then_inc(obT_hi, 1)

        @block.vector
        def _(dve):
            def norm(i, m, g):
                dve.wait_ge(rrms, i + 1)
                nc.vector.scalar_tensor_tensor(out=x[0:m, :], in0=x[0:m, :], scalar=tiny[0:m, 2:3], in1=g[0:m, 0, :],
                                               op0=ALU.mult, op1=ALU.mult).then_inc(d_norm, 1)
                dve.wait_ge(d_norm, i + 1)
                nc.vector.tensor_tensor(x[0:m, :], x[0:m, :], g[0:m, 1, :], ALU.add).then_inc(h_ready, 1)

            def low(i, m):
                dve.wait_ge(hi_ready, i + 1)
                for n in range(2):
                    last = nc.vector.tensor_tensor(hT[1][:, 4 * n:4 * n + 4, 0:m],
                                                   ps[n][:, :].rearrange("p (k m) -> p k m", m=P)[:, :, 0:m],
                                                   hT[0][:, 4 * n:4 * n + 4, 0:m].bitcast(F32), ALU.subtract)
                last.then_inc(lo_ready, 1)

            def rotary(i, m, src, heads, c, done):
                w = heads * HD
                r3 = lambda t: t[0:m, 0:w].rearrange("p (h d) -> p h d", d=HD)
                co = rope[0:m, 0:HD].unsqueeze(1).to_broadcast([m, heads, HD])
                si = rope[0:m, HD:HD + HALF].unsqueeze(1).to_broadcast([m, heads, HALF])
                so = rope[0:m, HD + HALF:2 * HD].unsqueeze(1).to_broadcast([m, heads, HALF])
                nc.vector.tensor_tensor(r3(t1), r3(src), co, ALU.mult)
                nc.vector.tensor_tensor(r3(t2)[:, :, 0:HALF], r3(src)[:, :, HALF:HD], si, ALU.mult)
                nc.vector.tensor_tensor(r3(t2)[:, :, HALF:HD], r3(src)[:, :, 0:HALF], so, ALU.mult).then_inc(done, 1)
                dve.wait_ge(done, i + 1)

            def queries(i, m):
                c = Count(i, 4)
                dve.wait_ge(rope_in, i * 16 + 16)
                dve.wait_ge(q_done, i + 1)
                rotary(i, m, ps[3], NH, c, q_parts)
                nc.vector.tensor_tensor(qr[0:m, :, :, :].rearrange("p c g d -> p g c d"),
                                        t1[0:m, :].rearrange("p (g c d) -> p g c d", g=NKV, c=NC),
                                        t2[0:m, :].rearrange("p (g c d) -> p g c d", g=NKV, c=NC), ALU.add).then_inc(d_front, 1)
                return c

            def keys(i, m, c):
                dve.wait_ge(d_front, c.next())
                dve.wait_ge(vb_ready, i + 1)
                rotary(i, m, ps[2], NKV, c, k_parts)
                nc.vector.tensor_tensor(kr[0:m, :], t1[0:m, 0:128], t2[0:m, 0:128], ALU.add).then_inc(qk_rot, 1)

            def norm_v(i, m, c, between=None):
                dve.wait_ge(v_gelu, i + 1)
                nc.vector.bn_stats(stats[0:m, 0:6], v[0:m, :]).then_inc(d_front, 1)
                wait_apart(dve, d_front, c.next(), passed)
                nc.vector.bn_aggr(stats[0:m, 6:8], stats[0:m, 0:6]).then_inc(lnr_in, 1)
                dve.wait_ge(lnr_in, i + 1)
                dve.wait_ge(lnr, i + 1)
                nc.vector.tensor_scalar(v[0:m, :], v[0:m, :], stats[0:m, 6:7], tiny[0:m, 4:5], ALU.subtract, ALU.mult).then_inc(d_front, 1)
                if between is not None:
                    between()
                dve.wait_ge(d_front, c.next())
                nc.vector.tensor_tensor(v[0:m, :], v[0:m, :], ln[0:m, 0, :], ALU.mult).then_inc(d_front, 1)
                dve.wait_ge(d_front, c.next())
                nc.vector.tensor_tensor(v[0:m, :], v[0:m, :], ln[0:m, 1, :], ALU.add).then_inc(ln_ready, 1)
                c.all()

            def out_a(i, m, b):
                dve.wait_ge(mixed, i + 1)
                dve.wait_ge(u_gelu, i + 1)
                for g in range(GROUPS_A):
                    at = slice(g * P, (g + 1) * P)
                    last = nc.vector.scalar_tensor_tensor(out=oa[0:m, at], in0=ps[3][0:m, at], scalar=b[0:m, g:g + 1],
                                                          in1=u[0:m, at], op0=ALU.add, op1=ALU.mult)
                last.then_inc(oa_ready, 1)

            def low_a(i, m):
                dve.wait_ge(oaT_hi, i + 1)
                view = lambda t: t.rearrange("p (k m) -> p k m", m=P)[:, :, 0:m]
                nc.vector.tensor_tensor(view(oaT[:, 1, :]), view(ps[2][:, :]), view(oaT[:, 0, :]).bitcast(F32),
                                        ALU.subtract).then_inc(oaT_lo, 1)

            def softmax(i, mask_i):
                c = Count(i, 5)
                dve.wait_ge(scored, i + 1)
                for n in range(4):
                    last = nc.vector.tensor_tensor(sc[:, 2 * n:2 * n + 2, :], ps[4 + n][:, :].rearrange("p (h k) -> p h k", h=2),
                                                   mask_i.unsqueeze(1).to_broadcast([P, 2, 2 * P]), ALU.add)
                last.then_inc(masked, 1)
                dve.wait_ge(masked, i + 1)
                nc.vector.tensor_reduce(tiny[:, 8:16], sc[:, :, :], AX_X, ALU.max).then_inc(d_back, 1)
                dve.wait_ge(d_back, c.next())
                nc.vector.scalar_tensor_tensor(out=tiny[:, 8:16], in0=tiny[:, 8:16], scalar=HD ** -0.5, in1=sink[:, :],
                                               op0=ALU.mult, op1=ALU.max).then_inc(d_back, 1)
                dve.wait_ge(d_back, c.next())
                nc.vector.tensor_scalar(tiny[:, 16:24], tiny[:, 8:16], -1.0, None, ALU.mult).then_inc(d_back, 1)
                nc.vector.tensor_tensor(tiny[:, 24:32], sink[:, :], tiny[:, 8:16], ALU.subtract).then_inc(maxed, 1)
                dve.wait_ge(d_back, c.next())

            def sums(i):
                c = Count(i, 5)
                c.n = 3
                dve.wait_ge(probs, i + 1)
                nc.vector.tensor_tensor(tiny[:, 32:40], tiny[:, 32:40], tiny[:, 40:48], ALU.add).then_inc(d_back, 1)
                dve.wait_ge(d_back, c.next())
                nc.vector.reciprocal(tiny[:, 48:56], tiny[:, 32:40]).then_inc(d_back, 1)
                dve.wait_ge(d_back, c.next())
                c.all()

            def back_probs(i):
                dve.wait_ge(p_turned, i + 1)
                for n in (4, 5):
                    last = nc.vector.tensor_copy(pT[:, 4 * n - 16:4 * n - 12, :], ps[n][:, :].rearrange("p (k m) -> p k m", m=P))
                last.then_inc(pT_d, 1)

            def out_b(i):
                dve.wait_ge(pv_done, i + 1)
                nc.vector.tensor_tensor(ob[:, :].rearrange("p (h d) -> p h d", d=HD), ps[4][:, :].rearrange("p (h d) -> p h d", d=HD),
                                        tiny[:, 48:56].unsqueeze(2).to_broadcast([P, NH, HD]), ALU.mult).then_inc(ob_ready, 1)

            def low_b(i):
                dve.wait_ge(obT_hi, i + 1)
                nc.vector.tensor_tensor(obT[:, 1, :], ps[5][:, :], obT[:, 0, :].bitcast(F32), ALU.subtract).then_inc(obT_lo, 1)

            def tile(i, mask_i, first=False, m_next=P, g_next=mod):
                c = queries(i, P)
                if not first:
                    sums(i - 1)
                keys(i, P, c)
                if not first:
                    back_probs(i - 1)
                norm_v(i, P, c, None if first else lambda: out_b(i - 1))
                if not first:
                    low_b(i - 1)
                norm(i + 1, m_next, g_next)
                out_a(i, P, bs)
                low(i + 1, m_next)
                softmax(i, mask_i)
                low_a(i, P)

            dve.wait_ge(mod_in, 16 * (2 + 2 * DEC_B))
            dve.wait_ge(const_in, 16 * (7 + DEC_B + DEC_B * NKV))
            norm(0, P, mod)
            low(0, P)
            tile(0, mask[:, 0, :], first=True)
            with dve.Fori(1, NT - 1) as i:
                tile(i, mask[:, 1, :])
            tile(NT - 1, mask[:, 1, :], m_next=MS, g_next=mod_s)
            c = queries(S, MS)
            sums(NT - 1)
            dve.wait_ge(stored_kv, 32)
            keys(S, MS, c)
            back_probs(NT - 1)
            norm_v(S, MS, c, lambda: out_b(NT - 1))
            low_b(NT - 1)
            out_a(S, MS, bs_s)
            low_a(S, MS)
            for n in range(2):
                dve.wait_ge(smp_turned, n + 1)
                last = nc.vector.tensor_copy(ckT[:, 4 * n:4 * n + 4, :], ps[6 + n][:, :].rearrange("p (b r) -> p b r", b=4)).then_inc(smp_dve, 1)
            dve.wait_ge(smp_scored, 1)
            for g in range(NKV):
                nc.vector.tensor_copy(sT[:, g * P:(g + 1) * P], ps[4 + g][:, 0:P])
                last = nc.vector.tensor_copy(sT2[:, g * P:(g + 1) * P], ps[6 + g][0:DEC_T, 0:P])
            last.then_inc(smp_dve, 2)
            dve.wait_ge(smp_scored, 2)
            nc.vector.tensor_tensor(s_rows[:, :, 0:P], ps[6][:, 0:2 * P].rearrange("p (j k) -> p j k", j=2),
                                    mask_s[:, 0:P].unsqueeze(1).to_broadcast([P, 2, P]), ALU.add).then_inc(smp_dve, 1)
            nc.vector.tensor_tensor(s_rows[:, :, P:P + DEC_T], ps[7][:, 0:2 * DEC_T].rearrange("p (j k) -> p j k", j=2),
                                    mask_s[:, P:P + DEC_T].unsqueeze(1).to_broadcast([P, 2, DEC_T]), ALU.add).then_inc(smp_dve, 1)
            dve.wait_ge(smp_dve, 6)
            nc.vector.tensor_reduce(tiny[:, 8:10], s_rows, AX_X, ALU.max).then_inc(smp_dve, 1)
            dve.wait_ge(smp_dve, 7)
            nc.vector.scalar_tensor_tensor(out=tiny[:, 8:10], in0=tiny[:, 8:10], scalar=HD ** -0.5, in1=sink_s[:, :],
                                           op0=ALU.mult, op1=ALU.max).then_inc(smp_dve, 1)
            dve.wait_ge(smp_dve, 8)
            nc.vector.tensor_scalar(tiny[:, 16:18], tiny[:, 8:10], -1.0, None, ALU.mult).then_inc(smp_dve, 1)
            dve.wait_ge(smp_dve, 9)
            nc.vector.tensor_tensor(tiny[:, 24:26], tiny[:, 16:18], sink_s[:, :], ALU.add).then_inc(smp_max, 1)
            dve.wait_ge(probs, S + 1)
            nc.vector.tensor_tensor(tiny[:, 32:34], tiny[:, 32:34], tiny[:, 40:42], ALU.add).then_inc(smp_dve, 1)
            dve.wait_ge(smp_dve, 10)
            nc.vector.reciprocal(tiny[:, 48:50], tiny[:, 32:34]).then_inc(smp_dve, 1)
            dve.wait_ge(smp_dve, 11)
            nc.vector.tensor_tensor(s_rows, s_rows, tiny[:, 48:50].unsqueeze(2).to_broadcast([P, 2, P + DEC_T]), ALU.mult).then_inc(smp_dve, 1)
            dve.wait_ge(smp_scored, 3)
            nc.vector.tensor_copy(pT_s, ps[4][:, 0:256]).then_inc(smp_dve, 1)
            nc.vector.tensor_copy(pT2_s, ps[5][0:DEC_T, 0:256]).then_inc(smp_dve, 1)
            dve.wait_ge(smp_scored, 4)
            for hh in range(2):
                for g in range(NKV):
                    src = ps[6][0:HD, g * P:(g + 1) * P].rearrange("p (b x h t) -> p h x b t", b=DEC_B, x=2, h=2)[:, hh]
                    dst = obT_f[hh * HD:(hh + 1) * HD, 2 * g:2 * g + 2, :].rearrange("p x (b t) -> p x b t", t=DEC_T)
                    last = nc.vector.tensor_copy(dst, src)
            last.then_inc(smp_out, 1)
            dve.wait_ge(obT_hi, S + 1)
            view = lambda t: t.rearrange("p (k m) -> p k m", m=P)[:, :, 0:MS]
            nc.vector.tensor_tensor(view(obT[:, 1, :]), obT_f, view(obT[:, 0, :]).bitcast(F32), ALU.subtract).then_inc(obT_lo, 1)

        @block.tensor
        def _(pe):
            ident = kept["ident"]

            def turn(out, src, m=P):
                return nc.tensor.transpose(out, src, ident[0:m, 0:m])

            def turn_h(i, m, first=False):
                pe.wait_ge(h_ready, i + 1)
                if not first:
                    pe.wait_ge(qT_ready, i)
                    pe.wait_ge(kT_ready, i)
                for k in range(KD):
                    last = turn(ps[k // 4][:, (k % 4) * P:(k % 4) * P + m], x[0:m, k * P:(k + 1) * P], m)
                last.then_inc(h_turned, 1)

            def project(bank, at, n, m):
                for k in range(KD):
                    last = three(nc.tensor, ps[bank][0:m, 0:n], (hT[0][:, k, 0:m], hT[1][:, k, 0:m]),
                                 (wa[0][:, k, at:at + n], wa[1][:, k, at:at + n]), k == 0, k == KD - 1)
                return last

            def tile(i, m, first=False):
                pe.wait_ge(hi_ready, i + 1)
                pe.wait_ge(lo_ready, i + 1)
                if not first:
                    pe.wait_ge(oa_ready, i)
                project(3, 2 * AW, 512, m).then_inc(q_done, 1)
                if not first:
                    pe.wait_ge(oaT_lo, i)
                project(2, 2 * AW + 512, 256, m).then_inc(kv_done, 1)
                if not first:
                    pe.wait_ge(probs, i)
                    for h in range(NH):
                        for j in range(2):
                            t = 2 * h + j
                            last = turn(ps[4 + t // 4][:, (t % 4) * P:(t % 4 + 1) * P], sc[:, h, j * P:(j + 1) * P])
                    last.then_inc(p_turned, 1)
                pe.wait_ge(q_parts, i + 1)
                project(3, AW, 512, m).then_inc(v_done, 1)
                if not first:
                    pe.wait_ge(pT_a, i)
                    pe.wait_ge(pT_d, i)
                    pe.wait_ge(v_moved, i * 2)
                    for h in range(NH):
                        g = h // NC
                        for j in range(2):
                            last = nc.tensor.matmul(ps[4][:, h * HD:(h + 1) * HD], pT[:, 2 * h + j, :],
                                                    vv[:, j, g * HD:(g + 1) * HD], start=(j == 0), stop=(j == 1))
                    last.then_inc(pv_done, 1)
                pe.wait_ge(qk_rot, i + 1)
                for c in range(NC):
                    turn(ps[0][:, c * P:c * P + m], qr[0:m, c, :, :].rearrange("p g d -> p (g d)"), m)
                turn(ps[1][:, 0:m], kr[0:m, :], m).then_inc(qk_turned, 1)
                if not first:
                    pe.wait_ge(ob_ready, i)
                    for k in range(4):
                        last = turn(ps[5][:, k * P:(k + 1) * P], ob[:, k * P:(k + 1) * P])
                    last.then_inc(ob_turned, 1)
                pe.wait_ge(k_parts, i + 1)
                pe.wait_ge(vb_ready, i + 1)
                project(2, 0, 512, m).then_inc(u_done, 1)
                pe.wait_ge(ln_ready, i + 1)
                for g in range(GROUPS_A):
                    w = wsT[:, g, :] if m == P else wsT_s[:, g, :]
                    last = nc.tensor.matmul(ps[3][0:m, g * P:(g + 1) * P], w, v[0:m, g * P:(g + 1) * P], start=True, stop=True)
                last.then_inc(mixed, 1)

            def scores(i, first):
                pe.wait_ge(qT_ready, i + 1)
                pe.wait_ge(kT_ready, i + 1)
                if not first:
                    pe.wait_ge(obT_lo, i)
                for h in (0, 4, 1, 5, 2, 6, 3, 7):
                    g, c = h // NC, h % NC
                    last = nc.tensor.matmul(ps[4 + h // 2][:, (h % 2) * 2 * P:(h % 2 + 1) * 2 * P],
                                            qT[g * HD:(g + 1) * HD, c, :],
                                            kT[g * HD:(g + 1) * HD, :, :].rearrange("p j k -> p (j k)"), start=True, stop=True)
                last.then_inc(scored, 1)

            def turn_a(i, m):
                pe.wait_ge(oa_ready, i + 1)
                for k in range(4):
                    last = turn(ps[2][:, k * P:k * P + m], oa[0:m, k * P:(k + 1) * P], m)
                last.then_inc(oa_turned, 1)

            pe.wait_ge(ws_ready, 5)
            for g in range(GROUPS_A):
                turn(ps[6][:, g * P:(g + 1) * P], ws[:, g, :])
            for g in range(GROUPS_A):
                last = turn(ps[7][0:MS, g * MS:(g + 1) * MS], ws_s[:, g, :], MS)
            last.then_inc(ws_turned, 1)
            pe.wait_ge(wsT_ready, 2)
            turn_h(0, P, True)
            tile(0, P, True)
            turn_h(1, P)
            scores(0, True)
            turn_a(0, P)
            with pe.Fori(1, NT - 1) as i:
                tile(i, P)
                turn_h(i + 1, P)
                scores(i, False)
                turn_a(i, P)
            tile(NT - 1, P)
            turn_h(S, MS)
            scores(NT - 1, False)
            turn_a(NT - 1, P)
            tile(S, MS)
            turn_a(S, MS)
            pe.wait_ge(cache_in, 16 * (DEC_B + 2))
            for n in range(2):
                if n == 0:
                    pe.wait_ge(obT_lo, NT)
                for b in range(4):
                    last = turn(ps[6 + n][:, b * P:(b + 1) * P], ck[:, 4 * n + b, :])
                last.then_inc(smp_turned, 1)
            pe.wait_ge(smp_dve, 2)
            pe.wait_ge(qT_ready, S + 1)
            pe.wait_ge(kT_ready, S + 1)
            for b in range(DEC_B):
                for g in range(NKV):
                    at = slice(g * P + b * 16, g * P + (b + 1) * 16)
                    rows = slice(g * HD, (g + 1) * HD)
                    q = qT[rows, :, b * DEC_T:(b + 1) * DEC_T]
                    own = slice(b * 16, (b + 1) * 16)
                    nc.tensor.matmul(ps[4 + g][:, own].rearrange("p (c t) -> p c t", t=DEC_T), ckT[rows, b, :], q, start=True, stop=True)
                    last = nc.tensor.matmul(ps[6 + g][0:DEC_T, own].rearrange("p (c t) -> p c t", t=DEC_T),
                                            kT[rows, 1, b * DEC_T:(b + 1) * DEC_T], q, start=True, stop=True)
            last.then_inc(smp_scored, 1)
            pe.wait_ge(smp_dve, 4)
            for j in range(2):
                turn(ps[6][:, j * P:(j + 1) * P], sT[:, j * P:(j + 1) * P])
                last = turn(ps[7][:, j * DEC_T:(j + 1) * DEC_T], sT2[:, j * P:(j + 1) * P], DEC_T)
            last.then_inc(smp_scored, 1)
            pe.wait_ge(smp_dve, 12)
            for j in range(2):
                turn(ps[4][:, j * P:(j + 1) * P], s_rows[:, j, 0:P])
                last = turn(ps[5][0:DEC_T, j * P:(j + 1) * P], s_rows[:, j, P:P + DEC_T])
            last.then_inc(smp_scored, 1)
            pe.wait_ge(smp_dve, 14)
            pe.wait_ge(vnew_in, 16)
            for b in range(DEC_B):
                for g in range(NKV):
                    at = slice(g * P + b * 16, g * P + (b + 1) * 16)
                    cols = slice(g * HD, (g + 1) * HD)
                    nc.tensor.matmul(ps[6][0:HD, at], cv[:, b, cols], pT_s[:, at], start=True, stop=False)
                    last = nc.tensor.matmul(ps[6][0:HD, at], v_new[:, b, cols], pT2_s[:, at], start=False, stop=True)
            last.then_inc(smp_scored, 1)


def view(t, m, n):
    return t.rearrange("p (k m) -> p k m", m=P)[:, 0:n, 0:m]


def sweep_gate_a(nc, a, s):
    with ExitStack() as ctx:
        sb, sem = tools(nc, ctx)
        ps = banks(nc, ctx, "ga")
        KW = KD + 8
        w = [sb(f"w_a_{n}", [P, KW, D], F32R) for n in ("hi", "lo")]
        raw = sb("w_a_raw", [P, 2, D])
        hb = sb("h_parts", [P, 2, 2 * D], F32R)
        ob = sb("mixer_parts", [P, 2, 2, 2 * AW], F32R)
        tg = sb("tanh_rows", [P, D])
        ma = sb("ma_rows", [P, 2, D])
        pb = sb("pb_rows", [P, 2, D])
        raw_in, raw_hi, raw_lo = (sem("ga_raw_in0"), sem("ga_raw_in1")), sem("ga_raw_hi"), sem("ga_raw_lo")
        tile_in = (sem("ga_tile_in0"), sem("ga_tile_in1"))
        gated, pa_done, pb_done = sem("ga_gate"), sem("ga_pa"), sem("ga_pb")
        tanhed, ma_ready, pb_ready = sem("ga_tanh"), sem("ga_ma"), sem("ga_pb_rows")
        stored_ma, stored_pb = (sem("ga_st_ma0"), sem("ga_st_ma1")), (sem("ga_st_pb0"), sem("ga_st_pb1"))
        passed = sem("ga_waits_passed")
        block = ctx.enter_context(nc.Block())

        def slices():
            for k in range(KD):
                yield a["w_in"][0, k * P:(k + 1) * P, GATE_A:GATE_A + D]
            for k in range(4):
                yield a["w_pa"][0, k * P:(k + 1) * P, :]
            for k in range(4):
                yield a["w_pb"][0, k * P:(k + 1) * P, :]

        @block.sync
        def _(sp):
            def load(i, par, m, before):
                if before is not None:
                    sp.wait_ge(pb_done, before)
                src = s["hT"][bass.ds(i, 1), :, :].rearrange("o p c -> p (o c)")
                sp.dma_start(view(hb[:, par, :], m, 16).bitcast(F32), view(src, m, 16)).then_inc(tile_in[par], 16)
                for n in range(2):
                    src = s["oT"][bass.ds(i, 1), n, :, :].rearrange("o p c -> p (o c)")
                    sp.dma_start(view(ob[:, par, n, :], m, 8).bitcast(F32), view(src, m, 8)).then_inc(tile_in[par], 16)

            load(0, 0, P, None)
            load(1, 1, P, None)
            for k, src in enumerate(slices()):
                if k >= 2:
                    sp.wait_ge(raw_lo, k - 1)
                sp.dma_start(raw[:, k % 2, :], src).then_inc(raw_in[k % 2], 16)
            with sp.Fori(1, NT // 2) as p:
                for par in range(2):
                    load(p * 2 + par, par, P, p * 2 + par - 1)
            load(NT, 0, MS, NT - 1)

        @block.gpsimd
        def _(pool):
            def store(i, par, m):
                pool.wait_ge(ma_ready, i + 1)
                pool.dma_start(s["ma"][bass.ds(i * P, m), :], ma[0:m, par, :]).then_inc(stored_ma[par], 16)
                wait_apart(pool, pb_ready, i + 1, passed)
                pool.dma_start(s["pb"][bass.ds(i * P, m), :], pb[0:m, par, :]).then_inc(stored_pb[par], 16)

            with pool.Fori(0, NT // 2) as p:
                for par in range(2):
                    store(p * 2 + par, par, P)
            store(NT, 0, MS)
            for par in range(2):
                pool.wait_ge(stored_ma[par], 16 * (NT // 2 + 1 - par))
                pool.wait_ge(stored_pb[par], 16 * (NT // 2 + 1 - par))

        @block.scalar
        def _(act):
            for k in range(KW):
                act.wait_ge(raw_in[k % 2], 16 * (k // 2 + 1))
                nc.scalar.copy(w[0][:, k, :], raw[:, k % 2, :]).then_inc(raw_hi, 1)

            def tile(i, par, m, first, second):
                act.wait_ge(gated, i + 1)
                if not first:
                    act.wait_ge(ma_ready, i)
                for n in range(2):
                    last = nc.scalar.activation(tg[0:m, n * 512:(n + 1) * 512], ps[n][0:m, :], ACT.Tanh, scale=0.5)
                last.then_inc(tanhed, 1)
                act.wait_ge(pb_done, i + 1)
                if second is not None:
                    act.wait_ge(stored_pb[par], second)
                for n in range(2):
                    last = nc.scalar.copy(pb[0:m, par, n * 512:(n + 1) * 512], ps[4 + n][0:m, :])
                last.then_inc(pb_ready, 1)

            tile(0, 0, P, True, None)
            tile(1, 1, P, False, None)
            with act.Fori(1, NT // 2) as p:
                for par in range(2):
                    tile(p * 2 + par, par, P, False, p * 16)
            tile(NT, 0, MS, False, 16 * NT // 2)

        @block.vector
        def _(dve):
            for k in range(KW):
                dve.wait_ge(raw_hi, k + 1)
                nc.vector.tensor_tensor(w[1][:, k, :], raw[:, k % 2, :], w[0][:, k, :].bitcast(F32), ALU.subtract).then_inc(raw_lo, 1)

            def tile(i, par, m, second):
                dve.wait_ge(tanhed, i + 1)
                dve.wait_ge(pa_done, i + 1)
                if second is not None:
                    dve.wait_ge(stored_ma[par], second)
                for n in range(2):
                    at = slice(n * 512, (n + 1) * 512)
                    last = nc.vector.scalar_tensor_tensor(out=ma[0:m, par, at], in0=tg[0:m, at], scalar=1.0, in1=ps[2 + n][0:m, :],
                                                          op0=ALU.add, op1=ALU.mult)
                last.then_inc(ma_ready, 1)

            tile(0, 0, P, None)
            tile(1, 1, P, None)
            with dve.Fori(1, NT // 2) as p:
                for par in range(2):
                    tile(p * 2 + par, par, P, p * 16)
            tile(NT, 0, MS, 16 * NT // 2)

        @block.tensor
        def _(pe):
            def product(bank, lhs, k0, nk, m):
                for n in range(2):
                    for k in range(nk):
                        last = three(nc.tensor, ps[bank + n][0:m, :], (lhs(0, k), lhs(1, k)),
                                     (w[0][:, k0 + k, n * 512:(n + 1) * 512], w[1][:, k0 + k, n * 512:(n + 1) * 512]),
                                     k == 0, k == nk - 1)
                return last

            def tile(i, par, m, landed, first):
                pe.wait_ge(tile_in[par], landed)
                if not first:
                    pe.wait_ge(tanhed, i)
                product(0, lambda h, k: hb[:, par, (h * KD + k) * P:(h * KD + k) * P + m], 0, KD, m).then_inc(gated, 1)
                if not first:
                    pe.wait_ge(ma_ready, i)
                product(2, lambda h, k: ob[:, par, 0, (h * 4 + k) * P:(h * 4 + k) * P + m], KD, 4, m).then_inc(pa_done, 1)
                if not first:
                    pe.wait_ge(pb_ready, i)
                product(4, lambda h, k: ob[:, par, 1, (h * 4 + k) * P:(h * 4 + k) * P + m], KD + 4, 4, m).then_inc(pb_done, 1)

            pe.wait_ge(raw_lo, KW)
            tile(0, 0, P, 48, True)
            tile(1, 1, P, 48, False)
            with pe.Fori(1, NT // 2) as p:
                for par in range(2):
                    tile(p * 2 + par, par, P, p * 48 + 48, False)
            tile(NT, 0, MS, 48 * (NT // 2 + 1), False)


def sweep_gate_b(nc, a, s, kept):
    with ExitStack() as ctx:
        sb, sem = tools(nc, ctx)
        ps = banks(nc, ctx, "gb")
        KW = 2 * KD
        w = [sb(f"w_b_{n}", [P, KW, D], F32R) for n in ("hi", "lo")]
        hb = sb("h_parts_b", [P, 2 * D], F32R)
        tg = sb("tanh_b", [P, D])
        ma = sb("ma_b", [P, D])
        pb = sb("pb_b", [P, D])
        mb = sb("merged", [P, D])
        mT = [sb(f"merged_T_{n}", [P, D], F32R) for n in ("hi", "lo")]
        x = sb("x_b", [P, D])
        h2 = sb("h2_b", [P, D])
        xo = sb("attn_out", [P, D])
        raw = (x, xo)
        h2T = sb("h2_T", [P, D])
        mods = sb("mod_b", [P, 3, D])
        mods_s = sb("mod_b_sample", [MS, 3, D])
        wr = sb("w_router", [P, KD, N_GROUPS + NE])
        rb = sb("b_router", [P, N_GROUPS + NE])
        small = sb("small_b", [P, 128])
        before = sb("before", [P, P])
        ones = sb("ones", [P, P])
        half = sb("half_b", [P, 1])
        zero = h2T[:, 0:TABLE // P].bitcast(I32)
        tb = sb("rms_b", [P, 8])
        r = sb("route", [P, 256])
        idx8 = sb("route_idx", [P, 8], U32)
        slots = sb("route_slots", [P, 2], U32)
        ids = sb("token_ids", [P, 1], I32)
        idf = sb("token_ids_f", [P, 1])

        raw_in, raw_hi, raw_lo = (sem("gb_raw_in0"), sem("gb_raw_in1")), sem("gb_raw_hi"), sem("gb_raw_lo")
        const_in, setup = sem("gb_const"), sem("gb_setup")
        h_in, m_in, x_in = sem("gb_h_in"), sem("gb_m_in"), sem("gb_x_in")
        gated, tanhed, merged = sem("gb_gate"), sem("gb_tanh"), sem("gb_merged")
        m_turned, mT_hi, mT_lo = sem("gb_m_turned"), sem("gb_mT_hi"), sem("gb_mT_lo")
        o_done, x1_step, x1_ready, x1_sumsq, root = sem("gb_o"), sem("gb_x1_step"), sem("gb_x1"), sem("gb_sumsq"), sem("gb_root")
        mean, m_step2, m_step3 = sem("gb_mean"), sem("gb_ready_consts"), sem("gb_gated_b")
        h2_step, h2_ready, h2_turned, h2T_ready = sem("gb_h2_step"), sem("gb_h2"), sem("gb_h2_turned"), sem("gb_h2T")
        logits, r_step, g_diff, g_exp, v_diff, v_exp = [sem(f"gb_{n}") for n in ("logits", "r_step", "g_diff", "g_exp", "v_diff", "v_exp")]
        chosen, ranked, slot_ready = sem("gb_chosen"), sem("gb_ranked"), sem("gb_slots")
        k_step, counted = sem("gb_rank_step"), sem("gb_counted")
        stored_x1, stored_h2, scattered, filled = sem("gb_st_x1"), sem("gb_st_h2"), sem("gb_scattered"), sem("gb_filled")
        passed = sem("gb_waits_passed")
        block = ctx.enter_context(nc.Block())
        S = NT

        @block.sync
        def _(sp):
            for k in range(KW):
                if k >= 2:
                    sp.wait_ge(raw_lo, k - 1)
                src = a["w_in"][0, k * P:(k + 1) * P, GATE_B:GATE_B + D] if k < KD else a["w_o"][0, (k - KD) * P:(k - KD + 1) * P, :]
                sp.dma_start(raw[k % 2][:, :], src).then_inc(raw_in[k % 2], 16)
                if k == 1:
                    for n, part in enumerate((GATE1, SCALE2, SHIFT2)):
                        cols = slice(part * D, (part + 1) * D)
                        sp.dma_start(mods[:, n, :], s["ada"][0:1, cols].to_broadcast([P, D])).then_inc(const_in, 16)
                        for b in range(DEC_B):
                            sp.dma_start(mods_s[b * DEC_T:(b + 1) * DEC_T, n, :],
                                         s["ada"][1 + b:2 + b, cols].to_broadcast([DEC_T, D])).then_inc(const_in, 16)
                    sp.dma_start(wr[:, :, 0:N_GROUPS], a["w_rg"][0].rearrange("(k p) c -> p k c", p=P)).then_inc(const_in, 16)
                    sp.dma_start(wr[:, :, N_GROUPS:], a["w_re"][0].rearrange("(k p) c -> p k c", p=P)).then_inc(const_in, 16)
                    sp.dma_start(rb[:, 0:N_GROUPS], a["b_rg"][0:1, :].to_broadcast([P, N_GROUPS])).then_inc(const_in, 16)
                    sp.dma_start(rb[:, N_GROUPS:], a["b_re"][0:1, :].to_broadcast([P, NE])).then_inc(const_in, 16)
                    sp.dma_start(small[:, :], a["small"]).then_inc(const_in, 16)
                    sp.dma_start(before[:, :], a["before"]).then_inc(const_in, 16)

            def load_h(i, m, first=False):
                if not first:
                    sp.wait_ge(gated, i)
                src = s["hT"][bass.ds(i, 1), :, :].rearrange("o p c -> p (o c)")
                sp.dma_start(view(hb[:, :], m, 16).bitcast(F32), view(src, m, 16)).then_inc(h_in, 16)

            def load_m(i, m, first=False):
                if not first:
                    sp.wait_ge(merged, i)
                sp.dma_start(ma[0:m, :], s["ma"][bass.ds(i * P, m), :]).then_inc(m_in, 16)
                sp.dma_start(pb[0:m, :], s["pb"][bass.ds(i * P, m), :]).then_inc(m_in, 16)

            def load_x(i, m, first=False):
                if not first:
                    wait_apart(sp, h2_ready, i, passed)
                    sp.wait_ge(stored_x1, i * 16)
                src = a["x_prompt"][0, bass.ds(i * P, P), :] if m == P else a["x_sample"].rearrange("b t d -> (b t) d")
                sp.dma_start(x[0:m, :], src).then_inc(x_in, 16)

            def stores(i, m):
                sp.wait_ge(x1_ready, i + 1)
                sp.dma_start(s["x1"][bass.ds(i * P, m), :], x[0:m, :]).then_inc(stored_x1, 16)
                sp.wait_ge(h2_ready, i + 1)
                sp.dma_start(s["h2"][bass.ds(i * P, m), :], h2[0:m, :]).then_inc(stored_h2, 16)

            load_h(0, P, True)
            load_m(0, P, True)
            sp.wait_ge(raw_lo, KW)
            load_x(0, P, True)
            load_h(1, P)
            load_m(1, P)
            with sp.Fori(0, NT - 2) as i:
                load_h(i + 2, P)
                load_m(i + 2, P)
                stores(i, P)
                load_x(i + 1, P)
            load_h(NT, MS)
            load_m(NT, MS)
            stores(NT - 2, P)
            load_x(NT - 1, P)
            stores(NT - 1, P)
            load_x(NT, MS)
            stores(NT, MS)
            sp.wait_ge(stored_x1, 16 * (NT + 1))
            sp.wait_ge(stored_h2, 16 * (NT + 1))

        @block.gpsimd
        def _(pool):
            pool.memset(half[:, :], -0.5).then_inc(setup, 1)
            pool.memset(ones[:, :], 1.0).then_inc(setup, 1)
            pool.memset(zero, 0).then_inc(setup, 1)
            for n in ("wts", "eid", "rank"):
                pool.memset(kept[n][:, :, :], 0.0).then_inc(setup, 1)
            pool.memset(kept["counts"][:, :], 0.0).then_inc(setup, 1)
            pool.wait_ge(setup, 7)
            pool.dma_start(s["table"].rearrange("(p c) o -> p (c o)", p=P), zero).then_inc(filled, 16)
            pool.wait_ge(filled, 16)

            def rms(i, m):
                wait_apart(pool, x1_sumsq, i + 1, passed)
                pool.tensor_scalar(tb[0:m, 1:2], tb[0:m, 0:1], 1.0 / D, EPS, ALU.mult, ALU.add).then_inc(mean, 1)
                pool.wait_ge(mean, i + 1)
                pool.tensor_tensor(tb[0:m, 2:3], tb[0:m, 1:2], half[0:m, :], ALU.pow).then_inc(root, 1)

            def scatter(i, m):
                wait_apart(pool, slot_ready, i + 1, passed)
                for k in range(2):
                    pool.indirect_dma_start(out=s["table"], out_offset=bass.IndirectOffsetOnAxis(ap=slots[0:m, k:k + 1], axis=0),
                                            in_=ids[0:m, :], in_offset=None).then_inc(scattered, 16)

            rms(0, P)
            rms(1, P)
            with pool.Fori(1, NT - 1) as i:
                scatter(i - 1, P)
                rms(i + 1, P)
            scatter(NT - 2, P)
            rms(NT, MS)
            scatter(NT - 1, P)
            scatter(NT, MS)
            pool.wait_ge(scattered, 32 * (NT + 1))

        @block.scalar
        def _(act):
            for k in range(KW):
                act.wait_ge(raw_in[k % 2], 16 * (k // 2 + 1))
                nc.scalar.copy(w[0][:, k, :], raw[k % 2][:, :]).then_inc(raw_hi, 1)

            def gate(i, m, first=False):
                act.wait_ge(gated, i + 1)
                if not first:
                    act.wait_ge(merged, i)
                for n in range(2):
                    last = nc.scalar.activation(tg[0:m, n * 512:(n + 1) * 512], ps[n][0:m, :], ACT.Tanh, scale=0.5)
                last.then_inc(tanhed, 1)

            def split(i, m, first=False):
                act.wait_ge(m_turned, i + 1)
                if not first:
                    act.wait_ge(o_done, i)
                for n in range(2):
                    last = nc.scalar.copy(view(mT[0][:, n * 512:(n + 1) * 512], m, 4), view(ps[2 + n][:, :], m, 4))
                last.then_inc(mT_hi, 1)

            def square(i, m):
                act.wait_ge(x1_ready, i + 1)
                if not isinstance(i, int) or i > 0:
                    act.wait_ge(h2_turned, i)
                    act.wait_ge(stored_h2, i * 16)
                nc.scalar.activation(h2[0:m, :], x[0:m, :], ACT.Square, accum_out=tb[0:m, 0:1]).then_inc(x1_sumsq, 1)

            def h2_out(i, m):
                act.wait_ge(h2_turned, i + 1)
                if not isinstance(i, int) or i > 0:
                    act.wait_ge(logits, i)
                for n in range(2):
                    last = nc.scalar.copy(view(h2T[:, n * 512:(n + 1) * 512], m, 4), view(ps[4 + n][:, :], m, 4))
                last.then_inc(h2T_ready, 1)

            def route(i, m):
                act.wait_ge(g_diff, i + 1)
                nc.scalar.activation(r[0:m, 44:48], r[0:m, 40:44], ACT.Exp, accum_out=r[0:m, 48:49]).then_inc(g_exp, 1)
                act.wait_ge(v_diff, i + 1)
                nc.scalar.activation(r[0:m, 50:51], r[0:m, 49:50], ACT.Exp).then_inc(v_exp, 1)

            gate(0, P, True)
            split(0, P, True)
            gate(1, P)
            square(0, P)
            act.wait_ge(filled, 16)
            with act.Fori(0, NT - 2) as i:
                split(i + 1, P)
                gate(i + 2, P)
                h2_out(i, P)
                square(i + 1, P)
                route(i, P)
            split(NT - 1, P)
            gate(NT, MS)
            h2_out(NT - 2, P)
            square(NT - 1, P)
            route(NT - 2, P)
            split(NT, MS)
            h2_out(NT - 1, P)
            square(NT, MS)
            route(NT - 1, P)
            h2_out(NT, MS)
            route(NT, MS)

        @block.vector
        def _(dve):
            for k in range(KW):
                dve.wait_ge(raw_hi, k + 1)
                nc.vector.tensor_tensor(w[1][:, k, :], raw[k % 2][:, :], w[0][:, k, :].bitcast(F32), ALU.subtract).then_inc(raw_lo, 1)
            dve.wait_ge(const_in, 16 * (3 * (1 + DEC_B) + 6))
            dve.wait_ge(setup, 7)
            nc.vector.tensor_scalar(mods[:, 0, :], mods[:, 0, :], 0.5, None, ALU.mult).then_inc(m_step2, 1)
            nc.vector.tensor_scalar(mods_s[:, 0, :], mods_s[:, 0, :], 0.5, None, ALU.mult).then_inc(m_step2, 1)
            nc.vector.tensor_copy(idf[:, :], small[:, 40:41]).then_inc(m_step2, 1)
            dve.wait_ge(m_step2, 3)

            def gate(i, m, first=False):
                dve.wait_ge(tanhed, i + 1)
                dve.wait_ge(m_in, i * 32 + 32)
                nc.vector.scalar_tensor_tensor(out=tg[0:m, :], in0=tg[0:m, :], scalar=1.0, in1=pb[0:m, :],
                                               op0=ALU.add, op1=ALU.mult).then_inc(m_step3, 1)
                dve.wait_ge(m_step3, i + 1)
                if not first:
                    dve.wait_ge(m_turned, i)
                nc.vector.tensor_tensor(mb[0:m, :], tg[0:m, :], ma[0:m, :], ALU.add).then_inc(merged, 1)

            def split(i, m):
                dve.wait_ge(mT_hi, i + 1)
                for n in range(2):
                    at = slice(n * 512, (n + 1) * 512)
                    last = nc.vector.tensor_tensor(view(mT[1][:, at], m, 4), view(ps[2 + n][:, :], m, 4), view(mT[0][:, at], m, 4).bitcast(F32), ALU.subtract)
                last.then_inc(mT_lo, 1)

            def residual(i, m, g):
                dve.wait_ge(o_done, i + 1)
                dve.wait_ge(x_in, i * 16 + 16)
                for n in range(2):
                    at = slice(n * 512, (n + 1) * 512)
                    last = nc.vector.tensor_tensor(xo[0:m, at], ps[6 + n][0:m, :], g[0:m, 0, at], ALU.mult)
                last.then_inc(x1_step, 1)
                dve.wait_ge(x1_step, i + 1)
                nc.vector.tensor_tensor(x[0:m, :], x[0:m, :], xo[0:m, :], ALU.add).then_inc(x1_ready, 1)

            def norm(i, m, g):
                dve.wait_ge(root, i + 1)
                nc.vector.scalar_tensor_tensor(out=h2[0:m, :], in0=x[0:m, :], scalar=tb[0:m, 2:3], in1=g[0:m, 1, :],
                                               op0=ALU.mult, op1=ALU.mult).then_inc(h2_step, 1)
                dve.wait_ge(h2_step, i + 1)
                nc.vector.tensor_tensor(h2[0:m, :], h2[0:m, :], g[0:m, 2, :], ALU.add).then_inc(h2_ready, 1)

            def route(i, m):
                c = Count(i, ROUTE_STEPS)

                def step(instruction):
                    instruction.then_inc(r_step, 1)
                    if c.n == 8:
                        wait_apart(dve, r_step, c.next(), passed)
                    else:
                        dve.wait_ge(r_step, c.next())

                lg, le = r[0:m, 0:4], r[0:m, 4:36]
                gm, pr, pm, oh = r[0:m, 36:37], r[0:m, 52:56], r[0:m, 37:38], r[0:m, 56:60]
                dve.wait_ge(logits, i + 1)
                step(nc.vector.tensor_tensor(r[0:m, 0:36], ps[4][0:m, 0:36], rb[0:m, :], ALU.add))
                step(nc.vector.tensor_reduce(gm, lg, AX_X, ALU.max))
                nc.vector.tensor_scalar(r[0:m, 40:44], lg, gm, None, ALU.subtract).then_inc(g_diff, 1)
                step(nc.vector.scalar_tensor_tensor(out=pr, in0=lg, scalar=gm, in1=small[0:m, 32:36], op0=ALU.is_equal, op1=ALU.mult))
                step(nc.vector.tensor_reduce(pm, pr, AX_X, ALU.max))
                step(nc.vector.tensor_scalar(oh, pr, pm, None, ALU.is_equal))
                step(nc.vector.tensor_tensor(r[0:m, 64:96].rearrange("p (g e) -> p g e", g=N_GROUPS), le.rearrange("p (g e) -> p g e", g=N_GROUPS),
                                             oh.unsqueeze(2).to_broadcast([m, N_GROUPS, PER_GROUP]), ALU.mult))
                step(nc.vector.tensor_reduce(r[0:m, 96:104], r[0:m, 64:96].rearrange("p (g e) -> p e g", g=N_GROUPS), AX_X, ALU.add))
                step(nc.vector.tensor_tensor(r[0:m, 60:64], oh, small[0:m, 36:40], ALU.mult))
                step(nc.vector.tensor_reduce(r[0:m, 38:39], r[0:m, 60:64], AX_X, ALU.add))
                step(nc.vector.max(r[0:m, 104:112], r[0:m, 96:104]))
                nc.vector.tensor_tensor(r[0:m, 49:50], r[0:m, 105:106], r[0:m, 104:105], ALU.subtract).then_inc(v_diff, 1)
                step(nc.vector.max_index(idx8[0:m, :], r[0:m, 104:112], r[0:m, 96:104]))
                step(nc.vector.tensor_copy(r[0:m, 112:114], idx8[0:m, 0:2]))
                step(nc.vector.scalar_tensor_tensor(out=r[0:m, 114:116], in0=r[0:m, 38:39].to_broadcast([m, 2]), scalar=float(PER_GROUP),
                                                    in1=r[0:m, 112:114], op0=ALU.mult, op1=ALU.add))
                e1, e2 = r[0:m, 114:115], r[0:m, 115:116]
                step(nc.vector.tensor_copy(kept["eid"][0:m, bass.ds(i, 1), :].rearrange("p o k -> p (o k)"), r[0:m, 114:116]))
                oh1, oh2, both = r[0:m, 128:160], r[0:m, 160:192], r[0:m, 192:224]
                step(nc.vector.tensor_scalar(oh1, small[0:m, 0:NE], e1, None, ALU.is_equal))
                step(nc.vector.tensor_scalar(oh2, small[0:m, 0:NE], e2, None, ALU.is_equal))
                nc.vector.tensor_tensor(both, oh1, oh2, ALU.add).then_inc(chosen, 1)
                dve.wait_ge(v_exp, i + 1)
                dve.wait_ge(g_exp, i + 1)
                step(nc.vector.scalar_tensor_tensor(out=r[0:m, 116:117], in0=r[0:m, 50:51], scalar=1.0, in1=r[0:m, 48:49], op0=ALU.add, op1=ALU.mult))
                step(nc.vector.reciprocal(r[0:m, 118:119], r[0:m, 116:117]))
                step(nc.vector.tensor_tensor(r[0:m, 119:120], r[0:m, 118:119], r[0:m, 50:51], ALU.mult))
                step(nc.vector.tensor_copy(kept["wts"][0:m, bass.ds(i, 1), :].rearrange("p o k -> p (o k)"), r[0:m, 118:120]))
                c.all()

            def rank(i, m):
                oh1, oh2 = r[0:m, 128:160], r[0:m, 160:192]
                c = Count(i, 8)

                def step(instruction):
                    instruction.then_inc(k_step, 1)
                    dve.wait_ge(k_step, c.next())

                dve.wait_ge(ranked, i + 1)
                step(nc.vector.tensor_tensor(r[0:m, 224:256], ps[5][0:m, 0:NE], kept["counts"][0:m, :], ALU.add))
                nc.vector.tensor_tensor(kept["counts"][:, :], kept["counts"][:, :], ps[5][:, 32:32 + NE], ALU.add).then_inc(counted, 1)
                step(nc.vector.tensor_tensor(oh1, oh1, r[0:m, 224:256], ALU.mult))
                step(nc.vector.tensor_tensor(oh2, oh2, r[0:m, 224:256], ALU.mult))
                step(nc.vector.tensor_reduce(r[0:m, 120:122], r[0:m, 128:192].rearrange("p (k e) -> p k e", k=2), AX_X, ALU.add))
                step(nc.vector.tensor_copy(kept["rank"][0:m, bass.ds(i, 1), :].rearrange("p o k -> p (o k)"), r[0:m, 120:122]))
                if not isinstance(i, int) or i > 0:
                    dve.wait_ge(scattered, i * 32)
                step(nc.vector.scalar_tensor_tensor(out=r[0:m, 122:124], in0=r[0:m, 114:116], scalar=float(REGION), in1=r[0:m, 120:122],
                                                    op0=ALU.mult, op1=ALU.add))
                step(nc.vector.tensor_copy(ids[0:m, :], idf[0:m, :]))
                step(nc.vector.tensor_scalar(idf[:, :], idf[:, :], float(P), None, ALU.add))
                nc.vector.tensor_copy(slots[0:m, :], r[0:m, 122:124]).then_inc(slot_ready, 1)
                c.all()

            gate(0, P, True)
            split(0, P)
            gate(1, P)
            residual(0, P, mods)
            norm(0, P, mods)

            def step_of(i, m2=P, first=False):
                split(i + 1, P)
                gate(i + 2, m2)
                if not first:
                    rank(i - 1, P)
                residual(i + 1, P, mods)
                norm(i + 1, P, mods)
                route(i, P)

            step_of(0, first=True)
            with dve.Fori(1, NT - 2) as i:
                step_of(i)
            step_of(NT - 2, MS)
            split(NT, MS)
            rank(NT - 2, P)
            residual(NT, MS, mods_s)
            norm(NT, MS, mods_s)
            route(NT - 1, P)
            rank(NT - 1, P)
            route(NT, MS)
            rank(NT, MS)

        @block.tensor
        def _(pe):
            ident = kept["ident"]

            def product(bank, lhs, k0, m):
                for n in range(2):
                    for k in range(KD):
                        last = three(nc.tensor, ps[bank + n][0:m, :], (lhs(0, k), lhs(1, k)),
                                     (w[0][:, k0 + k, n * 512:(n + 1) * 512], w[1][:, k0 + k, n * 512:(n + 1) * 512]),
                                     k == 0, k == KD - 1)
                return last

            def gate(i, m, first=False):
                pe.wait_ge(h_in, i * 16 + 16)
                if not first:
                    pe.wait_ge(tanhed, i)
                product(0, lambda h, k: hb[:, (h * KD + k) * P:(h * KD + k) * P + m], 0, m).then_inc(gated, 1)

            def turn(i, m, src, bank, done):
                for k in range(KD):
                    last = nc.tensor.transpose(ps[bank + k // 4][:, (k % 4) * P:(k % 4) * P + m], src[0:m, k * P:(k + 1) * P], ident[0:m, 0:m])
                last.then_inc(done, 1)

            def turn_m(i, m):
                pe.wait_ge(merged, i + 1)
                turn(i, m, mb, 2, m_turned)

            def out(i, m, first=False):
                pe.wait_ge(mT_hi, i + 1)
                pe.wait_ge(mT_lo, i + 1)
                if not first:
                    pe.wait_ge(x1_step, i)
                product(6, lambda h, k: mT[h][:, k * P:k * P + m], KD, m).then_inc(o_done, 1)

            def turn_h2(i, m):
                pe.wait_ge(h2_ready, i + 1)
                if not isinstance(i, int) or i > 0:
                    pe.wait_ge(counted, i)
                turn(i, m, h2, 4, h2_turned)

            def route(i, m):
                pe.wait_ge(h2T_ready, i + 1)
                for k in range(KD):
                    last = nc.tensor.matmul(ps[4][0:m, 0:N_GROUPS + NE], h2T[:, k * P:k * P + m], wr[:, k, :], start=(k == 0), stop=(k == KD - 1))
                last.then_inc(logits, 1)

            def rank(i, m):
                pe.wait_ge(chosen, i + 1)
                nc.tensor.matmul(ps[5][0:m, 0:NE], before[0:m, 0:m], r[0:m, 192:224], start=True, stop=True)
                nc.tensor.matmul(ps[5][:, 32:32 + NE], ones[0:m, :], r[0:m, 192:224], start=True, stop=True).then_inc(ranked, 1)

            pe.wait_ge(raw_lo, KW)
            gate(0, P, True)
            turn_m(0, P)
            gate(1, P)
            out(0, P, True)
            turn_m(1, P)

            def step_of(i, m2=P, first=False):
                gate(i + 2, m2)
                if not first:
                    rank(i - 1, P)
                turn_h2(i, P)
                out(i + 1, P)
                route(i, P)
                turn_m(i + 2, m2)

            step_of(0, first=True)
            with pe.Fori(1, NT - 2) as i:
                step_of(i)
            step_of(NT - 2, MS)
            rank(NT - 2, P)
            turn_h2(NT - 1, P)
            out(NT, MS)
            route(NT - 1, P)
            rank(NT - 1, P)
            turn_h2(NT, MS)
            route(NT, MS)
            rank(NT, MS)


def list_blocks(nc, a, s, kept):
    with ExitStack() as ctx:
        sb, sem = tools(nc, ctx)
        small = sb("small_l", [P, 128])
        ni = sb("blocks_i", [P, NE], I32)
        n = sb("blocks_f", [P, NE])
        zero = sb("zeros_l", [P, NE])
        ends = sb("block_ends_f", [P, NE])
        starts = sb("block_starts", [P, NE])
        ends_i = sb("block_ends_i", [P, NE], I32)
        m = sb("passed", [P, 2, NE])
        f = sb("fields_f", [P, 8])
        fi = sb("fields_i", [P, 4], I32)
        NK = (NT + 1) * 2
        eq = sb("expert_of_row", [P, NK, NE])
        ys = sb("y_rows_f", [P, NK])
        small_in, step_done, stored, zeroed = sem("l_small_in"), sem("l_step"), sem("l_stored"), sem("l_zeroed")
        listed = sem("l_listed")
        block = ctx.enter_context(nc.Block())

        @block.sync
        def _(sp):
            sp.dma_start(small[:, :], a["small"]).then_inc(small_in, 16)
            sp.wait_ge(listed, 1)
            with nc.allow_non_contiguous_dma(reason="the list of blocks, once"):
                sp.dma_start(s["blocks"].rearrange("f b -> b f"), fi[:, :]).then_inc(stored, 16)
            sp.dma_start(s["cum"], ends_i[0:1, :]).then_inc(stored, 16)
            sp.wait_ge(stored, 32)

        @block.gpsimd
        def _(pool):
            pool.memset(zero[:, :], 0.0).then_inc(zeroed, 1)

        @block.vector
        def _(dve):
            count = [0]

            def step(instruction):
                count[0] += 1
                instruction.then_inc(step_done, 1)
                dve.wait_ge(step_done, count[0])

            dve.wait_ge(small_in, 16)
            dve.wait_ge(zeroed, 1)
            number = small[:, 40:41]
            step(nc.vector.tensor_scalar(n[:, :], kept["counts"][:, :], float(P - 1), None, ALU.add))
            step(nc.vector.tensor_copy(ni[:, :], n[:, :]))
            step(nc.vector.tensor_scalar(ni[:, :], ni[:, :], 7, None, ALU.arith_shift_right))
            step(nc.vector.tensor_copy(n[:, :], ni[:, :]))
            step(nc.vector.tensor_scalar(n[:, :], n[:, :], 1.0, None, ALU.max))
            step(nc.vector.tensor_tensor_scan(ends[:, :], n[:, :], zero[:, :], 0.0, ALU.add, ALU.add))
            step(nc.vector.tensor_tensor(starts[:, :], ends[:, :], n[:, :], ALU.subtract))
            step(nc.vector.tensor_copy(ends_i[:, :], ends[:, :]))
            step(nc.vector.tensor_scalar(m[:, 0, :], ends[:, :], number, None, ALU.is_le))
            step(nc.vector.tensor_tensor(m[:, 1, :], m[:, 0, :], ends[:, :], ALU.mult))
            step(nc.vector.tensor_reduce(f[:, 0:1], m[:, 0, :], AX_X, ALU.add))
            step(nc.vector.tensor_reduce(f[:, 1:2], m[:, 1, :], AX_X, ALU.max))
            step(nc.vector.tensor_scalar(f[:, 2:3], f[:, 0:1], float(NE - 1), None, ALU.min))
            step(nc.vector.tensor_tensor(f[:, 3:4], number, f[:, 1:2], ALU.subtract))
            step(nc.vector.tensor_scalar(f[:, 5:6], f[:, 3:4], float(P), None, ALU.mult))
            step(nc.vector.scalar_tensor_tensor(out=f[:, 4:5], in0=f[:, 2:3], scalar=float(REGION), in1=f[:, 5:6], op0=ALU.mult, op1=ALU.add))
            step(nc.vector.tensor_scalar(f[:, 3:4], f[:, 2:3], 1.0, None, ALU.add))
            step(nc.vector.tensor_copy(fi[:, 0:3], f[:, 2:5]))
            step(nc.vector.tensor_scalar(fi[:, 0:1], fi[:, 0:1], RING - 1, None, ALU.bitwise_and))
            nc.vector.tensor_copy(fi[:, 3:4], ends_i[:, NE - 1:NE]).then_inc(listed, 1)
            eid = kept["eid"][:, :, :].rearrange("p t k -> p (t k)")
            step(nc.vector.tensor_tensor(eq[:, :, :], small[:, 0:NE].unsqueeze(1).to_broadcast([P, NK, NE]),
                                         eid.unsqueeze(2).to_broadcast([P, NK, NE]), ALU.is_equal))
            step(nc.vector.tensor_tensor(eq[:, :, :], eq[:, :, :], starts[:, :].unsqueeze(1).to_broadcast([P, NK, NE]), ALU.mult))
            step(nc.vector.tensor_reduce(ys[:, :], eq[:, :, :], AX_X, ALU.add))
            step(nc.vector.scalar_tensor_tensor(out=ys[:, :], in0=ys[:, :], scalar=float(P), in1=kept["rank"][:, :, :].rearrange("p t k -> p (t k)"),
                                                op0=ALU.mult, op1=ALU.add))
            step(nc.vector.tensor_copy(kept["yrow"][:, :, :].rearrange("p t k -> p (t k)"), ys[:, :]))


def experts(nc, a, s, kept):
    with ExitStack() as ctx:
        sb, sem = tools(nc, ctx)
        ps = banks(nc, ctx, "ex")
        WC = KD * 2 * EH + 2 * D
        w = sb("expert_ring", [P, RING * WC])
        lists = sb("block_lists", [1, 4 * P], I32)
        ends = sb("block_ends_row", [1, NE], I32)
        idx = sb("row_tokens", [P, 2], I32)
        xg = sb("gathered", [P, 2, D])
        xT = [sb(f"gathered_T{n}", [P, KD, P]) for n in range(2)]
        th = sb("tanh_e", [P, 2, EH])
        sg = sb("silu_e", [P, 2, EH])
        h = sb("hidden", [P, 2, EH])
        hT = [sb(f"hidden_T{n}", [P, 2, P]) for n in range(2)]
        y = sb("y_block", [P, 2, D])
        zero = sb("unused_rows", [P, 2 * D])
        lists_in = sem("e_lists_in")
        w_in, w_ready = [sem(f"e_w_in{n}") for n in range(RING)], sem("e_w_ready")
        idx_in, x_in = (sem("e_idx_in0"), sem("e_idx_in1")), (sem("e_x_in0"), sem("e_x_in1"))
        x_turned, xT_a, xT_d = sem("e_x_turned"), sem("e_xT_act"), sem("e_xT_dve")
        gu, tanhed, silued, h_ready, h_turned, hT_ready = [sem(f"e_{n}") for n in ("gate_up", "tanh", "silu", "h", "h_turned", "hT")]
        down, y_a, y_d, stored = sem("e_down"), sem("e_y_act"), sem("e_y_dve"), (sem("e_stored0"), sem("e_stored1"))
        zeroed, filled = sem("e_zeroed"), sem("e_filled")
        passed = sem("e_waits_passed")
        block = ctx.enter_context(nc.Block())
        PAIRS = MAX_BLOCKS // 2

        def listed(eng, field, b):
            at = field * P + b
            ap = lists[0:1, at:at + 1] if isinstance(at, int) else lists[0:1, bass.ds(at, 1)]
            return eng.value_load(ap, min_val=(0, 1, 0, NE)[field], max_val=(RING - 1, NE, TABLE - P, MAX_BLOCKS)[field])

        def pairs(eng, body):
            total = listed(eng, 3, 0)
            with eng.Fori(0, PAIRS) as p:
                with eng.If(p * 2 < total):
                    body(p * 2 + 1, 1)
                    body(p * 2 + 2, 0)

        @block.sync
        def _(sp):
            sp.dma_start(lists[:, :], s["blocks"].rearrange("f b -> (f b)").unsqueeze(0)).then_inc(lists_in, 16)
            sp.dma_start(ends[:, :], s["cum"]).then_inc(lists_in, 16)

            def load(e, slot):
                ww = w[:, slot * WC:(slot + 1) * WC]
                gu_w = ww[:, 0:KD * 2 * EH].rearrange("p (k c) -> p k c", k=KD)
                one = lambda t: t[0, bass.ds(e, 1), :, :]
                sp.dma_start(gu_w[:, :, 0:EH], one(a["w_gate"]).rearrange("o (k p) h -> p (o k) h", p=P)).then_inc(w_in[slot], 16)
                sp.dma_start(gu_w[:, :, EH:], one(a["w_up"]).rearrange("o (k p) h -> p (o k) h", p=P)).then_inc(w_in[slot], 16)
                sp.dma_start(ww[:, KD * 2 * EH:].rearrange("p (k c) -> p k c", k=2),
                             one(a["w_down"]).rearrange("o (k p) d -> p (o k) d", p=P)).then_inc(w_in[slot], 16)

            for e in range(RING):
                load(e, e)
            sp.wait_ge(lists_in, 32)

            def arrived(slot, times):
                sp.wait_ge(w_in[slot], times * 48)
                sp.sem_inc(w_ready, 1)

            arrived(0, 1)
            arrived(1, 1)
            with sp.Fori(1, NE // RING) as g:
                for slot in range(RING):
                    arrived((slot + 2) % RING, g + slot // 2)
                    last = sp.value_load(ends[0:1, bass.ds(g * RING + slot - RING, 1)], min_val=1, max_val=MAX_BLOCKS)
                    wait_apart(sp, down, last, passed)
                    load(g * RING + slot, slot)
            for slot in range(RING - 2, RING):
                arrived(slot, NE // RING)
            sp.wait_ge(zeroed, 1)
            total = listed(sp, 3, 0)
            with sp.Fori(0, PAIRS) as p:
                with sp.If(p * 2 < total):
                    sp.sem_inc(filled, 16)
                with sp.If(p * 2 >= total):
                    rows = s["ys"][bass.ds(p * (2 * P), 2 * P), :].rearrange("(q two) d -> q (two d)", two=2)
                    sp.dma_start(rows, zero[:, :]).then_inc(filled, 16)
            sp.wait_ge(filled, PAIRS * 16)

        @block.gpsimd
        def _(pool):
            pool.memset(zero[:, :], 0.0).then_inc(zeroed, 1)
            pool.wait_ge(lists_in, 32)

            def gather(b, par, n, first=False):
                if not first:
                    wait_apart(pool, x_turned, b - 1, passed)
                row = listed(pool, 2, b)
                pool.dma_start(idx[:, par:par + 1], s["table"][bass.ds(row, P), :]).then_inc(idx_in[par], 16)
                wait_apart(pool, idx_in[par], n * 16 + 16, passed)
                pool.indirect_dma_start(out=xg[:, par, :], out_offset=None, in_=s["h2"],
                                        in_offset=bass.IndirectOffsetOnAxis(ap=idx[:, par:par + 1].bitcast(U32), axis=0)).then_inc(x_in[par], 16)

            gather(0, 0, 0, True)
            gather(1, 1, 0, True)
            total = listed(pool, 3, 0)
            with pool.Fori(0, PAIRS) as p:
                with pool.If(p * 2 < total):
                    gather(p * 2 + 2, 0, p + 1)
                    gather(p * 2 + 3, 1, p + 1)

        @block.scalar
        def _(act):
            act.wait_ge(lists_in, 32)

            def turned(b, par):
                act.wait_ge(x_turned, b + 1)
                nc.scalar.copy(xT[par][:, 0:4, :], ps[0][:, :].rearrange("p (k m) -> p k m", m=P)).then_inc(xT_a, 1)

            def silu(b, par):
                act.wait_ge(gu, b + 1)
                nc.scalar.activation(th[:, par, :], ps[2 + par][:, 0:EH], ACT.Tanh, scale=0.5).then_inc(tanhed, 1)

            def hidden(b, par):
                act.wait_ge(h_turned, b + 1)
                nc.scalar.activation(hT[par][:, :, :], ps[4][:, 0:2 * P].rearrange("p (k m) -> p k m", m=P), ACT.Copy, scale=0.5).then_inc(hT_ready, 1)

            def store(b, par, before):
                act.wait_ge(down, b + 1)
                if before is not None:
                    act.wait_ge(stored[par], before)
                nc.scalar.copy(y[:, par, 0:512], ps[5][:, :]).then_inc(y_a, 1)
                act.wait_ge(y_a, b + 1)
                act.wait_ge(y_d, b + 1)
                act.dma_start(s["ys"][bass.ds(b * P, P), :], y[:, par, :]).then_inc(stored[par], 16)

            turned(0, 0)
            silu(0, 0)
            turned(1, 1)
            total = listed(act, 3, 0)

            def step(b, par, before):
                hidden(b - 1, 1 - par)
                silu(b, par)
                turned(b + 1, 1 - par)
                store(b - 1, 1 - par, before)

            step(1, 1, None)
            step(2, 0, None)
            with act.Fori(1, PAIRS) as p:
                with act.If(p * 2 < total):
                    step(p * 2 + 1, 1, p * 16)
                    step(p * 2 + 2, 0, p * 16)
            for par in range(2):
                wait_apart(act, stored[par], (total + 1) // 2 * 16, passed)

        @block.vector
        def _(dve):
            dve.wait_ge(lists_in, 32)

            def turned(b, par):
                dve.wait_ge(x_turned, b + 1)
                nc.vector.tensor_copy(xT[par][:, 4:8, :], ps[1][:, :].rearrange("p (k m) -> p k m", m=P)).then_inc(xT_d, 1)

            def silu(b, par):
                dve.wait_ge(tanhed, b + 1)
                nc.vector.scalar_tensor_tensor(out=sg[:, par, :], in0=th[:, par, :], scalar=1.0, in1=ps[2 + par][:, 0:EH],
                                               op0=ALU.add, op1=ALU.mult).then_inc(silued, 1)
                dve.wait_ge(silued, b + 1)
                nc.vector.tensor_tensor(h[:, par, :], ps[2 + par][:, EH:2 * EH], sg[:, par, :], ALU.mult).then_inc(h_ready, 1)

            def store(b, par, before):
                dve.wait_ge(down, b + 1)
                if before is not None:
                    dve.wait_ge(stored[par], before)
                nc.vector.tensor_copy(y[:, par, 512:1024], ps[6][:, :]).then_inc(y_d, 1)

            def step(b, par, before):
                silu(b, par)
                turned(b + 1, 1 - par)
                store(b - 1, 1 - par, before)

            turned(0, 0)
            silu(0, 0)
            turned(1, 1)
            total = listed(dve, 3, 0)
            step(1, 1, None)
            step(2, 0, None)
            with dve.Fori(1, PAIRS) as p:
                with dve.If(p * 2 < total):
                    step(p * 2 + 1, 1, p * 16)
                    step(p * 2 + 2, 0, p * 16)

        @block.tensor
        def _(pe):
            ident = kept["ident"]
            pe.wait_ge(lists_in, 32)

            def turn(b, par, n):
                pe.wait_ge(x_in[par], n * 16 + 16)
                if not isinstance(b, int) or b > 0:
                    pe.wait_ge(xT_a, b)
                    pe.wait_ge(xT_d, b)
                for k in range(KD):
                    last = nc.tensor.transpose(ps[k // 4][:, (k % 4) * P:(k % 4 + 1) * P], xg[:, par, k * P:(k + 1) * P], ident[:, :])
                last.then_inc(x_turned, 1)

            def gate_up(b, par):
                need, slot = listed(pe, 1, b), listed(pe, 0, b)
                pe.wait_ge(w_ready, need)
                pe.wait_ge(xT_a, b + 1)
                pe.wait_ge(xT_d, b + 1)
                if not isinstance(b, int) or b > 1:
                    pe.wait_ge(h_ready, b - 1)
                for k in range(KD):
                    last = nc.tensor.matmul(ps[2 + par][:, :], xT[par][:, k, :], w[:, bass.ds(slot * WC + k * 2 * EH, 2 * EH)],
                                            start=(k == 0), stop=(k == KD - 1))
                last.then_inc(gu, 1)

            def turn_h(b, par):
                pe.wait_ge(h_ready, b + 1)
                if not isinstance(b, int) or b > 0:
                    pe.wait_ge(hT_ready, b)
                for k in range(2):
                    last = nc.tensor.transpose(ps[4][:, k * P:(k + 1) * P], h[:, par, k * P:(k + 1) * P], ident[:, :])
                last.then_inc(h_turned, 1)

            def out(b, par):
                slot = listed(pe, 0, b)
                pe.wait_ge(hT_ready, b + 1)
                if not isinstance(b, int) or b > 0:
                    pe.wait_ge(y_a, b)
                    pe.wait_ge(y_d, b)
                for n in range(2):
                    for k in range(2):
                        at = slot * WC + KD * 2 * EH + k * D + n * 512
                        last = nc.tensor.matmul(ps[5 + n][:, :], hT[par][:, k, :], w[:, bass.ds(at, 512)], start=(k == 0), stop=(k == 1))
                last.then_inc(down, 1)

            def step(b, par, n):
                turn_h(b - 1, 1 - par)
                gate_up(b, par)
                turn(b + 1, 1 - par, n)
                out(b - 1, 1 - par)

            turn(0, 0, 0)
            gate_up(0, 0)
            turn(1, 1, 0)
            total = listed(pe, 3, 0)
            step(1, 1, 1)
            step(2, 0, 1)
            with pe.Fori(1, PAIRS) as p:
                with pe.If(p * 2 < total):
                    step(p * 2 + 1, 1, p + 1)
                    step(p * 2 + 2, 0, p + 1)


def combine(nc, a, s, kept, outs):
    y_prompt, y_sample = outs[0], outs[1]
    with ExitStack() as ctx:
        sb, sem = tools(nc, ctx)
        g = sb("expert_pairs", [P, 2, 2, D])
        x = sb("x_c", [P, 2, D])
        o = sb("out_rows", [P, 2, D])
        sq = sb("squares_c", [P, D])
        mods = sb("gate2", [P, D])
        mods_s = sb("gate2_sample", [MS, D])
        gf = sb("normf", [P, D])
        half = sb("half_c", [P, 1])
        t = sb("rms_c", [P, 2, 4])
        at = sb("gather_rows", [P, 4], I32)
        wt2 = sb("weights_now", [P, 4])
        at_ready = sem("c_rows_ready")
        const_in, half_ready = sem("c_const"), sem("c_half")
        g_in, x_in = (sem("c_g_in0"), sem("c_g_in1")), (sem("c_x_in0"), sem("c_x_in1"))
        c_step, summed, sumsq, mean, root, done = sem("c_step"), sem("c_summed"), sem("c_sumsq"), sem("c_mean"), sem("c_root"), sem("c_done")
        stored = (sem("c_stored0"), sem("c_stored1"))
        passed = sem("c_waits_passed")
        block = ctx.enter_context(nc.Block())

        @block.sync
        def _(sp):
            sp.dma_start(mods[:, :], s["ada"][0:1, GATE2 * D:].to_broadcast([P, D])).then_inc(const_in, 16)
            for b in range(DEC_B):
                sp.dma_start(mods_s[b * DEC_T:(b + 1) * DEC_T, :], s["ada"][1 + b:2 + b, GATE2 * D:].to_broadcast([DEC_T, D])).then_inc(const_in, 16)
            sp.dma_start(gf[:, :], a["normf_g"].unsqueeze(0).to_broadcast([P, D])).then_inc(const_in, 16)

            def load(i, par, m, wait=True):
                if wait:
                    sp.wait_ge(summed, i - 1)
                sp.dma_start(x[0:m, par, :], s["x1"][bass.ds(i * P, m), :]).then_inc(x_in[par], 16)

            def store(i, par, dst, m):
                sp.wait_ge(done, i + 1)
                sp.dma_start(dst, o[0:m, par, :]).then_inc(stored[par], 16)

            load(0, 0, P, False)
            load(1, 1, P, False)
            with sp.Fori(0, NT // 2 - 1) as p:
                for par in range(2):
                    load(p * 2 + par + 2, par, P)
                    store(p * 2 + par, par, y_prompt[0, bass.ds((p * 2 + par) * P, P), :], P)
            load(NT, 0, MS)
            for i in (NT - 2, NT - 1):
                store(i, i % 2, y_prompt[0, i * P:(i + 1) * P, :], P)
            store(NT, 0, y_sample.rearrange("b t d -> (b t) d"), MS)
            sp.wait_ge(stored[0], 16 * (NT // 2 + 1))
            sp.wait_ge(stored[1], 16 * (NT // 2))

        @block.gpsimd
        def _(pool):
            pool.memset(half[:, :], -0.5).then_inc(half_ready, 1)
            pool.wait_ge(half_ready, 1)

            def gather(i, par, m, wait=True):
                if wait:
                    wait_apart(pool, summed, i - 1, passed)
                for k in range(2):
                    ap = kept["yrow"][0:m, bass.ds(i, 1), k] if not isinstance(i, int) else kept["yrow"][0:m, i:i + 1, k]
                    pool.tensor_copy(at[0:m, 2 * par + k:2 * par + k + 1], ap).then_inc(at_ready, 1)
                wait_apart(pool, at_ready, i * 2 + 2, passed)
                for k in range(2):
                    pool.indirect_dma_start(out=g[0:m, par, k, :], out_offset=None, in_=s["ys"],
                                            in_offset=bass.IndirectOffsetOnAxis(ap=at[0:m, 2 * par + k:2 * par + k + 1].bitcast(U32), axis=0)).then_inc(g_in[par], 16)

            def rms(i, par, m):
                wait_apart(pool, sumsq, i + 1, passed)
                pool.tensor_scalar(t[0:m, par, 1:2], t[0:m, par, 0:1], 1.0 / D, EPS, ALU.mult, ALU.add).then_inc(mean, 1)
                pool.wait_ge(mean, i + 1)
                pool.tensor_tensor(t[0:m, par, 2:3], t[0:m, par, 1:2], half[0:m, :], ALU.pow).then_inc(root, 1)

            gather(0, 0, P, False)
            gather(1, 1, P, False)
            with pool.Fori(0, NT // 2 - 1) as p:
                for par in range(2):
                    gather(p * 2 + par + 2, par, P)
                    rms(p * 2 + par, par, P)
            gather(NT, 0, MS)
            rms(NT - 2, 0, P)
            rms(NT - 1, 1, P)
            rms(NT, 0, MS)

        @block.scalar
        def _(act):
            def tile(i, par, m, first=False):
                if not first:
                    act.wait_ge(sumsq, i)
                act.wait_ge(summed, i + 1)
                nc.scalar.activation(sq[0:m, :], o[0:m, par, :], ACT.Square, accum_out=t[0:m, par, 0:1]).then_inc(sumsq, 1)

            tile(0, 0, P, True)
            tile(1, 1, P)
            with act.Fori(1, NT // 2) as p:
                for par in range(2):
                    tile(p * 2 + par, par, P)
            tile(NT, 0, MS)

        @block.vector
        def _(dve):
            dve.wait_ge(const_in, 16 * (2 + DEC_B))

            def add(i, par, m, gate, n, before=None):
                w = kept["wts"]
                wt = lambda k: wt2[0:m, 2 * par + k:2 * par + k + 1]
                if before is not None:
                    dve.wait_ge(stored[par], before)
                nc.vector.tensor_copy(wt2[0:m, 2 * par:2 * par + 2], w[0:m, bass.ds(i, 1), :].rearrange("p o k -> p (o k)")).then_inc(c_step, 1)
                dve.wait_ge(g_in[par], n * 32 + 32)
                dve.wait_ge(x_in[par], n * 16 + 16)
                dve.wait_ge(c_step, i * 4 + 1)
                nc.vector.tensor_scalar(o[0:m, par, :], g[0:m, par, 0, :], wt(0), None, ALU.mult).then_inc(c_step, 1)
                dve.wait_ge(c_step, i * 4 + 2)
                nc.vector.scalar_tensor_tensor(out=o[0:m, par, :], in0=g[0:m, par, 1, :], scalar=wt(1), in1=o[0:m, par, :],
                                               op0=ALU.mult, op1=ALU.add).then_inc(c_step, 1)
                dve.wait_ge(c_step, i * 4 + 3)
                nc.vector.tensor_tensor(o[0:m, par, :], o[0:m, par, :], gate[0:m, :], ALU.mult).then_inc(c_step, 1)
                dve.wait_ge(c_step, i * 4 + 4)
                nc.vector.tensor_tensor(o[0:m, par, :], o[0:m, par, :], x[0:m, par, :], ALU.add).then_inc(summed, 1)

            def norm(i, par, m):
                dve.wait_ge(root, i + 1)
                nc.vector.scalar_tensor_tensor(out=o[0:m, par, :], in0=o[0:m, par, :], scalar=t[0:m, par, 2:3], in1=gf[0:m, :],
                                               op0=ALU.mult, op1=ALU.mult).then_inc(done, 1)

            add(0, 0, P, mods, 0)
            add(1, 1, P, mods, 0)
            norm(0, 0, P)
            norm(1, 1, P)
            with dve.Fori(1, NT // 2) as p:
                for par in range(2):
                    add(p * 2 + par, par, P, mods, p, p * 16)
                for par in range(2):
                    norm(p * 2 + par, par, P)
            add(NT, 0, MS, mods_s, NT // 2, 16 * (NT // 2))
            norm(NT, 0, MS)


_INS = ["x_prompt", "x_sample", "cache_k", "cache_v", "c_prompt", "c_sample", "w_ada", "b_ada", "norm1_g", "w_in", "ln_v_g",
        "ln_v_b", "w_s", "b_s", "attn_sinks", "w_pa", "w_pb", "w_o", "norm2_g", "w_rg", "b_rg", "w_re", "b_re", "w_gate", "w_up",
        "w_down", "normf_g"]
_OUTS = [(1, SEQ, D), (DEC_B, DEC_T, D), (1, 1, WIN, NKV, HD), (1, 1, WIN, NKV, HD), (1, DEC_B, DEC_T, NKV, HD),
         (1, DEC_B, DEC_T, NKV, HD), (1, DEC_B, DEC_T, AW)]


def kernel(**inputs):
    import concourse.bacc as bacc
    from concourse.bass_utils import run_bass_kernel_spmd

    nc = bacc.Bacc("TRN2", target_bir_lowering=False, num_devices=1)
    arrays = {f"in_{n}": np.ascontiguousarray(inputs[n]) for n in _INS}
    arrays.update({f"const_{n}": v for n, v in constants().items()})
    a = {}
    for n, v in arrays.items():
        a[n.split("_", 1)[1]] = nc.dram_tensor(n, v.shape, mybir.dt.from_np(v.dtype), kind="ExternalInput").ap()
    outs = [nc.dram_tensor(f"out_{i}", shape, F32, kind="ExternalOutput").ap() for i, shape in enumerate(_OUTS)]
    program(nc, a, outs)
    r = run_bass_kernel_spmd(nc, [arrays], core_ids=[0])
    return tuple(r.results[0][f"out_{i}"] for i in range(len(_OUTS)))
```

```python
from contextlib import ExitStack

import numpy as np

import concourse.bass as bass
from concourse import mybir

F32 = mybir.dt.float32
F32R = mybir.dt.float32r
I32 = mybir.dt.int32
U32 = mybir.dt.uint32
ALU = mybir.AluOpType
ACT = mybir.ActivationFunctionType
AX_X = mybir.AxisListType.X

P = 128
D = 1024
KD = D // P
SEQ = 2048
PAST = 2048
DEC_B, DEC_T = 8, 4
MS = DEC_B * DEC_T
NT = SEQ // P
TOKENS = SEQ + MS
AW = 512
GROUPS_A = 4
HD = 64
NH = 8
NKV = 2
NC = NH // NKV
WIN = 128
N_GROUPS, PER_GROUP = 4, 8
NE = N_GROUPS * PER_GROUP
EH = 256
HALF = HD // 2
EPS = 1e-6
MIX_COLS = 2 * AW + NH * HD + 2 * NKV * HD
GATE_A, GATE_B = MIX_COLS, MIX_COLS + D
MASKED = -1.0e30
REGION = (TOKENS + P - 1) // P * P
MAX_BLOCKS = (2 * TOKENS + NE * P) // P
TABLE = (NE + 1) * REGION + P
ROUTE_STEPS = 20
RING = 4
EXPERT_COLS = KD * 2 * EH + 2 * D
SHIFT1, SCALE1, GATE1, SHIFT2, SCALE2, GATE2 = range(6)


class Count:

    def __init__(self, tile, per):
        self.base, self.n, self.per = tile * per, 0, per

    def next(self):
        self.n += 1
        assert self.n <= self.per
        return self.base + self.n

    def all(self):
        assert self.n == self.per


def constants():
    inv = np.power(10000.0, -2.0 * np.arange(HALF) / HD).astype(np.float32)
    pos = np.concatenate([np.arange(SEQ), np.tile(PAST + np.arange(DEC_T), DEC_B)]).astype(np.float32)
    ang = (pos[:, None] * inv[None, :]).astype(np.float32)
    cos, sin = np.cos(ang).astype(np.float32), np.sin(ang).astype(np.float32)
    rope = np.concatenate([cos, cos, -sin, sin], axis=1).astype(np.float32)
    q = np.arange(P)[:, None]
    k = np.arange(P)[None, :]
    ok_prev, ok_cur = k >= q, k <= q
    mask = np.full((P, 2, 2 * P), MASKED, np.float32)
    mask[:, 0, P:][ok_cur] = 0.0
    mask[:, 1, :P][ok_prev] = 0.0
    mask[:, 1, P:][ok_cur] = 0.0
    t = (np.arange(P) % DEC_T)[:, None]
    mask_s = np.full((P, P + DEC_T), MASKED, np.float32)
    mask_s[:, :P][k >= t] = 0.0
    mask_s[:, P:][np.arange(DEC_T)[None, :] <= t] = 0.0
    small = np.zeros((P, 128), np.float32)
    small[:, 0:NE] = np.arange(NE)
    small[:, 32:36] = [4, 3, 2, 1]
    small[:, 36:40] = [0, 1, 2, 3]
    small[:, 40] = np.arange(P)
    tri = (np.arange(P)[:, None] < np.arange(P)[None, :]).astype(np.float32)
    return {"rope": rope, "mask": mask.reshape(P, 4 * P), "mask_s": mask_s, "small": small, "before": tri,
            "ident": np.eye(P, dtype=np.float32)}


def program(nc, a, outs):
    stack = ExitStack()
    with stack:
        def dram(name, shape, dt=F32):
            return nc.dram_tensor(name, shape, dt).ap()

        s = {
            "ada": dram("ada_rows", (1 + DEC_B, 6 * D)),
            "hT": dram("hT_split", (NT + 1, P, 2 * D)),
            "oT": dram("oT_split", (NT + 1, 2, P, 2 * AW)),
            "ma": dram("gated_a", (TOKENS, D)),
            "pb": dram("out_b_projected", (TOKENS, D)),
            "x1": dram("x_after_mixers", (TOKENS, D)),
            "h2": dram("h2_rows", (TOKENS, D)),
            "table": dram("slot_tokens", (TABLE, 1), I32),
            "blocks": dram("block_list", (4, P), I32),
            "cum": dram("block_ends", (1, NE), I32),
            "ys": dram("expert_rows", (MAX_BLOCKS * P, D)),
        }
        kept = {
            "wts": stack.enter_context(nc.sbuf_tensor("route_weights", [P, NT + 1, 2], F32)),
            "eid": stack.enter_context(nc.sbuf_tensor("route_experts", [P, NT + 1, 2], F32)),
            "rank": stack.enter_context(nc.sbuf_tensor("route_ranks", [P, NT + 1, 2], F32)),
            "counts": stack.enter_context(nc.sbuf_tensor("expert_counts", [P, NE], F32)),
            "ident": stack.enter_context(nc.sbuf_tensor("identity", [P, P], F32)),
            "yrow": stack.enter_context(nc.sbuf_tensor("y_rows", [P, NT + 1, 2], I32)),
        }
        with ExitStack() as weights_a:
            wa = [weights_a.enter_context(nc.sbuf_tensor(f"w_mix_{x}", [P, KD, MIX_COLS], F32R)) for x in ("hi", "lo")]
            condition(nc, a, s, kept, wa)
            sweep_mixers(nc, a, s, kept, wa, outs)
        sweep_gate_a(nc, a, s)
        sweep_gate_b(nc, a, s, kept)
        with nc.sbuf_tensor("expert_ring", [P, RING * EXPERT_COLS], F32) as ring:
            list_blocks(nc, a, s, kept, ring)
            experts(nc, a, s, kept, ring)
        combine(nc, a, s, kept, outs)


def tools(nc, ctx):
    def sb(name, shape, dt=F32):
        return ctx.enter_context(nc.sbuf_tensor(name, shape, dt))

    used = []

    def clear():
        nc.clear_and_free_semaphores(used)
        nc.all_engine_barrier()

    ctx.callback(clear)

    def sem(name):
        used.append(nc.alloc_semaphore(name))
        return used[-1]

    return sb, sem


def wait_apart(eng, sem, value, passed):
    eng.wait_ge(sem, value)
    eng.sem_inc(passed, 1)


def banks(nc, ctx, name):
    return [ctx.enter_context(nc.psum_tensor(f"{name}{n}", [P, 512], F32)) for n in range(8)]


def condition(nc, a, s, kept, wa):
    CH = 256
    NCH = 6 * D // CH
    BUFS = 4
    with ExitStack() as ctx:
        sb, sem = tools(nc, ctx)
        ps = banks(nc, ctx, "cond")
        R = 1 + DEC_B
        c_rows = sb("c_rows", [R, D])
        c_tanh = sb("c_tanh", [R, D])
        c_t = sb("c_t", [P, KD, R])
        w = sb("w_ada_ring", [P, BUFS, KD, CH])
        rows = sb("ada_sums", [R, 6 * D])
        gains = sb("gain_rows", [R, 2, D])
        raw = sb("w_mix_raw", [P, 2, MIX_COLS])
        c_in, ident_in, b_in, raw_in0, raw_in1 = [sem(n) for n in ("c_in", "ident_in", "b_ada_in", "raw_in0", "raw_in1")]
        w_in, raw_in = [sem(f"w_ada_in{n}") for n in range(BUFS)], (raw_in0, raw_in1)
        tanhed, silued, turned, c_ready, summed, row_ready, stored = [
            sem(n) for n in ("c_tanhed", "c_silued", "c_turned", "c_t_ready", "ada_summed", "ada_row", "ada_stored")]
        hi_ready, lo_ready = sem("w_hi_ready"), sem("w_lo_ready")
        block = ctx.enter_context(nc.Block())

        @block.sync
        def _(sp):
            sp.dma_start(c_rows[0:1, :], a["c_prompt"]).then_inc(c_in, 16)
            sp.dma_start(c_rows[1:R, :], a["c_sample"]).then_inc(c_in, 16)
            sp.dma_start(kept["ident"][:, :], a["ident"]).then_inc(ident_in, 16)
            for n in range(NCH):
                if n == BUFS:
                    sp.dma_start(rows[:, :], a["b_ada"][0:1, :].to_broadcast([R, 6 * D])).then_inc(b_in, 16)
                    for k, g in enumerate(("norm1_g", "norm2_g")):
                        sp.dma_start(gains[:, k, :], a[g][0:1, :].to_broadcast([R, D])).then_inc(b_in, 16)
                if n >= BUFS:
                    sp.wait_ge(summed, n - BUFS + 1)
                sp.dma_start(w[:, n % BUFS, :, :],
                             a["w_ada"][0, :, n * CH:(n + 1) * CH].rearrange("(k p) c -> p k c", p=P)).then_inc(w_in[n % BUFS], 16)
            sp.wait_ge(row_ready, NCH + 2)
            sp.dma_start(s["ada"], rows[:, :]).then_inc(stored, 16)
            sp.wait_ge(stored, 16)

        @block.gpsimd
        def _(pool):
            for k in range(KD):
                if k >= 2:
                    pool.wait_ge(lo_ready, k - 1)
                pool.dma_start(raw[:, k % 2, :], a["w_in"][0, k * P:(k + 1) * P, 0:MIX_COLS]).then_inc(raw_in[k % 2], 16)

        @block.scalar
        def _(act):
            act.wait_ge(c_in, 32)
            nc.scalar.activation(c_tanh[:, :], c_rows[:, :], ACT.Tanh, scale=0.5).then_inc(tanhed, 1)
            for k in range(KD):
                act.wait_ge(raw_in[k % 2], 16 * (k // 2 + 1))
                nc.scalar.copy(wa[0][:, k, :], raw[:, k % 2, :]).then_inc(hi_ready, 1)

        @block.vector
        def _(dve):
            dve.wait_ge(tanhed, 1)
            nc.vector.scalar_tensor_tensor(out=c_rows[:, :], in0=c_tanh[:, :], scalar=1.0, in1=c_rows[:, :],
                                           op0=ALU.add, op1=ALU.mult).then_inc(silued, 1)
            dve.wait_ge(turned, 1)
            nc.vector.tensor_scalar(c_t[:, :, :], ps[0][:, 0:KD * R].rearrange("p (k r) -> p k r", r=R), 0.5, None,
                                    ALU.mult).then_inc(c_ready, 1)
            dve.wait_ge(b_in, 48)
            for n in range(NCH):
                if n % 3 == 0:
                    k = n // 3
                    dve.wait_ge(hi_ready, k + 1)
                    nc.vector.tensor_tensor(wa[1][:, k, :], raw[:, k % 2, :], wa[0][:, k, :].bitcast(F32),
                                            ALU.subtract).then_inc(lo_ready, 1)
                dve.wait_ge(summed, n + 1)
                at = slice(n * CH, (n + 1) * CH)
                nc.vector.tensor_tensor(rows[:, at], ps[1 + n % 2][0:R, 0:CH], rows[:, at], ALU.add).then_inc(row_ready, 1)
            dve.wait_ge(row_ready, NCH)
            for n, at in enumerate((SCALE1, SCALE2)):
                part = rows[:, at * D:(at + 1) * D]
                nc.vector.scalar_tensor_tensor(out=part, in0=part, scalar=1.0, in1=gains[:, n, :],
                                               op0=ALU.add, op1=ALU.mult).then_inc(row_ready, 1)

        @block.tensor
        def _(pe):
            pe.wait_ge(silued, 1)
            pe.wait_ge(ident_in, 16)
            for k in range(KD):
                last = nc.tensor.transpose(ps[0][:, k * R:(k + 1) * R], c_rows[:, k * P:(k + 1) * P],
                                           kept["ident"][0:R, 0:R])
            last.then_inc(turned, 1)
            pe.wait_ge(c_ready, 1)
            for n in range(NCH):
                pe.wait_ge(w_in[n % BUFS], 16 * (n // BUFS + 1))
                if n >= 2:
                    pe.wait_ge(row_ready, n - 1)
                for k in range(KD):
                    last = nc.tensor.matmul(ps[1 + n % 2][0:R, 0:CH], c_t[:, k, :], w[:, n % BUFS, k, :],
                                            start=(k == 0), stop=(k == KD - 1))
                last.then_inc(summed, 1)


def three(pe, out, left, right, first=True, last=True):
    nc_mm = pe.matmul
    nc_mm(out, left[0], right[0], start=first, stop=False)
    nc_mm(out, left[1], right[0], start=False, stop=False)
    return nc_mm(out, left[0], right[1], start=False, stop=last)


def sweep_mixers(nc, a, s, kept, wa, outs):
    k_prompt, v_prompt, k_sample, v_sample, chunk_v = outs[2:]
    with ExitStack() as ctx:
        sb, sem = tools(nc, ctx)
        ps = banks(nc, ctx, "mix")
        x = sb("x_rows", [P, D])
        hT = [sb(f"hT_{n}", [P, KD, P], F32R) for n in ("hi", "lo")]
        mod = sb("mod_prompt", [P, 2, D])
        mod_s = sb("mod_sample", [MS, 2, D])
        u = sb("u_rows", [P, AW])
        v = sb("v_rows", [P, AW])
        ln = sb("ln_rows", [P, 2, AW])
        t1 = sb("rope_cos_part", [P, AW])
        t2 = sb("rope_sin_part", [P, AW])
        qr = sb("q_rotated", [P, NC, NKV, HD])
        kr = sb("k_rotated", [P, NKV * HD])
        qT = sb("qT", [P, NC, P])
        kT = sb("kT_prev_cur", [P, 2, P])
        vv = sb("v_prev_cur_next", [P, 3, NKV * HD])
        sc = sb("scores", [P, NH, 2 * P])
        pT = sb("probs_T", [P, 2 * NH, P])
        ob = sb("out_b_rows", [P, AW])
        oa = sb("out_a_rows", [P, AW])
        oaT = sb("out_a_T", [P, 2, AW], F32R)
        obT = sb("out_b_T", [P, 2, AW], F32R)
        rope = sb("rope_rows", [P, 2 * HD])
        mask = sb("masks", [P, 2, 2 * P])
        mask_s = sb("mask_sample", [P, P + DEC_T])
        ws = sb("w_s_rows", [P, GROUPS_A, P])
        wsT = sb("w_s_T", [P, GROUPS_A, P])
        ws_s = sb("w_s_sample_rows", [MS, GROUPS_A, MS])
        wsT_s = sb("w_s_sample_T", [MS, GROUPS_A, MS])
        bs = sb("b_s_cols", [P, GROUPS_A])
        bs_s = sb("b_s_sample", [MS, GROUPS_A])
        sink = sb("sink_rows", [P, NH])
        sink_s = sb("sink_sample", [P, NKV])
        tiny = sb("tiny", [P, 64])
        stats = sb("ln_stats", [P, 8])
        half = sb("minus_half", [P, 1])
        sq = sb("squares", [P, D])

        x_in, rope_in, const_in, mod_in = sem("x_in"), sem("rope_in"), sem("const_in"), sem("mod_in")
        sample_in = sem("sample_consts_in")
        d_front, d_back, d_norm = sem("dve_front_steps"), sem("dve_back_steps"), sem("dve_norm_steps")
        mean_sq, var_eps, half_ready = sem("mean_sq"), sem("var_eps"), sem("half_ready")
        k_moved, v_moved = sem("k_moved"), sem("v_moved")
        sumsq, rrms, h_ready = sem("sumsq"), sem("rrms"), sem("h_ready")
        h_turned, hi_ready, lo_ready = sem("h_turned"), sem("h_hi_ready"), sem("h_lo_ready")
        q_done, kv_done, v_done, u_done = sem("q_proj"), sem("kv_proj"), sem("v_proj"), sem("u_proj")
        q_parts, k_parts, qk_rot = sem("q_parts"), sem("k_parts"), sem("qk_rotated")
        vb_ready, v_gelu, u_gelu = sem("vb_ready"), sem("v_gelu"), sem("u_gelu")
        ln_ready, lnr_in, lnr = sem("v_n_ready"), sem("ln_var"), sem("ln_rstd")
        qk_turned, qT_ready, kT_ready = sem("qk_turned"), sem("qT_ready"), sem("kT_ready")
        scored, masked, maxed, probs = sem("scored"), sem("masked"), sem("maxed"), sem("probs")
        p_turned, pT_a, pT_d = sem("probs_turned"), sem("pT_act"), sem("pT_dve")
        pv_done, ob_ready, ob_turned, obT_hi, obT_lo = (sem("pv"), sem("out_b"), sem("ob_turned"), sem("obT_hi"), sem("obT_lo"))
        mixed, oa_ready, oa_turned, oaT_hi, oaT_lo = (sem("mixed"), sem("out_a"), sem("oa_turned"), sem("oaT_hi"), sem("oaT_lo"))
        stored_h, stored_oa, stored_ob, stored_kv = sem("stored_h"), sem("stored_oa"), sem("stored_ob"), sem("stored_kv")
        ws_zeroed, ws_ready, ws_turned, wsT_ready = sem("w_s_zeroed"), sem("w_s_ready"), sem("w_s_turned"), sem("w_s_T_ready")
        cache_in, vnew_in = sem("cache_in"), sem("v_new_in")
        smp_turned, smp_scored, smp_dve, smp_max, smp_out = [sem(f"sample_{n}") for n in ("turned", "pe", "dve", "max", "out")]
        passed = sem("waits_passed")
        block = ctx.enter_context(nc.Block())
        S = NT

        def tok(ap, i, m):
            return ap[bass.ds(i * P, m), :] if not isinstance(i, int) else ap[i * P:i * P + m, :]

        ck = mod[:, 0, :].rearrange("p (b d) -> p b d", b=DEC_B)
        cv = mod[:, 1, :].rearrange("p (b d) -> p b d", b=DEC_B)
        ckT = x[:, :].rearrange("p (b r) -> p b r", b=DEC_B)
        sT = t1[:, 0:256]
        sT2 = t2[0:DEC_T, 0:256]
        s_rows = sc[:, 0:2, 0:P + DEC_T]
        pT_s = pT[:, 0:2, :].rearrange("p a b -> p (a b)")
        pT2_s = pT[0:DEC_T, 2:4, :].rearrange("p a b -> p (a b)")
        v_new = pT[0:DEC_T, 4:12, :]
        obT_f = ob[:, 0:4 * MS].rearrange("p (k m) -> p k m", m=MS)

        @block.sync
        def _(sp):
            sp.dma_start(x[:, :], a["x_prompt"][0, 0:P, :]).then_inc(x_in, 16)
            sp.dma_start(mod[:, 0, :], s["ada"][0:1, SCALE1 * D:(SCALE1 + 1) * D].to_broadcast([P, D])).then_inc(mod_in, 16)
            sp.dma_start(mod[:, 1, :], s["ada"][0:1, SHIFT1 * D:(SHIFT1 + 1) * D].to_broadcast([P, D])).then_inc(mod_in, 16)
            sp.dma_start(rope[:, :], a["rope"][0:P, :]).then_inc(rope_in, 16)
            sp.dma_start(ws[:, :, :], a["w_s"][0].rearrange("g i j -> i g j")).then_inc(const_in, 16)
            sp.dma_start(ln[:, 0, :], a["ln_v_g"][0:1, :].to_broadcast([P, AW])).then_inc(const_in, 16)
            sp.dma_start(ln[:, 1, :], a["ln_v_b"][0:1, :].to_broadcast([P, AW])).then_inc(const_in, 16)
            sp.dma_start(mask[:, :, :], a["mask"].rearrange("p (n k) -> p n k", n=2)).then_inc(const_in, 16)
            sp.dma_start(sink[:, :], a["attn_sinks"][0:1, :].to_broadcast([P, NH])).then_inc(const_in, 16)
            with nc.allow_non_contiguous_dma(reason="a few small transposed vectors, once"):
                sp.dma_start(bs[:, :], a["b_s"][0].rearrange("g i -> i g")).then_inc(const_in, 16)

            def sample_constants():
                sp.wait_ge(ws_zeroed, 1)
                for b in range(DEC_B):
                    at = slice(b * DEC_T, (b + 1) * DEC_T)
                    sp.dma_start(ws_s[at, :, at], a["w_s"][0, :, 0:DEC_T, 0:DEC_T].rearrange("g i j -> i g j")).then_inc(cache_in, 16)
                for n, part in enumerate((SCALE1, SHIFT1)):
                    sp.dma_start(mod_s[:, n, :], s["ada"][1:1 + DEC_B, part * D:(part + 1) * D].unsqueeze(1)
                                 .to_broadcast([DEC_B, DEC_T, D])).then_inc(sample_in, 16)
                sp.dma_start(mask_s[:, :], a["mask_s"]).then_inc(sample_in, 16)
                with nc.allow_non_contiguous_dma(reason="a few small transposed vectors, once"):
                    for g in range(GROUPS_A):
                        sp.dma_start(bs_s[:, g:g + 1], a["b_s"][0, g:g + 1, 0:DEC_T].unsqueeze(2)
                                     .to_broadcast([DEC_B, DEC_T, 1])).then_inc(sample_in, 16)
                    by_head = a["attn_sinks"].rearrange("o (h x) -> (o h) x", x=1)
                    for b in range(DEC_B):
                        for g in range(NKV):
                            sp.dma_start(sink_s[b * 16:(b + 1) * 16, g:g + 1],
                                         by_head[g * NC:(g + 1) * NC, :].unsqueeze(1).to_broadcast([NC, DEC_T, 1])).then_inc(sample_in, 16)

            def stores(i, m):
                sp.wait_ge(lo_ready, i + 1)
                sp.wait_ge(hi_ready, i + 1)
                for n in range(2):
                    dst = s["hT"][bass.ds(i, 1), :, n * D:(n + 1) * D] if not isinstance(i, int) else s["hT"][i:i + 1, :, n * D:(n + 1) * D]
                    sp.dma_start(dst.rearrange("o p (k m) -> p (o k) m", m=P)[:, :, 0:m], hT[n][:, :, 0:m].bitcast(F32)).then_inc(stored_h, 16)

            def rows_b(i):
                sp.wait_ge(obT_lo, i + 1)
                dst = s["oT"][bass.ds(i, 1), 1, :, :] if not isinstance(i, int) else s["oT"][i:i + 1, 1, :, :]
                sp.dma_start(dst.rearrange("o p c -> p (o c)"), obT[:, :, :].rearrange("p n c -> p (n c)").bitcast(F32)).then_inc(stored_ob, 16)

            def rows_a(i, m):
                sp.wait_ge(oaT_lo, i + 1)
                dst = s["oT"][bass.ds(i, 1), 0, :, :] if not isinstance(i, int) else s["oT"][i:i + 1, 0, :, :]
                if m == P:
                    sp.dma_start(dst.rearrange("o p c -> p (o c)"), oaT[:, :, :].rearrange("p n c -> p (n c)").bitcast(F32)).then_inc(stored_oa, 16)
                else:
                    sp.dma_start(dst.rearrange("o p (c m) -> p (o c) m", m=P)[:, :, 0:m],
                                 oaT[:, :, :].rearrange("p n (k m) -> p (n k) m", m=P)[:, :, 0:m].bitcast(F32)).then_inc(stored_oa, 16)

            def ahead(i):
                sp.wait_ge(h_turned, i)
                sp.dma_start(x[:, :], tok(a["x_prompt"][0], i, P)).then_inc(x_in, 16)

            def angles(i, m):
                sp.wait_ge(k_parts, i)
                sp.dma_start(rope[0:m, :], tok(a["rope"], i, m)).then_inc(rope_in, 16)

            ahead(1)
            stores(0, P)
            sample_constants()
            angles(1, P)
            ahead(2)
            stores(1, P)
            rows_a(0, P)
            with sp.Fori(1, NT - 2) as i:
                angles(i + 1, P)
                rows_b(i - 1)
                ahead(i + 2)
                stores(i + 1, P)
                rows_a(i, P)
            angles(NT - 1, P)
            rows_b(NT - 3)
            sp.wait_ge(h_turned, NT)
            sp.dma_start(x[0:MS, :], a["x_sample"].rearrange("b t d -> (b t) d")).then_inc(x_in, 16)
            for t, src in ((ck, "cache_k"), (cv, "cache_v")):
                sp.dma_start(t, a[src][0].rearrange("b r g d -> r b (g d)")).then_inc(cache_in, 16)
            stores(NT - 1, P)
            rows_a(NT - 2, P)
            angles(S, MS)
            sp.wait_ge(qk_rot, NT)
            sp.wait_ge(vb_ready, NT)
            sp.dma_start(k_prompt[0, 0].rearrange("r g d -> r (g d)"), kr[:, :]).then_inc(stored_kv, 16)
            sp.dma_start(v_prompt[0, 0].rearrange("r g d -> r (g d)"), vv[:, 2, :]).then_inc(stored_kv, 16)
            rows_b(NT - 2)
            stores(S, MS)
            rows_a(NT - 1, P)
            rows_b(NT - 1)
            sp.wait_ge(qk_rot, S + 1)
            sp.wait_ge(vb_ready, S + 1)
            sp.dma_start(k_sample[0].rearrange("b t g d -> (b t) (g d)"), kr[0:MS, :]).then_inc(stored_kv, 16)
            sp.dma_start(v_sample[0].rearrange("b t g d -> (b t) (g d)"), vv[0:MS, 2, :]).then_inc(stored_kv, 16)
            sp.wait_ge(stored_kv, 64)
            sp.wait_ge(pv_done, NT)
            sp.dma_start(v_new, v_sample[0].rearrange("b t g d -> t b (g d)")).then_inc(vnew_in, 16)
            sp.wait_ge(ln_ready, S + 1)
            sp.dma_start(chunk_v[0].rearrange("b t w -> (b t) w"), v[0:MS, :]).then_inc(stored_kv, 16)
            rows_a(S, MS)
            sp.wait_ge(obT_lo, S + 1)
            sp.dma_start(s["oT"][S, 1].rearrange("p (c m) -> p c m", m=P)[:, :, 0:MS],
                         obT[:, :, :].rearrange("p n (k m) -> p (n k) m", m=P)[:, :, 0:MS].bitcast(F32)).then_inc(stored_ob, 16)
            sp.wait_ge(stored_kv, 80)
            sp.wait_ge(stored_h, 32 * (NT + 1))
            sp.wait_ge(stored_oa, 16 * (NT + 1))
            sp.wait_ge(stored_ob, 16 * (NT + 1))

        @block.gpsimd
        def _(pool):
            pool.memset(half[:, :], -0.5).then_inc(half_ready, 1)
            pool.memset(ws_s[:, :, :], 0.0).then_inc(ws_zeroed, 1)
            pool.memset(kT[:, 0, :], 0.0).then_inc(ws_zeroed, 1)
            pool.memset(vv[:, 0:2, :], 0.0).then_inc(ws_zeroed, 1)
            pool.wait_ge(half_ready, 1)

            def rms_root(i, m):
                wait_apart(pool, sumsq, i + 1, passed)
                pool.tensor_scalar(tiny[0:m, 1:2], tiny[0:m, 0:1], 1.0 / D, EPS, ALU.mult, ALU.add).then_inc(mean_sq, 1)
                pool.wait_ge(mean_sq, i + 1)
                pool.tensor_tensor(tiny[0:m, 2:3], tiny[0:m, 1:2], half[0:m, :], ALU.pow).then_inc(rrms, 1)

            def ln_root(i, m):
                wait_apart(pool, lnr_in, i + 1, passed)
                pool.tensor_scalar(tiny[0:m, 3:4], stats[0:m, 7:8], EPS, None, ALU.add).then_inc(var_eps, 1)
                pool.wait_ge(var_eps, i + 1)
                pool.tensor_tensor(tiny[0:m, 4:5], tiny[0:m, 3:4], half[0:m, :], ALU.pow).then_inc(lnr, 1)

            rms_root(0, P)
            rms_root(1, P)
            pool.wait_ge(ws_zeroed, 3)
            pool.wait_ge(const_in, 16 * 6)
            pool.affine_select(out=ws[:, :, :], in_=ws[:, :, :], compare_op=ALU.is_ge, fill=0.0, base=0,
                               pattern=[[0, GROUPS_A], [-1, P]], channel_multiplier=1).then_inc(ws_ready, 1)
            pool.wait_ge(cache_in, 16 * DEC_B)
            pool.affine_select(out=ws_s[:, :, :], in_=ws_s[:, :, :], compare_op=ALU.is_ge, fill=0.0, base=0,
                               pattern=[[0, GROUPS_A], [-1, MS]], channel_multiplier=1).then_inc(ws_ready, 1)
            with pool.Fori(0, NT - 2) as i:
                ln_root(i, P)
                rms_root(i + 2, P)
            ln_root(NT - 2, P)
            rms_root(S, MS)
            ln_root(NT - 1, P)
            ln_root(S, MS)

        @block.scalar
        def _(act):
            def square(i, m):
                act.wait_ge(x_in, i * 16 + 16)
                nc.scalar.activation(sq[0:m, :], x[0:m, :], ACT.Square, accum_out=tiny[0:m, 0:1]).then_inc(sumsq, 1)

            def high(i, m, first=False):
                act.wait_ge(h_turned, i + 1)
                if not first:
                    act.wait_ge(u_done, i)
                    act.wait_ge(stored_h, i * 32)
                for n in range(2):
                    last = nc.scalar.copy(hT[0][:, 4 * n:4 * n + 4, 0:m],
                                          ps[n][:, :].rearrange("p (k m) -> p k m", m=P)[:, :, 0:m])
                last.then_inc(hi_ready, 1)

            def keep_k(i):
                act.wait_ge(scored, i + 1)
                nc.scalar.copy(kT[:, 0, :], kT[:, 1, :]).then_inc(k_moved, 1)

            def keep_v(i, first):
                if not first:
                    act.wait_ge(pv_done, i)
                nc.scalar.copy(vv[:, 0, :], vv[:, 1, :]).then_inc(v_moved, 1)
                act.wait_ge(v_moved, i * 2 + 1)
                nc.scalar.copy(vv[:, 1, :], vv[:, 2, :]).then_inc(v_moved, 1)

            def back_probs(i):
                act.wait_ge(p_turned, i + 1)
                for n in (6, 7):
                    last = nc.scalar.copy(pT[:, 4 * n - 16:4 * n - 12, :], ps[n][:, :].rearrange("p (k m) -> p k m", m=P))
                last.then_inc(pT_a, 1)

            def back_out(i):
                act.wait_ge(ob_turned, i + 1)
                if not isinstance(i, int) or i > 0:
                    act.wait_ge(stored_ob, i * 16)
                nc.scalar.copy(obT[:, 0, :], ps[5][:, :]).then_inc(obT_hi, 1)

            def values(i, m, first):
                act.wait_ge(kv_done, i + 1)
                if not first:
                    act.wait_ge(v_moved, i * 2)
                nc.scalar.copy(vv[0:m, 2, :], ps[2][0:m, 128:256]).then_inc(vb_ready, 1)

            def gelu_v(i, m):
                act.wait_ge(v_done, i + 1)
                nc.scalar.activation(v[0:m, :], ps[3][0:m, :], ACT.Gelu_apprx_tanh).then_inc(v_gelu, 1)

            def turned(i, m, first):
                act.wait_ge(qk_turned, i + 1)
                nc.scalar.copy(qT[:, :, 0:m], ps[0][:, :].rearrange("p (k m) -> p k m", m=P)[:, :, 0:m]).then_inc(qT_ready, 1)
                if not first:
                    act.wait_ge(k_moved, i)
                nc.scalar.copy(kT[:, 1, 0:m], ps[1][:, 0:m]).then_inc(kT_ready, 1)

            def gelu_u(i, m, first):
                act.wait_ge(u_done, i + 1)
                if not first:
                    act.wait_ge(oa_ready, i)
                nc.scalar.activation(u[0:m, :], ps[2][0:m, :], ACT.Gelu_apprx_tanh).then_inc(u_gelu, 1)

            def out_a(i, m, first):
                act.wait_ge(oa_turned, i + 1)
                if not first:
                    act.wait_ge(stored_oa, i * 16)
                view = lambda t: t.rearrange("p (k m) -> p k m", m=P)[:, :, 0:m]
                nc.scalar.copy(view(oaT[:, 0, :]), view(ps[2][:, :])).then_inc(oaT_hi, 1)

            def softmax(i):
                for h in range(NH):
                    act.wait_ge(maxed, i * 2 + 1 + h // 4)
                    last = nc.scalar.activation(sc[:, h, :], sc[:, h, :], ACT.Exp, scale=HD ** -0.5,
                                                bias=tiny[:, 16 + h:17 + h], accum_out=tiny[:, 32 + h:33 + h])
                last = nc.scalar.activation(tiny[:, 40:48], tiny[:, 24:32], ACT.Exp).then_inc(probs, 1)

            def tile(i, first=False, m_next=P):
                values(i, P, first)
                if not first:
                    back_probs(i - 1)
                gelu_v(i, P)
                keep_v(i, first)
                turned(i, P, first)
                if first:
                    act.wait_ge(ws_turned, 1)
                    nc.scalar.copy(wsT[:, :, :], ps[6][:, :].rearrange("p (g i) -> p g i", i=P)).then_inc(wsT_ready, 1)
                    nc.scalar.copy(wsT_s[:, :, :], ps[7][0:MS, 0:4 * MS].rearrange("p (g i) -> p g i", i=MS)).then_inc(wsT_ready, 1)
                else:
                    back_out(i - 1)
                gelu_u(i, P, first)
                high(i + 1, m_next)
                out_a(i, P, first)
                softmax(i)
                keep_k(i)

            square(0, P)
            high(0, P, True)
            square(1, P)
            tile(0, True)
            square(2, P)
            with act.Fori(1, NT - 2) as i:
                tile(i)
                square(i + 2, P)
            tile(NT - 2)
            square(S, MS)
            tile(NT - 1, m_next=MS)
            act.wait_ge(stored_kv, 32)
            values(S, MS, False)
            back_probs(NT - 1)
            gelu_v(S, MS)
            turned(S, MS, False)
            back_out(NT - 1)
            gelu_u(S, MS, False)
            out_a(S, MS, False)
            act.wait_ge(smp_max, 1)
            for j in range(2):
                nc.scalar.activation(s_rows[:, j, :], s_rows[:, j, :], ACT.Exp, scale=HD ** -0.5,
                                     bias=tiny[:, 16 + j:17 + j], accum_out=tiny[:, 32 + j:33 + j])
            nc.scalar.activation(tiny[:, 40:42], tiny[:, 24:26], ACT.Exp).then_inc(probs, 1)
            act.wait_ge(smp_out, 1)
            act.wait_ge(stored_ob, 16 * NT)
            nc.scalar.copy(obT[:, 0, :].rearrange("p (k m) -> p k m", m=P)[:, :, 0:MS], obT_f).then_inc(obT_hi, 1)

        @block.vector
        def _(dve):
            def norm(i, m, g):
                dve.wait_ge(rrms, i + 1)
                nc.vector.scalar_tensor_tensor(out=x[0:m, :], in0=x[0:m, :], scalar=tiny[0:m, 2:3], in1=g[0:m, 0, :],
                                               op0=ALU.mult, op1=ALU.mult).then_inc(d_norm, 1)
                dve.wait_ge(d_norm, i + 1)
                nc.vector.tensor_tensor(x[0:m, :], x[0:m, :], g[0:m, 1, :], ALU.add).then_inc(h_ready, 1)

            def low(i, m):
                dve.wait_ge(hi_ready, i + 1)
                for n in range(2):
                    last = nc.vector.tensor_tensor(hT[1][:, 4 * n:4 * n + 4, 0:m],
                                                   ps[n][:, :].rearrange("p (k m) -> p k m", m=P)[:, :, 0:m],
                                                   hT[0][:, 4 * n:4 * n + 4, 0:m].bitcast(F32), ALU.subtract)
                last.then_inc(lo_ready, 1)

            def rotary(i, m, src, heads, done):
                w = heads * HD
                r3 = lambda t: t[0:m, 0:w].rearrange("p (h d) -> p h d", d=HD)
                co = rope[0:m, 0:HD].unsqueeze(1).to_broadcast([m, heads, HD])
                si = rope[0:m, HD:HD + HALF].unsqueeze(1).to_broadcast([m, heads, HALF])
                so = rope[0:m, HD + HALF:2 * HD].unsqueeze(1).to_broadcast([m, heads, HALF])
                nc.vector.tensor_tensor(r3(t1), r3(src), co, ALU.mult)
                nc.vector.tensor_tensor(r3(t2)[:, :, 0:HALF], r3(src)[:, :, HALF:HD], si, ALU.mult)
                nc.vector.tensor_tensor(r3(t2)[:, :, HALF:HD], r3(src)[:, :, 0:HALF], so, ALU.mult).then_inc(done, 1)
                dve.wait_ge(done, i + 1)

            def queries(i, m):
                c = Count(i, 4)
                dve.wait_ge(rope_in, i * 16 + 16)
                dve.wait_ge(q_done, i + 1)
                rotary(i, m, ps[3], NH, q_parts)
                nc.vector.tensor_tensor(qr[0:m, :, :, :].rearrange("p c g d -> p g c d"),
                                        t1[0:m, :].rearrange("p (g c d) -> p g c d", g=NKV, c=NC),
                                        t2[0:m, :].rearrange("p (g c d) -> p g c d", g=NKV, c=NC), ALU.add).then_inc(d_front, 1)
                return c

            def keys(i, m, c):
                dve.wait_ge(d_front, c.next())
                dve.wait_ge(vb_ready, i + 1)
                rotary(i, m, ps[2], NKV, k_parts)
                nc.vector.tensor_tensor(kr[0:m, :], t1[0:m, 0:128], t2[0:m, 0:128], ALU.add).then_inc(qk_rot, 1)

            def norm_v(i, m, c, between=None):
                dve.wait_ge(v_gelu, i + 1)
                nc.vector.bn_stats(stats[0:m, 0:6], v[0:m, :]).then_inc(d_front, 1)
                wait_apart(dve, d_front, c.next(), passed)
                nc.vector.bn_aggr(stats[0:m, 6:8], stats[0:m, 0:6]).then_inc(lnr_in, 1)
                dve.wait_ge(lnr_in, i + 1)
                dve.wait_ge(lnr, i + 1)
                nc.vector.tensor_scalar(v[0:m, :], v[0:m, :], stats[0:m, 6:7], tiny[0:m, 4:5], ALU.subtract, ALU.mult).then_inc(d_front, 1)
                if between is not None:
                    between()
                dve.wait_ge(d_front, c.next())
                nc.vector.tensor_tensor(v[0:m, :], v[0:m, :], ln[0:m, 0, :], ALU.mult).then_inc(d_front, 1)
                dve.wait_ge(d_front, c.next())
                nc.vector.tensor_tensor(v[0:m, :], v[0:m, :], ln[0:m, 1, :], ALU.add).then_inc(ln_ready, 1)
                c.all()

            def out_a(i, m, b):
                dve.wait_ge(mixed, i + 1)
                dve.wait_ge(u_gelu, i + 1)
                for g in range(GROUPS_A):
                    at = slice(g * P, (g + 1) * P)
                    last = nc.vector.scalar_tensor_tensor(out=oa[0:m, at], in0=ps[3][0:m, at], scalar=b[0:m, g:g + 1],
                                                          in1=u[0:m, at], op0=ALU.add, op1=ALU.mult)
                last.then_inc(oa_ready, 1)

            def low_a(i, m):
                dve.wait_ge(oaT_hi, i + 1)
                view = lambda t: t.rearrange("p (k m) -> p k m", m=P)[:, :, 0:m]
                nc.vector.tensor_tensor(view(oaT[:, 1, :]), view(ps[2][:, :]), view(oaT[:, 0, :]).bitcast(F32),
                                        ALU.subtract).then_inc(oaT_lo, 1)

            def softmax(i, mask_i, half):
                c = Count(i, 8)
                c.n = 3 * half
                heads = slice(4 * half, 4 * half + 4)
                at = lambda base: tiny[:, base + 4 * half:base + 4 * half + 4]
                if half == 0:
                    dve.wait_ge(scored, i + 1)
                for n in (2 * half, 2 * half + 1):
                    last = nc.vector.tensor_tensor(sc[:, 2 * n:2 * n + 2, :], ps[4 + n][:, :].rearrange("p (h k) -> p h k", h=2),
                                                   mask_i.unsqueeze(1).to_broadcast([P, 2, 2 * P]), ALU.add)
                last.then_inc(masked, 1)
                dve.wait_ge(masked, i * 2 + half + 1)
                nc.vector.tensor_reduce(at(8), sc[:, heads, :], AX_X, ALU.max).then_inc(d_back, 1)
                dve.wait_ge(d_back, c.next())
                nc.vector.scalar_tensor_tensor(out=at(8), in0=at(8), scalar=HD ** -0.5, in1=sink[:, heads],
                                               op0=ALU.mult, op1=ALU.max).then_inc(d_back, 1)
                dve.wait_ge(d_back, c.next())
                nc.vector.tensor_scalar(at(16), at(8), -1.0, None, ALU.mult).then_inc(d_back, 1)
                nc.vector.tensor_tensor(at(24), sink[:, heads], at(8), ALU.subtract).then_inc(maxed, 1)
                dve.wait_ge(d_back, c.next())

            def sums(i):
                c = Count(i, 8)
                c.n = 6
                dve.wait_ge(probs, i + 1)
                nc.vector.tensor_tensor(tiny[:, 32:40], tiny[:, 32:40], tiny[:, 40:48], ALU.add).then_inc(d_back, 1)
                dve.wait_ge(d_back, c.next())
                nc.vector.reciprocal(tiny[:, 48:56], tiny[:, 32:40]).then_inc(d_back, 1)
                dve.wait_ge(d_back, c.next())
                c.all()

            def back_probs(i):
                dve.wait_ge(p_turned, i + 1)
                for n in (4, 5):
                    last = nc.vector.tensor_copy(pT[:, 4 * n - 16:4 * n - 12, :], ps[n][:, :].rearrange("p (k m) -> p k m", m=P))
                last.then_inc(pT_d, 1)

            def out_b(i):
                dve.wait_ge(pv_done, i + 1)
                nc.vector.tensor_tensor(ob[:, :].rearrange("p (h d) -> p h d", d=HD), ps[4][:, :].rearrange("p (h d) -> p h d", d=HD),
                                        tiny[:, 48:56].unsqueeze(2).to_broadcast([P, NH, HD]), ALU.mult).then_inc(ob_ready, 1)

            def low_b(i):
                dve.wait_ge(obT_hi, i + 1)
                nc.vector.tensor_tensor(obT[:, 1, :], ps[5][:, :], obT[:, 0, :].bitcast(F32), ALU.subtract).then_inc(obT_lo, 1)

            def tile(i, mask_i, first=False, m_next=P, g_next=mod):
                c = queries(i, P)
                if not first:
                    sums(i - 1)
                keys(i, P, c)
                if not first:
                    back_probs(i - 1)
                norm_v(i, P, c, None if first else lambda: out_b(i - 1))
                if not first:
                    low_b(i - 1)
                norm(i + 1, m_next, g_next)
                out_a(i, P, bs)
                low(i + 1, m_next)
                softmax(i, mask_i, 0)
                low_a(i, P)
                softmax(i, mask_i, 1)

            dve.wait_ge(mod_in, 32)
            norm(0, P, mod)
            low(0, P)
            dve.wait_ge(const_in, 16 * 6)
            tile(0, mask[:, 0, :], first=True)
            with dve.Fori(1, NT - 1) as i:
                tile(i, mask[:, 1, :])
            dve.wait_ge(sample_in, 16 * (3 + GROUPS_A + DEC_B * NKV))
            tile(NT - 1, mask[:, 1, :], m_next=MS, g_next=mod_s)
            c = queries(S, MS)
            sums(NT - 1)
            dve.wait_ge(stored_kv, 32)
            keys(S, MS, c)
            back_probs(NT - 1)
            norm_v(S, MS, c, lambda: out_b(NT - 1))
            low_b(NT - 1)
            out_a(S, MS, bs_s)
            low_a(S, MS)
            for n in range(2):
                dve.wait_ge(smp_turned, n + 1)
                last = nc.vector.tensor_copy(ckT[:, 4 * n:4 * n + 4, :], ps[6 + n][:, :].rearrange("p (b r) -> p b r", b=4)).then_inc(smp_dve, 1)
            dve.wait_ge(smp_scored, 1)
            for g in range(NKV):
                nc.vector.tensor_copy(sT[:, g * P:(g + 1) * P], ps[4 + g][:, 0:P])
                last = nc.vector.tensor_copy(sT2[:, g * P:(g + 1) * P], ps[6 + g][0:DEC_T, 0:P])
            last.then_inc(smp_dve, 2)
            dve.wait_ge(smp_scored, 2)
            nc.vector.tensor_tensor(s_rows[:, :, 0:P], ps[6][:, 0:2 * P].rearrange("p (j k) -> p j k", j=2),
                                    mask_s[:, 0:P].unsqueeze(1).to_broadcast([P, 2, P]), ALU.add).then_inc(smp_dve, 1)
            nc.vector.tensor_tensor(s_rows[:, :, P:P + DEC_T], ps[7][:, 0:2 * DEC_T].rearrange("p (j k) -> p j k", j=2),
                                    mask_s[:, P:P + DEC_T].unsqueeze(1).to_broadcast([P, 2, DEC_T]), ALU.add).then_inc(smp_dve, 1)
            dve.wait_ge(smp_dve, 6)
            nc.vector.tensor_reduce(tiny[:, 8:10], s_rows, AX_X, ALU.max).then_inc(smp_dve, 1)
            dve.wait_ge(smp_dve, 7)
            nc.vector.scalar_tensor_tensor(out=tiny[:, 8:10], in0=tiny[:, 8:10], scalar=HD ** -0.5, in1=sink_s[:, :],
                                           op0=ALU.mult, op1=ALU.max).then_inc(smp_dve, 1)
            dve.wait_ge(smp_dve, 8)
            nc.vector.tensor_scalar(tiny[:, 16:18], tiny[:, 8:10], -1.0, None, ALU.mult).then_inc(smp_dve, 1)
            dve.wait_ge(smp_dve, 9)
            nc.vector.tensor_tensor(tiny[:, 24:26], tiny[:, 16:18], sink_s[:, :], ALU.add).then_inc(smp_max, 1)
            dve.wait_ge(probs, S + 1)
            nc.vector.tensor_tensor(tiny[:, 32:34], tiny[:, 32:34], tiny[:, 40:42], ALU.add).then_inc(smp_dve, 1)
            dve.wait_ge(smp_dve, 10)
            nc.vector.reciprocal(tiny[:, 48:50], tiny[:, 32:34]).then_inc(smp_dve, 1)
            dve.wait_ge(smp_dve, 11)
            nc.vector.tensor_tensor(s_rows, s_rows, tiny[:, 48:50].unsqueeze(2).to_broadcast([P, 2, P + DEC_T]), ALU.mult).then_inc(smp_dve, 1)
            dve.wait_ge(smp_scored, 3)
            nc.vector.tensor_copy(pT_s, ps[4][:, 0:256]).then_inc(smp_dve, 1)
            nc.vector.tensor_copy(pT2_s, ps[5][0:DEC_T, 0:256]).then_inc(smp_dve, 1)
            dve.wait_ge(smp_scored, 4)
            for hh in range(2):
                for g in range(NKV):
                    src = ps[6][0:HD, g * P:(g + 1) * P].rearrange("p (b x h t) -> p h x b t", b=DEC_B, x=2, h=2)[:, hh]
                    dst = obT_f[hh * HD:(hh + 1) * HD, 2 * g:2 * g + 2, :].rearrange("p x (b t) -> p x b t", t=DEC_T)
                    last = nc.vector.tensor_copy(dst, src)
            last.then_inc(smp_out, 1)
            dve.wait_ge(obT_hi, S + 1)
            view = lambda t: t.rearrange("p (k m) -> p k m", m=P)[:, :, 0:MS]
            nc.vector.tensor_tensor(view(obT[:, 1, :]), obT_f, view(obT[:, 0, :]).bitcast(F32), ALU.subtract).then_inc(obT_lo, 1)

        @block.tensor
        def _(pe):
            ident = kept["ident"]

            def turn(out, src, m=P):
                return nc.tensor.transpose(out, src, ident[0:m, 0:m])

            def turn_h(i, m, first=False):
                pe.wait_ge(h_ready, i + 1)
                if not first:
                    pe.wait_ge(qT_ready, i)
                    pe.wait_ge(kT_ready, i)
                for k in range(KD):
                    last = turn(ps[k // 4][:, (k % 4) * P:(k % 4) * P + m], x[0:m, k * P:(k + 1) * P], m)
                last.then_inc(h_turned, 1)

            def project(bank, at, n, m, ks=range(KD)):
                for k in ks:
                    last = three(nc.tensor, ps[bank][0:m, 0:n], (hT[0][:, k, 0:m], hT[1][:, k, 0:m]),
                                 (wa[0][:, k, at:at + n], wa[1][:, k, at:at + n]), k == 0, k == KD - 1)
                return last

            def tile(i, m, first=False):
                pe.wait_ge(hi_ready, i + 1)
                pe.wait_ge(lo_ready, i + 1)
                if not first:
                    pe.wait_ge(oa_ready, i)
                project(3, 2 * AW, 512, m).then_inc(q_done, 1)
                if not first:
                    pe.wait_ge(oaT_lo, i)
                project(2, 2 * AW + 512, 256, m).then_inc(kv_done, 1)
                if not first:
                    pe.wait_ge(probs, i)
                    for h in range(NH):
                        for j in range(2):
                            t = 2 * h + j
                            last = turn(ps[4 + t // 4][:, (t % 4) * P:(t % 4 + 1) * P], sc[:, h, j * P:(j + 1) * P])
                    last.then_inc(p_turned, 1)
                pe.wait_ge(q_parts, i + 1)
                project(3, AW, 512, m).then_inc(v_done, 1)
                if not first:
                    pe.wait_ge(pT_a, i)
                    pe.wait_ge(pT_d, i)
                    pe.wait_ge(v_moved, i * 2)
                    for h in range(NH):
                        g = h // NC
                        for j in range(2):
                            last = nc.tensor.matmul(ps[4][:, h * HD:(h + 1) * HD], pT[:, 2 * h + j, :],
                                                    vv[:, j, g * HD:(g + 1) * HD], start=(j == 0), stop=(j == 1))
                    last.then_inc(pv_done, 1)
                pe.wait_ge(qk_rot, i + 1)
                for c in range(NC):
                    turn(ps[0][:, c * P:c * P + m], qr[0:m, c, :, :].rearrange("p g d -> p (g d)"), m)
                turn(ps[1][:, 0:m], kr[0:m, :], m).then_inc(qk_turned, 1)
                if first:
                    pe.wait_ge(ws_ready, 2)
                    for g in range(GROUPS_A):
                        turn(ps[6][:, g * P:(g + 1) * P], ws[:, g, :])
                    for g in range(GROUPS_A):
                        last = turn(ps[7][0:MS, g * MS:(g + 1) * MS], ws_s[:, g, :], MS)
                    last.then_inc(ws_turned, 1)
                pe.wait_ge(k_parts, i + 1)
                pe.wait_ge(vb_ready, i + 1)
                project(2, 0, 512, m, range(0, 2))
                if not first:
                    pe.wait_ge(ob_ready, i)
                    for k in range(4):
                        last = turn(ps[5][:, k * P:(k + 1) * P], ob[:, k * P:(k + 1) * P])
                    last.then_inc(ob_turned, 1)
                project(2, 0, 512, m, range(2, KD)).then_inc(u_done, 1)
                pe.wait_ge(ln_ready, i + 1)
                if first:
                    pe.wait_ge(wsT_ready, 2)
                for g in range(GROUPS_A):
                    w = wsT[:, g, :] if m == P else wsT_s[:, g, :]
                    last = nc.tensor.matmul(ps[3][0:m, g * P:(g + 1) * P], w, v[0:m, g * P:(g + 1) * P], start=True, stop=True)
                last.then_inc(mixed, 1)

            def scores(i, first):
                pe.wait_ge(qT_ready, i + 1)
                pe.wait_ge(kT_ready, i + 1)
                if not first:
                    pe.wait_ge(obT_lo, i)
                for h in (0, 4, 1, 5, 2, 6, 3, 7):
                    g, c = h // NC, h % NC
                    last = nc.tensor.matmul(ps[4 + h // 2][:, (h % 2) * 2 * P:(h % 2 + 1) * 2 * P],
                                            qT[g * HD:(g + 1) * HD, c, :],
                                            kT[g * HD:(g + 1) * HD, :, :].rearrange("p j k -> p (j k)"), start=True, stop=True)
                last.then_inc(scored, 1)

            def turn_a(i, m):
                pe.wait_ge(oa_ready, i + 1)
                for k in range(4):
                    last = turn(ps[2][:, k * P:k * P + m], oa[0:m, k * P:(k + 1) * P], m)
                last.then_inc(oa_turned, 1)

            turn_h(0, P, True)
            tile(0, P, True)
            turn_h(1, P)
            scores(0, True)
            turn_a(0, P)
            with pe.Fori(1, NT - 1) as i:
                tile(i, P)
                turn_h(i + 1, P)
                scores(i, False)
                turn_a(i, P)
            tile(NT - 1, P)
            turn_h(S, MS)
            scores(NT - 1, False)
            turn_a(NT - 1, P)
            tile(S, MS)
            turn_a(S, MS)
            pe.wait_ge(cache_in, 16 * (DEC_B + 2))
            for n in range(2):
                if n == 0:
                    pe.wait_ge(obT_lo, NT)
                for b in range(4):
                    last = turn(ps[6 + n][:, b * P:(b + 1) * P], ck[:, 4 * n + b, :])
                last.then_inc(smp_turned, 1)
            pe.wait_ge(smp_dve, 2)
            pe.wait_ge(qT_ready, S + 1)
            pe.wait_ge(kT_ready, S + 1)
            for b in range(DEC_B):
                for g in range(NKV):
                    at = slice(g * P + b * 16, g * P + (b + 1) * 16)
                    rows = slice(g * HD, (g + 1) * HD)
                    q = qT[rows, :, b * DEC_T:(b + 1) * DEC_T]
                    own = slice(b * 16, (b + 1) * 16)
                    nc.tensor.matmul(ps[4 + g][:, own].rearrange("p (c t) -> p c t", t=DEC_T), ckT[rows, b, :], q, start=True, stop=True)
                    last = nc.tensor.matmul(ps[6 + g][0:DEC_T, own].rearrange("p (c t) -> p c t", t=DEC_T),
                                            kT[rows, 1, b * DEC_T:(b + 1) * DEC_T], q, start=True, stop=True)
            last.then_inc(smp_scored, 1)
            pe.wait_ge(smp_dve, 4)
            for j in range(2):
                turn(ps[6][:, j * P:(j + 1) * P], sT[:, j * P:(j + 1) * P])
                last = turn(ps[7][:, j * DEC_T:(j + 1) * DEC_T], sT2[:, j * P:(j + 1) * P], DEC_T)
            last.then_inc(smp_scored, 1)
            pe.wait_ge(smp_dve, 12)
            for j in range(2):
                turn(ps[4][:, j * P:(j + 1) * P], s_rows[:, j, 0:P])
                last = turn(ps[5][0:DEC_T, j * P:(j + 1) * P], s_rows[:, j, P:P + DEC_T])
            last.then_inc(smp_scored, 1)
            pe.wait_ge(smp_dve, 14)
            pe.wait_ge(vnew_in, 16)
            for b in range(DEC_B):
                for g in range(NKV):
                    at = slice(g * P + b * 16, g * P + (b + 1) * 16)
                    cols = slice(g * HD, (g + 1) * HD)
                    nc.tensor.matmul(ps[6][0:HD, at], cv[:, b, cols], pT_s[:, at], start=True, stop=False)
                    last = nc.tensor.matmul(ps[6][0:HD, at], v_new[:, b, cols], pT2_s[:, at], start=False, stop=True)
            last.then_inc(smp_scored, 1)


def view(t, m, n):
    return t.rearrange("p (k m) -> p k m", m=P)[:, 0:n, 0:m]


def sweep_gate_a(nc, a, s):
    with ExitStack() as ctx:
        sb, sem = tools(nc, ctx)
        ps = banks(nc, ctx, "ga")
        KW = KD + 8
        w = [sb(f"w_a_{n}", [P, KW, D], F32R) for n in ("hi", "lo")]
        hb = sb("h_parts", [P, 2, 2 * D], F32R)
        ob = sb("mixer_parts", [P, 2, 2, 2 * AW], F32R)
        tg = sb("tanh_rows", [P, D])
        ma = sb("ma_rows", [P, 2, D])
        pb = sb("pb_rows", [P, 2, D])
        raw = (sb("w_a_raw0", [P, D])[:, :], sb("w_a_raw1", [P, D])[:, :], ma[:, 0, :], ma[:, 1, :])
        raw_in, raw_hi, raw_lo = [sem(f"ga_raw_in{n}") for n in range(4)], sem("ga_raw_hi"), sem("ga_raw_lo")
        tile_in = (sem("ga_tile_in0"), sem("ga_tile_in1"))
        gated, pa_done, pb_done = sem("ga_gate"), sem("ga_pa"), sem("ga_pb")
        tanhed, ma_ready, pb_ready = sem("ga_tanh"), sem("ga_ma"), sem("ga_pb_rows")
        stored_ma, stored_pb = (sem("ga_st_ma0"), sem("ga_st_ma1")), (sem("ga_st_pb0"), sem("ga_st_pb1"))
        passed = sem("ga_waits_passed")
        block = ctx.enter_context(nc.Block())

        def slices():
            for k in range(KD):
                yield a["w_in"][0, k * P:(k + 1) * P, GATE_A:GATE_A + D]
            for k in range(4):
                yield a["w_pa"][0, k * P:(k + 1) * P, :]
            for k in range(4):
                yield a["w_pb"][0, k * P:(k + 1) * P, :]

        @block.sync
        def _(sp):
            def load_h(i, par, m):
                src = s["hT"][bass.ds(i, 1), :, :].rearrange("o p c -> p (o c)")
                sp.dma_start(view(hb[:, par, :], m, 16).bitcast(F32), view(src, m, 16)).then_inc(tile_in[par], 16)

            def load_o(i, par, m):
                for n in range(2):
                    src = s["oT"][bass.ds(i, 1), n, :, :].rearrange("o p c -> p (o c)")
                    sp.dma_start(view(ob[:, par, n, :], m, 8).bitcast(F32), view(src, m, 8)).then_inc(tile_in[par], 16)

            def load(i, par, m, before):
                sp.wait_ge(pb_done, before)
                load_h(i, par, m)
                load_o(i, par, m)

            load_h(0, 0, P)
            for k, src in enumerate(slices()):
                if k >= 4:
                    sp.wait_ge(raw_lo, k - 3)
                sp.dma_start(raw[k % 4], src).then_inc(raw_in[k % 4], 16)
                if k == KD:
                    load_o(0, 0, P)
            load_h(1, 1, P)
            load_o(1, 1, P)
            with sp.Fori(1, NT // 2) as p:
                for par in range(2):
                    load(p * 2 + par, par, P, p * 2 + par - 1)
            load(NT, 0, MS, NT - 1)

        @block.gpsimd
        def _(pool):
            def store(i, par, m):
                pool.wait_ge(ma_ready, i + 1)
                pool.dma_start(s["ma"][bass.ds(i * P, m), :], ma[0:m, par, :]).then_inc(stored_ma[par], 16)
                wait_apart(pool, pb_ready, i + 1, passed)
                pool.dma_start(s["pb"][bass.ds(i * P, m), :], pb[0:m, par, :]).then_inc(stored_pb[par], 16)

            with pool.Fori(0, NT // 2) as p:
                for par in range(2):
                    store(p * 2 + par, par, P)
            store(NT, 0, MS)
            for par in range(2):
                pool.wait_ge(stored_ma[par], 16 * (NT // 2 + 1 - par))
                pool.wait_ge(stored_pb[par], 16 * (NT // 2 + 1 - par))

        @block.scalar
        def _(act):
            for k in range(KW):
                act.wait_ge(raw_in[k % 4], 16 * (k // 4 + 1))
                nc.scalar.copy(w[0][:, k, :], raw[k % 4]).then_inc(raw_hi, 1)

            def tile(i, par, m, first, second):
                act.wait_ge(gated, i + 1)
                if not first:
                    act.wait_ge(ma_ready, i)
                for n in range(2):
                    last = nc.scalar.activation(tg[0:m, n * 512:(n + 1) * 512], ps[n][0:m, :], ACT.Tanh, scale=0.5)
                last.then_inc(tanhed, 1)
                act.wait_ge(pb_done, i + 1)
                if second is not None:
                    act.wait_ge(stored_pb[par], second)
                for n in range(2):
                    last = nc.scalar.copy(pb[0:m, par, n * 512:(n + 1) * 512], ps[4 + n][0:m, :])
                last.then_inc(pb_ready, 1)

            tile(0, 0, P, True, None)
            tile(1, 1, P, False, None)
            with act.Fori(1, NT // 2) as p:
                for par in range(2):
                    tile(p * 2 + par, par, P, False, p * 16)
            tile(NT, 0, MS, False, 16 * NT // 2)

        @block.vector
        def _(dve):
            for k in range(KW):
                dve.wait_ge(raw_hi, k + 1)
                nc.vector.tensor_tensor(w[1][:, k, :], raw[k % 4], w[0][:, k, :].bitcast(F32), ALU.subtract).then_inc(raw_lo, 1)
            dve.wait_ge(raw_lo, KW)

            def tile(i, par, m, second):
                dve.wait_ge(tanhed, i + 1)
                dve.wait_ge(pa_done, i + 1)
                if second is not None:
                    dve.wait_ge(stored_ma[par], second)
                for n in range(2):
                    at = slice(n * 512, (n + 1) * 512)
                    last = nc.vector.scalar_tensor_tensor(out=ma[0:m, par, at], in0=tg[0:m, at], scalar=1.0, in1=ps[2 + n][0:m, :],
                                                          op0=ALU.add, op1=ALU.mult)
                last.then_inc(ma_ready, 1)

            tile(0, 0, P, None)
            tile(1, 1, P, None)
            with dve.Fori(1, NT // 2) as p:
                for par in range(2):
                    tile(p * 2 + par, par, P, p * 16)
            tile(NT, 0, MS, 16 * NT // 2)

        @block.tensor
        def _(pe):
            def product(bank, lhs, k0, nk, m, first):
                for k in range(nk):
                    if first:
                        pe.wait_ge(raw_lo, k0 + k + 1)
                    for n in range(2):
                        last = three(nc.tensor, ps[bank + n][0:m, :], (lhs(0, k), lhs(1, k)),
                                     (w[0][:, k0 + k, n * 512:(n + 1) * 512], w[1][:, k0 + k, n * 512:(n + 1) * 512]),
                                     k == 0, k == nk - 1)
                return last

            def tile(i, par, m, landed, first):
                pe.wait_ge(tile_in[par], landed if not first else 16)
                if not first:
                    pe.wait_ge(tanhed, i)
                product(0, lambda h, k: hb[:, par, (h * KD + k) * P:(h * KD + k) * P + m], 0, KD, m, first).then_inc(gated, 1)
                if first:
                    pe.wait_ge(tile_in[par], landed)
                else:
                    pe.wait_ge(ma_ready, i)
                product(2, lambda h, k: ob[:, par, 0, (h * 4 + k) * P:(h * 4 + k) * P + m], KD, 4, m, first).then_inc(pa_done, 1)
                if not first:
                    pe.wait_ge(pb_ready, i)
                product(4, lambda h, k: ob[:, par, 1, (h * 4 + k) * P:(h * 4 + k) * P + m], KD + 4, 4, m, first).then_inc(pb_done, 1)

            tile(0, 0, P, 48, True)
            tile(1, 1, P, 48, False)
            with pe.Fori(1, NT // 2) as p:
                for par in range(2):
                    tile(p * 2 + par, par, P, p * 48 + 48, False)
            tile(NT, 0, MS, 48 * (NT // 2 + 1), False)


def sweep_gate_b(nc, a, s, kept):
    with ExitStack() as ctx:
        sb, sem = tools(nc, ctx)
        ps = banks(nc, ctx, "gb")
        KW = 2 * KD
        w = [sb(f"w_b_{n}", [P, KW, D], F32R) for n in ("hi", "lo")]
        hb = sb("h_parts_b", [P, 2 * D], F32R)
        tg = sb("tanh_b", [P, D])
        ma = sb("ma_b", [P, D])
        pb = sb("pb_b", [P, D])
        mb = sb("merged", [P, D])
        mT = [sb(f"merged_T_{n}", [P, D], F32R) for n in ("hi", "lo")]
        x = sb("x_b", [P, D])
        h2 = sb("h2_b", [P, D])
        xo = sb("attn_out", [P, D])
        raw = (x, xo, mb, h2)
        h2T = sb("h2_T", [P, D])
        mods = sb("mod_b", [P, 3, D])
        mods_s = sb("mod_b_sample", [MS, 3, D])
        wr = sb("w_router", [P, KD, N_GROUPS + NE])
        rb = sb("b_router", [P, N_GROUPS + NE])
        small = sb("small_b", [P, 128])
        before = sb("before", [P, P])
        ones = sb("ones", [P, P])
        half = sb("half_b", [P, 1])
        zero = h2T[:, 0:TABLE // P].bitcast(I32)
        tb = sb("rms_b", [P, 8])
        r = sb("route", [P, 256])
        idx8 = sb("route_idx", [P, 8], U32)
        slots = sb("route_slots", [P, 2], U32)
        ids = sb("token_ids", [P, 1], I32)
        idf = sb("token_ids_f", [P, 1])

        raw_in, raw_hi, raw_lo = [sem(f"gb_raw_in{n}") for n in range(4)], sem("gb_raw_hi"), sem("gb_raw_lo")
        const_in, setup = sem("gb_const"), sem("gb_setup")
        h_in, m_in, x_in = sem("gb_h_in"), sem("gb_m_in"), sem("gb_x_in")
        gated, tanhed, merged = sem("gb_gate"), sem("gb_tanh"), sem("gb_merged")
        m_turned, mT_hi, mT_lo = sem("gb_m_turned"), sem("gb_mT_hi"), sem("gb_mT_lo")
        o_done, x1_step, x1_ready, x1_sumsq, root = sem("gb_o"), sem("gb_x1_step"), sem("gb_x1"), sem("gb_sumsq"), sem("gb_root")
        mean, gate1_halved, gate_weighted = sem("gb_mean"), sem("gb_ready_consts"), sem("gb_gated_b")
        h2_step, h2_ready, h2_turned, h2T_ready = sem("gb_h2_step"), sem("gb_h2"), sem("gb_h2_turned"), sem("gb_h2T")
        logits, r_step, g_diff, g_exp, v_diff, v_exp = [sem(f"gb_{n}") for n in ("logits", "r_step", "g_diff", "g_exp", "v_diff", "v_exp")]
        chosen, ranked, slot_ready = sem("gb_chosen"), sem("gb_ranked"), sem("gb_slots")
        k_step, counted = sem("gb_rank_step"), sem("gb_counted")
        stored_x1, stored_h2, scattered, filled = sem("gb_st_x1"), sem("gb_st_h2"), sem("gb_scattered"), sem("gb_filled")
        passed = sem("gb_waits_passed")
        block = ctx.enter_context(nc.Block())

        @block.sync
        def _(sp):
            def weights(k):
                if k >= 4:
                    sp.wait_ge(raw_lo, k - 3)
                src = a["w_in"][0, k * P:(k + 1) * P, GATE_B:GATE_B + D] if k < KD else a["w_o"][0, (k - KD) * P:(k - KD + 1) * P, :]
                sp.dma_start(raw[k % 4][:, :], src).then_inc(raw_in[k % 4], 16)
            def load_h(i, m, first=False):
                if not first:
                    sp.wait_ge(gated, i)
                src = s["hT"][bass.ds(i, 1), :, :].rearrange("o p c -> p (o c)")
                sp.dma_start(view(hb[:, :], m, 16).bitcast(F32), view(src, m, 16)).then_inc(h_in, 16)

            def load_m(i, m, first=False):
                if not first:
                    sp.wait_ge(merged, i)
                sp.dma_start(ma[0:m, :], s["ma"][bass.ds(i * P, m), :]).then_inc(m_in, 16)
                sp.dma_start(pb[0:m, :], s["pb"][bass.ds(i * P, m), :]).then_inc(m_in, 16)

            def load_x(i, m, first=False):
                if not first:
                    wait_apart(sp, h2_ready, i, passed)
                    sp.wait_ge(stored_x1, i * 16)
                src = a["x_prompt"][0, bass.ds(i * P, P), :] if m == P else a["x_sample"].rearrange("b t d -> (b t) d")
                sp.dma_start(x[0:m, :], src).then_inc(x_in, 16)

            def stores(i, m):
                sp.wait_ge(x1_ready, i + 1)
                sp.dma_start(s["x1"][bass.ds(i * P, m), :], x[0:m, :]).then_inc(stored_x1, 16)
                sp.wait_ge(h2_ready, i + 1)
                sp.dma_start(s["h2"][bass.ds(i * P, m), :], h2[0:m, :]).then_inc(stored_h2, 16)

            load_h(0, P, True)
            for k in range(KW):
                weights(k)
                if k == KD:
                    load_m(0, P, True)
            for n, part in enumerate((GATE1, SCALE2, SHIFT2)):
                cols = slice(part * D, (part + 1) * D)
                sp.dma_start(mods[:, n, :], s["ada"][0:1, cols].to_broadcast([P, D])).then_inc(const_in, 16)
                sp.dma_start(mods_s[:, n, :], s["ada"][1:1 + DEC_B, cols].unsqueeze(1).to_broadcast([DEC_B, DEC_T, D])).then_inc(const_in, 16)
            sp.dma_start(wr[:, :, 0:N_GROUPS], a["w_rg"][0].rearrange("(k p) c -> p k c", p=P)).then_inc(const_in, 16)
            sp.dma_start(wr[:, :, N_GROUPS:], a["w_re"][0].rearrange("(k p) c -> p k c", p=P)).then_inc(const_in, 16)
            sp.dma_start(rb[:, 0:N_GROUPS], a["b_rg"][0:1, :].to_broadcast([P, N_GROUPS])).then_inc(const_in, 16)
            sp.dma_start(rb[:, N_GROUPS:], a["b_re"][0:1, :].to_broadcast([P, NE])).then_inc(const_in, 16)
            sp.dma_start(small[:, :], a["small"]).then_inc(const_in, 16)
            sp.dma_start(before[:, :], a["before"]).then_inc(const_in, 16)
            sp.wait_ge(raw_lo, KW)
            load_x(0, P, True)
            load_h(1, P)
            load_m(1, P)
            with sp.Fori(0, NT - 2) as i:
                load_h(i + 2, P)
                load_m(i + 2, P)
                stores(i, P)
                load_x(i + 1, P)
            load_h(NT, MS)
            load_m(NT, MS)
            stores(NT - 2, P)
            load_x(NT - 1, P)
            stores(NT - 1, P)
            load_x(NT, MS)
            stores(NT, MS)
            sp.wait_ge(stored_x1, 16 * (NT + 1))
            sp.wait_ge(stored_h2, 16 * (NT + 1))

        @block.gpsimd
        def _(pool):
            pool.memset(half[:, :], -0.5).then_inc(setup, 1)
            pool.memset(ones[:, :], 1.0).then_inc(setup, 1)
            pool.memset(zero, 0).then_inc(setup, 1)
            for n in ("wts", "eid", "rank"):
                pool.memset(kept[n][:, :, :], 0.0).then_inc(setup, 1)
            pool.memset(kept["counts"][:, :], 0.0).then_inc(setup, 1)
            pool.wait_ge(setup, 7)
            pool.dma_start(s["table"].rearrange("(p c) o -> p (c o)", p=P), zero).then_inc(filled, 16)
            pool.wait_ge(filled, 16)

            def rms(i, m):
                wait_apart(pool, x1_sumsq, i + 1, passed)
                pool.tensor_scalar(tb[0:m, 1:2], tb[0:m, 0:1], 1.0 / D, EPS, ALU.mult, ALU.add).then_inc(mean, 1)
                pool.wait_ge(mean, i + 1)
                pool.tensor_tensor(tb[0:m, 2:3], tb[0:m, 1:2], half[0:m, :], ALU.pow).then_inc(root, 1)

            def scatter(i, m):
                wait_apart(pool, slot_ready, i + 1, passed)
                for k in range(2):
                    pool.indirect_dma_start(out=s["table"], out_offset=bass.IndirectOffsetOnAxis(ap=slots[0:m, k:k + 1], axis=0),
                                            in_=ids[0:m, :], in_offset=None).then_inc(scattered, 16)

            rms(0, P)
            with pool.Fori(1, NT) as i:
                rms(i, P)
                scatter(i - 1, P)
            rms(NT, MS)
            scatter(NT - 1, P)
            scatter(NT, MS)
            pool.wait_ge(scattered, 32 * (NT + 1))

        @block.scalar
        def _(act):
            for k in range(KW):
                act.wait_ge(raw_in[k % 4], 16 * (k // 4 + 1))
                nc.scalar.copy(w[0][:, k, :], raw[k % 4][:, :]).then_inc(raw_hi, 1)

            def gate(i, m, first=False):
                act.wait_ge(gated, i + 1)
                if not first:
                    act.wait_ge(merged, i)
                for n in range(2):
                    last = nc.scalar.activation(tg[0:m, n * 512:(n + 1) * 512], ps[n][0:m, :], ACT.Tanh, scale=0.5)
                last.then_inc(tanhed, 1)

            def split(i, m, first=False):
                act.wait_ge(m_turned, i + 1)
                if not first:
                    act.wait_ge(o_done, i)
                for n in range(2):
                    last = nc.scalar.copy(view(mT[0][:, n * 512:(n + 1) * 512], m, 4), view(ps[2 + n][:, :], m, 4))
                last.then_inc(mT_hi, 1)

            def square(i, m):
                act.wait_ge(x1_ready, i + 1)
                if not isinstance(i, int) or i > 0:
                    act.wait_ge(h2_turned, i)
                    act.wait_ge(stored_h2, i * 16)
                nc.scalar.activation(h2[0:m, :], x[0:m, :], ACT.Square, accum_out=tb[0:m, 0:1]).then_inc(x1_sumsq, 1)

            def h2_out(i, m):
                act.wait_ge(h2_turned, i + 1)
                if not isinstance(i, int) or i > 0:
                    act.wait_ge(logits, i)
                for n in range(2):
                    last = nc.scalar.copy(view(h2T[:, n * 512:(n + 1) * 512], m, 4), view(ps[4 + n][:, :], m, 4))
                last.then_inc(h2T_ready, 1)

            def route(i, m):
                act.wait_ge(g_diff, i + 1)
                nc.scalar.activation(r[0:m, 44:48], r[0:m, 40:44], ACT.Exp, accum_out=r[0:m, 48:49]).then_inc(g_exp, 1)
                act.wait_ge(v_diff, i + 1)
                nc.scalar.activation(r[0:m, 50:51], r[0:m, 49:50], ACT.Exp).then_inc(v_exp, 1)

            gate(0, P, True)
            split(0, P, True)
            gate(1, P)
            act.wait_ge(filled, 16)

            def frame(i, m=P, m1=P, m2=P, first=False):
                if m1:
                    split(i + 1, m1)
                square(i, m)
                if not first:
                    route(i - 1, P)
                if m2:
                    gate(i + 2, m2)
                h2_out(i, m)

            frame(0, first=True)
            with act.Fori(1, NT - 2) as i:
                frame(i)
            frame(NT - 2, m2=MS)
            frame(NT - 1, m1=MS, m2=0)
            frame(NT, m=MS, m1=0, m2=0)
            route(NT, MS)

        @block.vector
        def _(dve):
            for k in range(KW):
                dve.wait_ge(raw_hi, k + 1)
                nc.vector.tensor_tensor(w[1][:, k, :], raw[k % 4][:, :], w[0][:, k, :].bitcast(F32), ALU.subtract).then_inc(raw_lo, 1)
            dve.wait_ge(raw_lo, KW)
            def constants_ready():
                dve.wait_ge(const_in, 16 * 12)
                dve.wait_ge(setup, 7)
                nc.vector.tensor_scalar(mods[:, 0, :], mods[:, 0, :], 0.5, None, ALU.mult).then_inc(gate1_halved, 1)
                nc.vector.tensor_scalar(mods_s[:, 0, :], mods_s[:, 0, :], 0.5, None, ALU.mult).then_inc(gate1_halved, 1)
                nc.vector.tensor_copy(idf[:, :], small[:, 40:41]).then_inc(gate1_halved, 1)
                dve.wait_ge(gate1_halved, 3)

            def gate(i, m, first=False):
                dve.wait_ge(tanhed, i + 1)
                dve.wait_ge(m_in, i * 32 + 32)
                nc.vector.scalar_tensor_tensor(out=tg[0:m, :], in0=tg[0:m, :], scalar=1.0, in1=pb[0:m, :],
                                               op0=ALU.add, op1=ALU.mult).then_inc(gate_weighted, 1)
                dve.wait_ge(gate_weighted, i + 1)
                if not first:
                    dve.wait_ge(m_turned, i)
                nc.vector.tensor_tensor(mb[0:m, :], tg[0:m, :], ma[0:m, :], ALU.add).then_inc(merged, 1)

            def split(i, m):
                dve.wait_ge(mT_hi, i + 1)
                for n in range(2):
                    at = slice(n * 512, (n + 1) * 512)
                    last = nc.vector.tensor_tensor(view(mT[1][:, at], m, 4), view(ps[2 + n][:, :], m, 4), view(mT[0][:, at], m, 4).bitcast(F32), ALU.subtract)
                last.then_inc(mT_lo, 1)

            def residual(i, m, g):
                dve.wait_ge(o_done, i + 1)
                dve.wait_ge(x_in, i * 16 + 16)
                for n in range(2):
                    at = slice(n * 512, (n + 1) * 512)
                    last = nc.vector.tensor_tensor(xo[0:m, at], ps[6 + n][0:m, :], g[0:m, 0, at], ALU.mult)
                last.then_inc(x1_step, 1)
                dve.wait_ge(x1_step, i + 1)
                nc.vector.tensor_tensor(x[0:m, :], x[0:m, :], xo[0:m, :], ALU.add).then_inc(x1_ready, 1)

            def norm(i, m, g):
                dve.wait_ge(root, i + 1)
                nc.vector.scalar_tensor_tensor(out=h2[0:m, :], in0=x[0:m, :], scalar=tb[0:m, 2:3], in1=g[0:m, 1, :],
                                               op0=ALU.mult, op1=ALU.mult).then_inc(h2_step, 1)
                dve.wait_ge(h2_step, i + 1)
                nc.vector.tensor_tensor(h2[0:m, :], h2[0:m, :], g[0:m, 2, :], ALU.add).then_inc(h2_ready, 1)

            def route(i, m):
                c = Count(i, ROUTE_STEPS)

                def step(instruction):
                    instruction.then_inc(r_step, 1)
                    if c.n == 8:
                        wait_apart(dve, r_step, c.next(), passed)
                    else:
                        dve.wait_ge(r_step, c.next())

                lg, le = r[0:m, 0:4], r[0:m, 4:36]
                gm, pr, pm, oh = r[0:m, 36:37], r[0:m, 52:56], r[0:m, 37:38], r[0:m, 56:60]
                dve.wait_ge(logits, i + 1)
                step(nc.vector.tensor_tensor(r[0:m, 0:36], ps[4][0:m, 0:36], rb[0:m, :], ALU.add))
                step(nc.vector.tensor_reduce(gm, lg, AX_X, ALU.max))
                nc.vector.tensor_scalar(r[0:m, 40:44], lg, gm, None, ALU.subtract).then_inc(g_diff, 1)
                step(nc.vector.scalar_tensor_tensor(out=pr, in0=lg, scalar=gm, in1=small[0:m, 32:36], op0=ALU.is_equal, op1=ALU.mult))
                step(nc.vector.tensor_reduce(pm, pr, AX_X, ALU.max))
                step(nc.vector.tensor_scalar(oh, pr, pm, None, ALU.is_equal))
                step(nc.vector.tensor_tensor(r[0:m, 64:96].rearrange("p (g e) -> p g e", g=N_GROUPS), le.rearrange("p (g e) -> p g e", g=N_GROUPS),
                                             oh.unsqueeze(2).to_broadcast([m, N_GROUPS, PER_GROUP]), ALU.mult))
                step(nc.vector.tensor_reduce(r[0:m, 96:104], r[0:m, 64:96].rearrange("p (g e) -> p e g", g=N_GROUPS), AX_X, ALU.add))
                step(nc.vector.tensor_tensor(r[0:m, 60:64], oh, small[0:m, 36:40], ALU.mult))
                step(nc.vector.tensor_reduce(r[0:m, 38:39], r[0:m, 60:64], AX_X, ALU.add))
                step(nc.vector.max(r[0:m, 104:112], r[0:m, 96:104]))
                nc.vector.tensor_tensor(r[0:m, 49:50], r[0:m, 105:106], r[0:m, 104:105], ALU.subtract).then_inc(v_diff, 1)
                step(nc.vector.max_index(idx8[0:m, :], r[0:m, 104:112], r[0:m, 96:104]))
                step(nc.vector.tensor_copy(r[0:m, 112:114], idx8[0:m, 0:2]))
                step(nc.vector.scalar_tensor_tensor(out=r[0:m, 114:116], in0=r[0:m, 38:39].to_broadcast([m, 2]), scalar=float(PER_GROUP),
                                                    in1=r[0:m, 112:114], op0=ALU.mult, op1=ALU.add))
                e1, e2 = r[0:m, 114:115], r[0:m, 115:116]
                step(nc.vector.tensor_copy(kept["eid"][0:m, bass.ds(i, 1), :].rearrange("p o k -> p (o k)"), r[0:m, 114:116]))
                oh1, oh2, both = r[0:m, 128:160], r[0:m, 160:192], r[0:m, 192:224]
                step(nc.vector.tensor_scalar(oh1, small[0:m, 0:NE], e1, None, ALU.is_equal))
                step(nc.vector.tensor_scalar(oh2, small[0:m, 0:NE], e2, None, ALU.is_equal))
                nc.vector.tensor_tensor(both, oh1, oh2, ALU.add).then_inc(chosen, 1)
                dve.wait_ge(v_exp, i + 1)
                dve.wait_ge(g_exp, i + 1)
                step(nc.vector.scalar_tensor_tensor(out=r[0:m, 116:117], in0=r[0:m, 50:51], scalar=1.0, in1=r[0:m, 48:49], op0=ALU.add, op1=ALU.mult))
                step(nc.vector.reciprocal(r[0:m, 118:119], r[0:m, 116:117]))
                step(nc.vector.tensor_tensor(r[0:m, 119:120], r[0:m, 118:119], r[0:m, 50:51], ALU.mult))
                step(nc.vector.tensor_copy(kept["wts"][0:m, bass.ds(i, 1), :].rearrange("p o k -> p (o k)"), r[0:m, 118:120]))
                c.all()

            def rank(i, m):
                oh1, oh2 = r[0:m, 128:160], r[0:m, 160:192]
                c = Count(i, 8)

                def step(instruction):
                    instruction.then_inc(k_step, 1)
                    dve.wait_ge(k_step, c.next())

                dve.wait_ge(ranked, i + 1)
                step(nc.vector.tensor_tensor(r[0:m, 224:256], ps[2][0:m, 0:NE], kept["counts"][0:m, :], ALU.add))
                nc.vector.tensor_tensor(kept["counts"][:, :], kept["counts"][:, :], ps[2][:, 32:32 + NE], ALU.add).then_inc(counted, 1)
                step(nc.vector.tensor_tensor(oh1, oh1, r[0:m, 224:256], ALU.mult))
                step(nc.vector.tensor_tensor(oh2, oh2, r[0:m, 224:256], ALU.mult))
                step(nc.vector.tensor_reduce(r[0:m, 120:122], r[0:m, 128:192].rearrange("p (k e) -> p k e", k=2), AX_X, ALU.add))
                step(nc.vector.tensor_copy(kept["rank"][0:m, bass.ds(i, 1), :].rearrange("p o k -> p (o k)"), r[0:m, 120:122]))
                if not isinstance(i, int) or i > 0:
                    dve.wait_ge(scattered, i * 32)
                step(nc.vector.scalar_tensor_tensor(out=r[0:m, 122:124], in0=r[0:m, 114:116], scalar=float(REGION), in1=r[0:m, 120:122],
                                                    op0=ALU.mult, op1=ALU.add))
                step(nc.vector.tensor_copy(ids[0:m, :], idf[0:m, :]))
                step(nc.vector.tensor_scalar(idf[:, :], idf[:, :], float(P), None, ALU.add))
                nc.vector.tensor_copy(slots[0:m, :], r[0:m, 122:124]).then_inc(slot_ready, 1)
                c.all()

            gate(0, P, True)
            split(0, P)
            gate(1, P)
            constants_ready()
            residual(0, P, mods)

            def frame(i, m=P, m1=P, m2=P, first=False):
                if m1:
                    split(i + 1, m1)
                norm(i, m, mods if m == P else mods_s)
                if not first:
                    route(i - 1, P)
                if m2:
                    gate(i + 2, m2)
                if not first:
                    rank(i - 1, P)
                if m1:
                    residual(i + 1, m1, mods if m1 == P else mods_s)

            frame(0, first=True)
            with dve.Fori(1, NT - 2) as i:
                frame(i)
            frame(NT - 2, m2=MS)
            frame(NT - 1, m1=MS, m2=0)
            frame(NT, m=MS, m1=0, m2=0)
            route(NT, MS)
            rank(NT, MS)

        @block.tensor
        def _(pe):
            ident = kept["ident"]

            def product(bank, lhs, k0, m, first=False):
                for k in range(KD):
                    if first:
                        pe.wait_ge(raw_lo, k0 + k + 1)
                    for n in range(2):
                        last = three(nc.tensor, ps[bank + n][0:m, :], (lhs(0, k), lhs(1, k)),
                                     (w[0][:, k0 + k, n * 512:(n + 1) * 512], w[1][:, k0 + k, n * 512:(n + 1) * 512]),
                                     k == 0, k == KD - 1)
                return last

            def gate(i, m, first=False):
                pe.wait_ge(h_in, i * 16 + 16)
                if not first:
                    pe.wait_ge(tanhed, i)
                product(0, lambda h, k: hb[:, (h * KD + k) * P:(h * KD + k) * P + m], 0, m, first).then_inc(gated, 1)

            def turn(i, m, src, bank, done):
                for k in range(KD):
                    last = nc.tensor.transpose(ps[bank + k // 4][:, (k % 4) * P:(k % 4) * P + m], src[0:m, k * P:(k + 1) * P], ident[0:m, 0:m])
                last.then_inc(done, 1)

            def turn_m(i, m):
                pe.wait_ge(merged, i + 1)
                if not isinstance(i, int) or i > 2:
                    pe.wait_ge(counted, i - 2)
                turn(i, m, mb, 2, m_turned)

            def out(i, m, first=False):
                pe.wait_ge(mT_hi, i + 1)
                pe.wait_ge(mT_lo, i + 1)
                if not first:
                    pe.wait_ge(x1_step, i)
                product(6, lambda h, k: mT[h][:, k * P:k * P + m], KD, m, first).then_inc(o_done, 1)

            def turn_h2(i, m):
                pe.wait_ge(h2_ready, i + 1)
                if not isinstance(i, int) or i > 0:
                    pe.wait_ge(chosen, i)
                turn(i, m, h2, 4, h2_turned)

            def route(i, m):
                pe.wait_ge(h2T_ready, i + 1)
                if isinstance(i, int) and i == 0:
                    pe.wait_ge(const_in, 16 * 12)
                for k in range(KD):
                    last = nc.tensor.matmul(ps[4][0:m, 0:N_GROUPS + NE], h2T[:, k * P:k * P + m], wr[:, k, :], start=(k == 0), stop=(k == KD - 1))
                last.then_inc(logits, 1)

            def rank(i, m):
                pe.wait_ge(chosen, i + 1)
                pe.wait_ge(mT_lo, min(i + 3, NT + 1) if isinstance(i, int) else i + 3)
                nc.tensor.matmul(ps[2][0:m, 0:NE], before[0:m, 0:m], r[0:m, 192:224], start=True, stop=True)
                nc.tensor.matmul(ps[2][:, 32:32 + NE], ones[0:m, :], r[0:m, 192:224], start=True, stop=True).then_inc(ranked, 1)

            gate(0, P, True)
            turn_m(0, P)
            gate(1, P)
            out(0, P, True)
            turn_m(1, P)

            def frame(i, m=P, m1=P, m2=P, first=False):
                if m2:
                    gate(i + 2, m2)
                elif m1:
                    out(i + 1, m1)
                turn_h2(i, m)
                if not first:
                    rank(i - 1, P)
                if m1 and m2:
                    out(i + 1, m1)
                route(i, m)
                if m2:
                    turn_m(i + 2, m2)

            frame(0, first=True)
            with pe.Fori(1, NT - 2) as i:
                frame(i)
            frame(NT - 2, m2=MS)
            frame(NT - 1, m1=MS, m2=0)
            frame(NT, m=MS, m1=0, m2=0)
            rank(NT, MS)


def load_expert(sp, a, w, e, slot, done):
    ww = w[:, slot * EXPERT_COLS:(slot + 1) * EXPERT_COLS]
    gate_up = ww[:, 0:KD * 2 * EH].rearrange("p (k c) -> p k c", k=KD)
    one = lambda t: t[0, bass.ds(e, 1), :, :]
    sp.dma_start(gate_up[:, :, 0:EH], one(a["w_gate"]).rearrange("o (k p) h -> p (o k) h", p=P)).then_inc(done, 16)
    sp.dma_start(gate_up[:, :, EH:], one(a["w_up"]).rearrange("o (k p) h -> p (o k) h", p=P)).then_inc(done, 16)
    sp.dma_start(ww[:, KD * 2 * EH:].rearrange("p (k c) -> p k c", k=2),
                 one(a["w_down"]).rearrange("o (k p) d -> p (o k) d", p=P)).then_inc(done, 16)


def list_blocks(nc, a, s, kept, w):
    with ExitStack() as ctx:
        sb, sem = tools(nc, ctx)
        small = sb("small_l", [P, 128])
        ni = sb("blocks_i", [P, NE], I32)
        n = sb("blocks_f", [P, NE])
        zero = sb("zeros_l", [P, NE])
        ends = sb("block_ends_f", [P, NE])
        starts = sb("block_starts", [P, NE])
        ends_i = sb("block_ends_i", [P, NE], I32)
        m = sb("passed", [P, 2, NE])
        f = sb("fields_f", [P, 8])
        fi = sb("fields_i", [P, 4], I32)
        NK = (NT + 1) * 2
        eq = sb("expert_of_row", [P, NK, NE])
        ys = sb("y_rows_f", [P, NK])
        small_in, step_done, stored, zeroed = sem("l_small_in"), sem("l_step"), sem("l_stored"), sem("l_zeroed")
        listed, w_in = sem("l_listed"), sem("l_expert_0_in")
        block = ctx.enter_context(nc.Block())

        @block.sync
        def _(sp):
            sp.dma_start(small[:, :], a["small"]).then_inc(small_in, 16)
            load_expert(sp, a, w, 0, 0, w_in)
            sp.wait_ge(listed, 1)
            with nc.allow_non_contiguous_dma(reason="the list of blocks, once"):
                sp.dma_start(s["blocks"].rearrange("f b -> b f"), fi[:, :]).then_inc(stored, 16)
            sp.dma_start(s["cum"], ends_i[0:1, :]).then_inc(stored, 16)
            sp.wait_ge(stored, 32)
            sp.wait_ge(w_in, 48)

        @block.gpsimd
        def _(pool):
            pool.memset(zero[:, :], 0.0).then_inc(zeroed, 1)

        @block.vector
        def _(dve):
            count = [0]

            def step(instruction):
                count[0] += 1
                instruction.then_inc(step_done, 1)
                dve.wait_ge(step_done, count[0])

            dve.wait_ge(small_in, 16)
            dve.wait_ge(zeroed, 1)
            number = small[:, 40:41]
            step(nc.vector.tensor_scalar(n[:, :], kept["counts"][:, :], float(P - 1), None, ALU.add))
            step(nc.vector.tensor_copy(ni[:, :], n[:, :]))
            step(nc.vector.tensor_scalar(ni[:, :], ni[:, :], 7, None, ALU.arith_shift_right))
            step(nc.vector.tensor_copy(n[:, :], ni[:, :]))
            step(nc.vector.tensor_scalar(n[:, :], n[:, :], 1.0, None, ALU.max))
            step(nc.vector.tensor_tensor_scan(ends[:, :], n[:, :], zero[:, :], 0.0, ALU.add, ALU.add))
            step(nc.vector.tensor_tensor(starts[:, :], ends[:, :], n[:, :], ALU.subtract))
            step(nc.vector.tensor_copy(ends_i[:, :], ends[:, :]))
            step(nc.vector.tensor_scalar(m[:, 0, :], ends[:, :], number, None, ALU.is_le))
            step(nc.vector.tensor_tensor(m[:, 1, :], m[:, 0, :], ends[:, :], ALU.mult))
            step(nc.vector.tensor_reduce(f[:, 0:1], m[:, 0, :], AX_X, ALU.add))
            step(nc.vector.tensor_reduce(f[:, 1:2], m[:, 1, :], AX_X, ALU.max))
            step(nc.vector.tensor_scalar(f[:, 2:3], f[:, 0:1], float(NE - 1), None, ALU.min))
            step(nc.vector.tensor_tensor(f[:, 3:4], number, f[:, 1:2], ALU.subtract))
            step(nc.vector.tensor_scalar(f[:, 5:6], f[:, 3:4], float(P), None, ALU.mult))
            step(nc.vector.scalar_tensor_tensor(out=f[:, 4:5], in0=f[:, 2:3], scalar=float(REGION), in1=f[:, 5:6], op0=ALU.mult, op1=ALU.add))
            step(nc.vector.tensor_scalar(f[:, 3:4], f[:, 2:3], 1.0, None, ALU.add))
            step(nc.vector.tensor_copy(fi[:, 0:3], f[:, 2:5]))
            step(nc.vector.tensor_scalar(fi[:, 0:1], fi[:, 0:1], RING - 1, None, ALU.bitwise_and))
            nc.vector.tensor_copy(fi[:, 3:4], ends_i[:, NE - 1:NE]).then_inc(listed, 1)
            eid = kept["eid"][:, :, :].rearrange("p t k -> p (t k)")
            step(nc.vector.tensor_tensor(eq[:, :, :], small[:, 0:NE].unsqueeze(1).to_broadcast([P, NK, NE]),
                                         eid.unsqueeze(2).to_broadcast([P, NK, NE]), ALU.is_equal))
            step(nc.vector.tensor_tensor(eq[:, :, :], eq[:, :, :], starts[:, :].unsqueeze(1).to_broadcast([P, NK, NE]), ALU.mult))
            step(nc.vector.tensor_reduce(ys[:, :], eq[:, :, :], AX_X, ALU.add))
            step(nc.vector.scalar_tensor_tensor(out=ys[:, :], in0=ys[:, :], scalar=float(P), in1=kept["rank"][:, :, :].rearrange("p t k -> p (t k)"),
                                                op0=ALU.mult, op1=ALU.add))
            step(nc.vector.tensor_copy(kept["yrow"][:, :, :].rearrange("p t k -> p (t k)"), ys[:, :]))


def experts(nc, a, s, kept, w):
    with ExitStack() as ctx:
        sb, sem = tools(nc, ctx)
        ps = banks(nc, ctx, "ex")
        WC = EXPERT_COLS
        lists = sb("block_lists", [1, 4 * P], I32)
        ends = sb("block_ends_row", [1, NE], I32)
        idx = sb("row_tokens", [P, 2], I32)
        xg = sb("gathered", [P, 2, D])
        xT = [sb(f"gathered_T{n}", [P, KD, P]) for n in range(2)]
        th = sb("tanh_e", [P, 2, EH])
        sg = sb("silu_e", [P, 2, EH])
        h = sb("hidden", [P, 2, EH])
        hT = [sb(f"hidden_T{n}", [P, 2, P]) for n in range(2)]
        y = sb("y_block", [P, 2, D])
        zero = sb("unused_rows", [P, 2 * D])
        lists_in = sem("e_lists_in")
        w_in, w_ready = [sem(f"e_w_in{n}") for n in range(RING)], sem("e_w_ready")
        idx_in, x_in = (sem("e_idx_in0"), sem("e_idx_in1")), (sem("e_x_in0"), sem("e_x_in1"))
        x_turned, xT_a, xT_d = sem("e_x_turned"), sem("e_xT_act"), sem("e_xT_dve")
        gu, tanhed, silued, h_ready, h_turned, hT_ready = [sem(f"e_{n}") for n in ("gate_up", "tanh", "silu", "h", "h_turned", "hT")]
        down, y_a, y_d, stored = sem("e_down"), sem("e_y_act"), sem("e_y_dve"), (sem("e_stored0"), sem("e_stored1"))
        zeroed, filled = sem("e_zeroed"), sem("e_filled")
        passed = sem("e_waits_passed")
        block = ctx.enter_context(nc.Block())
        PAIRS = MAX_BLOCKS // 2

        def listed(eng, field, b):
            at = field * P + b
            ap = lists[0:1, at:at + 1] if isinstance(at, int) else lists[0:1, bass.ds(at, 1)]
            return eng.value_load(ap, min_val=(0, 1, 0, NE)[field], max_val=(RING - 1, NE, TABLE - P, MAX_BLOCKS)[field])

        @block.sync
        def _(sp):
            sp.dma_start(lists[:, :], s["blocks"].rearrange("f b -> (f b)").unsqueeze(0)).then_inc(lists_in, 16)
            sp.dma_start(ends[:, :], s["cum"]).then_inc(lists_in, 16)

            def arrived(slot, times):
                sp.wait_ge(w_in[slot], times * 48)
                sp.sem_inc(w_ready, 1)

            sp.sem_inc(w_ready, 1)
            sp.wait_ge(x_in[0], 16)
            load_expert(sp, a, w, 1, 1, w_in[1])
            sp.wait_ge(x_in[1], 16)
            load_expert(sp, a, w, 2, 2, w_in[2])
            arrived(1, 1)
            sp.wait_ge(x_in[0], 32)
            load_expert(sp, a, w, 3, 3, w_in[3])
            assert RING == 4
            sp.wait_ge(lists_in, 32)

            def unused(p, total):
                with sp.If(p * 2 < total):
                    sp.sem_inc(filled, 16)
                with sp.If(p * 2 >= total):
                    rows = s["ys"][bass.ds(p * (2 * P), 2 * P), :].rearrange("(q two) d -> q (two d)", two=2)
                    sp.dma_start(rows, zero[:, :]).then_inc(filled, 16)

            sp.wait_ge(zeroed, 1)
            assert PAIRS == NE and RING * 2 <= NE
            total = listed(sp, 3, 0)
            with sp.Fori(1, NE // RING) as g:
                for slot in range(RING):
                    arrived((slot + 2) % RING, g + slot // (RING - 1))
                    last = sp.value_load(ends[0:1, bass.ds(g * RING + slot - RING, 1)], min_val=1, max_val=MAX_BLOCKS)
                    wait_apart(sp, down, last, passed)
                    load_expert(sp, a, w, g * RING + slot, slot, w_in[slot])
                    unused(g * (-RING) + (PAIRS + RING - 1 - slot), total)
            for slot in range(RING - 2, RING):
                arrived(slot, NE // RING)
            sp.wait_ge(filled, (PAIRS - RING) * 16)

        @block.gpsimd
        def _(pool):
            pool.memset(zero[:, :], 0.0).then_inc(zeroed, 1)
            pool.wait_ge(lists_in, 32)

            def gather(b, par, n, first=False):
                if not first:
                    wait_apart(pool, x_turned, b - 1, passed)
                row = listed(pool, 2, b)
                pool.dma_start(idx[:, par:par + 1], s["table"][bass.ds(row, P), :]).then_inc(idx_in[par], 16)
                wait_apart(pool, idx_in[par], n * 16 + 16, passed)
                pool.indirect_dma_start(out=xg[:, par, :], out_offset=None, in_=s["h2"],
                                        in_offset=bass.IndirectOffsetOnAxis(ap=idx[:, par:par + 1].bitcast(U32), axis=0)).then_inc(x_in[par], 16)

            gather(0, 0, 0, True)
            gather(1, 1, 0, True)
            total = listed(pool, 3, 0)
            with pool.Fori(0, PAIRS) as p:
                with pool.If(p * 2 < total):
                    gather(p * 2 + 2, 0, p + 1)
                    gather(p * 2 + 3, 1, p + 1)

        @block.scalar
        def _(act):
            act.wait_ge(lists_in, 32)

            def turned(b, par):
                act.wait_ge(x_turned, b + 1)
                nc.scalar.copy(xT[par][:, 0:4, :], ps[0][:, :].rearrange("p (k m) -> p k m", m=P)).then_inc(xT_a, 1)

            def silu(b, par):
                act.wait_ge(gu, b + 1)
                nc.scalar.activation(th[:, par, :], ps[2 + par][:, 0:EH], ACT.Tanh, scale=0.5).then_inc(tanhed, 1)

            def hidden(b, par):
                act.wait_ge(h_turned, b + 1)
                nc.scalar.activation(hT[par][:, :, :], ps[4][:, 0:2 * P].rearrange("p (k m) -> p k m", m=P), ACT.Copy, scale=0.5).then_inc(hT_ready, 1)

            def store(b, par, before):
                act.wait_ge(down, b + 1)
                if before is not None:
                    act.wait_ge(stored[par], before)
                nc.scalar.copy(y[:, par, 0:512], ps[5][:, :]).then_inc(y_a, 1)
                act.wait_ge(y_a, b + 1)
                act.wait_ge(y_d, b + 1)
                act.dma_start(s["ys"][bass.ds(b * P, P), :], y[:, par, :]).then_inc(stored[par], 16)

            turned(0, 0)
            silu(0, 0)
            turned(1, 1)
            total = listed(act, 3, 0)

            def step(b, par, before):
                hidden(b - 1, 1 - par)
                silu(b, par)
                turned(b + 1, 1 - par)
                store(b - 1, 1 - par, before)

            step(1, 1, None)
            step(2, 0, None)
            with act.Fori(1, PAIRS) as p:
                with act.If(p * 2 < total):
                    step(p * 2 + 1, 1, p * 16)
                    step(p * 2 + 2, 0, p * 16)
            for par in range(2):
                wait_apart(act, stored[par], (total + 1) // 2 * 16, passed)

        @block.vector
        def _(dve):
            dve.wait_ge(lists_in, 32)

            def turned(b, par):
                dve.wait_ge(x_turned, b + 1)
                nc.vector.tensor_copy(xT[par][:, 4:8, :], ps[1][:, :].rearrange("p (k m) -> p k m", m=P)).then_inc(xT_d, 1)

            def silu(b, par):
                dve.wait_ge(tanhed, b + 1)
                nc.vector.scalar_tensor_tensor(out=sg[:, par, :], in0=th[:, par, :], scalar=1.0, in1=ps[2 + par][:, 0:EH],
                                               op0=ALU.add, op1=ALU.mult).then_inc(silued, 1)
                dve.wait_ge(silued, b + 1)
                nc.vector.tensor_tensor(h[:, par, :], ps[2 + par][:, EH:2 * EH], sg[:, par, :], ALU.mult).then_inc(h_ready, 1)

            def store(b, par, before):
                dve.wait_ge(down, b + 1)
                if before is not None:
                    dve.wait_ge(stored[par], before)
                nc.vector.tensor_copy(y[:, par, 512:1024], ps[6][:, :]).then_inc(y_d, 1)

            def step(b, par, before):
                silu(b, par)
                turned(b + 1, 1 - par)
                store(b - 1, 1 - par, before)

            turned(0, 0)
            silu(0, 0)
            turned(1, 1)
            total = listed(dve, 3, 0)
            step(1, 1, None)
            step(2, 0, None)
            with dve.Fori(1, PAIRS) as p:
                with dve.If(p * 2 < total):
                    step(p * 2 + 1, 1, p * 16)
                    step(p * 2 + 2, 0, p * 16)

        @block.tensor
        def _(pe):
            ident = kept["ident"]
            pe.wait_ge(lists_in, 32)

            def turn(b, par, n):
                pe.wait_ge(x_in[par], n * 16 + 16)
                if not isinstance(b, int) or b > 0:
                    pe.wait_ge(xT_a, b)
                    pe.wait_ge(xT_d, b)
                for k in range(KD):
                    last = nc.tensor.transpose(ps[k // 4][:, (k % 4) * P:(k % 4 + 1) * P], xg[:, par, k * P:(k + 1) * P], ident[:, :])
                last.then_inc(x_turned, 1)

            def gate_up(b, par):
                need, slot = listed(pe, 1, b), listed(pe, 0, b)
                pe.wait_ge(w_ready, need)
                pe.wait_ge(xT_a, b + 1)
                pe.wait_ge(xT_d, b + 1)
                if not isinstance(b, int) or b > 1:
                    pe.wait_ge(h_ready, b - 1)
                for k in range(KD):
                    last = nc.tensor.matmul(ps[2 + par][:, :], xT[par][:, k, :], w[:, bass.ds(slot * WC + k * 2 * EH, 2 * EH)],
                                            start=(k == 0), stop=(k == KD - 1))
                last.then_inc(gu, 1)

            def turn_h(b, par):
                pe.wait_ge(h_ready, b + 1)
                if not isinstance(b, int) or b > 0:
                    pe.wait_ge(hT_ready, b)
                for k in range(2):
                    last = nc.tensor.transpose(ps[4][:, k * P:(k + 1) * P], h[:, par, k * P:(k + 1) * P], ident[:, :])
                last.then_inc(h_turned, 1)

            def out(b, par):
                slot = listed(pe, 0, b)
                pe.wait_ge(hT_ready, b + 1)
                if not isinstance(b, int) or b > 0:
                    pe.wait_ge(y_a, b)
                    pe.wait_ge(y_d, b)
                for n in range(2):
                    for k in range(2):
                        at = slot * WC + KD * 2 * EH + k * D + n * 512
                        last = nc.tensor.matmul(ps[5 + n][:, :], hT[par][:, k, :], w[:, bass.ds(at, 512)], start=(k == 0), stop=(k == 1))
                last.then_inc(down, 1)

            def step(b, par, n):
                turn_h(b - 1, 1 - par)
                gate_up(b, par)
                turn(b + 1, 1 - par, n)
                out(b - 1, 1 - par)

            turn(0, 0, 0)
            gate_up(0, 0)
            turn(1, 1, 0)
            total = listed(pe, 3, 0)
            step(1, 1, 1)
            step(2, 0, 1)
            with pe.Fori(1, PAIRS) as p:
                with pe.If(p * 2 < total):
                    step(p * 2 + 1, 1, p + 1)
                    step(p * 2 + 2, 0, p + 1)


def combine(nc, a, s, kept, outs):
    y_prompt, y_sample = outs[0], outs[1]
    NB = 4
    with ExitStack() as ctx:
        sb, sem = tools(nc, ctx)
        g = sb("expert_pairs", [P, NB, 2, D])
        x = sb("x_c", [P, NB, D])
        o = sb("out_rows", [P, NB, D])
        sq = sb("squares_c", [P, D])
        mods = sb("gate2", [P, D])
        mods_s = sb("gate2_sample", [MS, D])
        gf = sb("normf", [P, D])
        half = sb("half_c", [P, 1])
        t = sb("rms_c", [P, NB, 4])
        at = sb("gather_rows", [P, NB, 2], I32)
        wt2 = sb("weights_now", [P, NB, 2])
        const_in, half_ready, at_ready = sem("c_const"), sem("c_half"), sem("c_rows_ready")
        g_in, x_in, stored = [[sem(f"c_{n}{k}") for k in range(NB)] for n in ("g_in", "x_in", "stored")]
        wt_ready, weighted, summed = sem("c_weights"), sem("c_weighted"), sem("c_summed")
        sumsq, mean, root, done = sem("c_sumsq"), sem("c_mean"), sem("c_root"), sem("c_done")
        passed = sem("c_waits_passed")
        block = ctx.enter_context(nc.Block())
        GROUPS = NT // NB

        @block.sync
        def _(sp):
            def load(i, k, m, first=False):
                if not first:
                    sp.wait_ge(summed, i - NB + 1)
                sp.dma_start(x[0:m, k, :], s["x1"][bass.ds(i * P, m), :]).then_inc(x_in[k], 16)

            def store(i, k, dst, m):
                sp.wait_ge(done, i + 1)
                sp.dma_start(dst, o[0:m, k, :]).then_inc(stored[k], 16)

            load(0, 0, P, True)
            sp.dma_start(mods[:, :], s["ada"][0:1, GATE2 * D:].to_broadcast([P, D])).then_inc(const_in, 16)
            sp.dma_start(gf[:, :], a["normf_g"].unsqueeze(0).to_broadcast([P, D])).then_inc(const_in, 16)
            for k in range(1, NB):
                load(k, k, P, True)
            sp.dma_start(mods_s[:, :], s["ada"][1:1 + DEC_B, GATE2 * D:].unsqueeze(1).to_broadcast([DEC_B, DEC_T, D])).then_inc(const_in, 16)
            with sp.Fori(0, GROUPS - 1) as p:
                for k in range(NB):
                    load(p * NB + k + NB, k, P)
                    store(p * NB + k, k, y_prompt[0, bass.ds((p * NB + k) * P, P), :], P)
            load(NT, 0, MS)
            for i in range(NT - NB, NT):
                store(i, i % NB, y_prompt[0, i * P:(i + 1) * P, :], P)
            store(NT, 0, y_sample.rearrange("b t d -> (b t) d"), MS)
            sp.wait_ge(stored[0], 16 * (GROUPS + 1))
            for k in range(1, NB):
                sp.wait_ge(stored[k], 16 * GROUPS)

        @block.gpsimd
        def _(pool):
            pool.memset(half[:, :], -0.5).then_inc(half_ready, 1)
            pool.wait_ge(half_ready, 1)

            def gather(i, k, m, first=False):
                if not first:
                    wait_apart(pool, summed, i - NB + 1, passed)
                rows = kept["yrow"][0:m, bass.ds(i, 1), :] if not isinstance(i, int) else kept["yrow"][0:m, i:i + 1, :]
                for n in range(2):
                    pool.tensor_copy(at[0:m, k, n:n + 1], rows[:, :, n]).then_inc(at_ready, 1)
                wait_apart(pool, at_ready, i * 2 + 2, passed)
                for n in range(2):
                    pool.indirect_dma_start(out=g[0:m, k, n, :], out_offset=None, in_=s["ys"],
                                            in_offset=bass.IndirectOffsetOnAxis(ap=at[0:m, k, n:n + 1].bitcast(U32), axis=0)).then_inc(g_in[k], 16)

            def rms(i, k, m):
                wait_apart(pool, sumsq, i + 1, passed)
                pool.tensor_scalar(t[0:m, k, 1:2], t[0:m, k, 0:1], 1.0 / D, EPS, ALU.mult, ALU.add).then_inc(mean, 1)
                pool.wait_ge(mean, i + 1)
                pool.tensor_tensor(t[0:m, k, 2:3], t[0:m, k, 1:2], half[0:m, :], ALU.pow).then_inc(root, 1)

            for k in range(NB):
                gather(k, k, P, True)
            with pool.Fori(0, GROUPS - 1) as p:
                for k in range(NB):
                    rms(p * NB + k, k, P)
                    gather(p * NB + k + NB, k, P)
            rms(NT - NB, 0, P)
            gather(NT, 0, MS)
            for k in range(1, NB):
                rms(NT - NB + k, k, P)
            rms(NT, 0, MS)

        @block.scalar
        def _(act):
            def tile(i, k, m, first=False):
                if not first:
                    act.wait_ge(sumsq, i)
                act.wait_ge(summed, i + 1)
                nc.scalar.activation(sq[0:m, :], o[0:m, k, :], ACT.Square, accum_out=t[0:m, k, 0:1]).then_inc(sumsq, 1)

            for k in range(NB):
                tile(k, k, P, k == 0)
            with act.Fori(1, GROUPS) as p:
                for k in range(NB):
                    tile(p * NB + k, k, P)
            tile(NT, 0, MS)

        @block.vector
        def _(dve):
            dve.wait_ge(const_in, 16 * 3)

            def add(i, k, m, gate, n, first=False):
                nc.vector.tensor_copy(wt2[0:m, k, :], kept["wts"][0:m, bass.ds(i, 1), :].rearrange("p o k -> p (o k)")).then_inc(wt_ready, 1)
                if not first:
                    dve.wait_ge(stored[k], n * 16)
                dve.wait_ge(g_in[k], n * 32 + 32)
                dve.wait_ge(x_in[k], n * 16 + 16)
                dve.wait_ge(wt_ready, i + 1)
                nc.vector.tensor_scalar(o[0:m, k, :], g[0:m, k, 0, :], wt2[0:m, k, 0:1], None, ALU.mult).then_inc(weighted, 1)
                dve.wait_ge(weighted, i * 3 + 1)
                nc.vector.scalar_tensor_tensor(out=o[0:m, k, :], in0=g[0:m, k, 1, :], scalar=wt2[0:m, k, 1:2], in1=o[0:m, k, :],
                                               op0=ALU.mult, op1=ALU.add).then_inc(weighted, 1)
                dve.wait_ge(weighted, i * 3 + 2)
                nc.vector.tensor_tensor(o[0:m, k, :], o[0:m, k, :], gate[0:m, :], ALU.mult).then_inc(weighted, 1)
                dve.wait_ge(weighted, i * 3 + 3)
                nc.vector.tensor_tensor(o[0:m, k, :], o[0:m, k, :], x[0:m, k, :], ALU.add).then_inc(summed, 1)

            def norm(i, k, m):
                dve.wait_ge(root, i + 1)
                nc.vector.scalar_tensor_tensor(out=o[0:m, k, :], in0=o[0:m, k, :], scalar=t[0:m, k, 2:3], in1=gf[0:m, :],
                                               op0=ALU.mult, op1=ALU.mult).then_inc(done, 1)

            add(0, 0, P, mods, 0, True)
            for k in range(1, NB):
                add(k, k, P, mods, 0, True)
                norm(k - 1, k - 1, P)
            with dve.Fori(1, GROUPS) as p:
                for k in range(NB):
                    add(p * NB + k, k, P, mods, p)
                    norm(p * NB + k - 1, (k - 1) % NB, P)
            add(NT, 0, MS, mods_s, GROUPS)
            norm(NT - 1, NB - 1, P)
            norm(NT, 0, MS)


_INS = ["x_prompt", "x_sample", "cache_k", "cache_v", "c_prompt", "c_sample", "w_ada", "b_ada", "norm1_g", "w_in", "ln_v_g",
        "ln_v_b", "w_s", "b_s", "attn_sinks", "w_pa", "w_pb", "w_o", "norm2_g", "w_rg", "b_rg", "w_re", "b_re", "w_gate", "w_up",
        "w_down", "normf_g"]
_OUTS = [(1, SEQ, D), (DEC_B, DEC_T, D), (1, 1, WIN, NKV, HD), (1, 1, WIN, NKV, HD), (1, DEC_B, DEC_T, NKV, HD),
         (1, DEC_B, DEC_T, NKV, HD), (1, DEC_B, DEC_T, AW)]


def kernel(**inputs):
    import concourse.bacc as bacc
    from concourse.bass_utils import run_bass_kernel_spmd

    nc = bacc.Bacc("TRN2", target_bir_lowering=False, num_devices=1)
    arrays = {f"in_{n}": np.ascontiguousarray(inputs[n]) for n in _INS}
    arrays.update({f"const_{n}": v for n, v in constants().items()})
    a = {}
    for n, v in arrays.items():
        a[n.split("_", 1)[1]] = nc.dram_tensor(n, v.shape, mybir.dt.from_np(v.dtype), kind="ExternalInput").ap()
    outs = [nc.dram_tensor(f"out_{i}", shape, F32, kind="ExternalOutput").ap() for i, shape in enumerate(_OUTS)]
    program(nc, a, outs)
    r = run_bass_kernel_spmd(nc, [arrays], core_ids=[0])
    return tuple(r.results[0][f"out_{i}"] for i in range(len(_OUTS)))
```
